# Optimizing a Trainium2 kernel written in Bass

```python
import jax
import jax.numpy as jnp
from jax import lax
import numpy as np

D_MODEL = 1024
BATCH = 1
SEQ = 512
DEPTH = 1

HEAD_DIM = 64
NSA_HEADS = 6
NSA_KV_HEADS = 2
NSA_GROUP = NSA_HEADS // NSA_KV_HEADS
CMP_BLOCK = 32
CMP_STRIDE = 16
CMP_HIDDEN = 256
SLC_BLOCK = 64
SLC_TOPN = 8
WIN = 512
NSA_QB = 64
FORCE_SCORE = 1e9
DIL_PAIRS = ((128, 1), (512, 4), (2048, 16))
DIL_HPG = 2
DIL_HEADS = DIL_HPG * len(DIL_PAIRS)
DIL_QB = 128
HG_HEADS = 4
HG_DIM = 64
HG_CHUNK = 64
LB_TINY = 1e-30
D_FF = 4 * D_MODEL
PLE_DIM = 256
EPS = 1e-6
NEG = -1e30
NSA_Q_W = NSA_HEADS * HEAD_DIM
NSA_KV_W = NSA_KV_HEADS * HEAD_DIM
DIL_W = DIL_HEADS * HEAD_DIM
HG_W = HG_HEADS * HG_DIM
IN_WIDTHS = (NSA_Q_W,) + (NSA_KV_W,) * 6 + (3 * NSA_HEADS,) + (DIL_W,) * 3 + (HG_W,) * 4
IN_TOTAL = sum(IN_WIDTHS)
MIX_W = NSA_Q_W + DIL_W + HG_W

kernel_name = 'hybrid_nsa_dilated_hgrn2_parallel'

def _rmsnorm(x, g):
    xf = x.astype(jnp.float32)
    y = xf * lax.rsqrt(jnp.mean(xf * xf, axis=-1, keepdims=True) + EPS)
    return (y * g.astype(jnp.float32)).astype(x.dtype)

def _softmax_masked(s, mask):
    s = jnp.where(mask, s, NEG)
    m = jnp.max(s, axis=-1, keepdims=True)
    e = jnp.where(mask, jnp.exp(s - m), 0.0)
    den = jnp.maximum(jnp.sum(e, axis=-1, keepdims=True), 1e-30)
    return e / den, (m + jnp.log(den))[..., 0]

def _alibi_slopes():
    n = NSA_HEADS + DIL_HEADS
    s = 2.0 ** (-8.0 * np.arange(1, n + 1) / n)
    quads = s.reshape(-1, 4)
    nsa = quads[:, 2:].reshape(-1)
    dil = quads[:, :2].reshape(-1)
    return jnp.asarray(nsa, jnp.float32), jnp.asarray(dil, jnp.float32)

def _compress(x, pos, w1, w2):
    B, Hk, S, Dh = x.shape
    n_cmp = (S - CMP_BLOCK) // CMP_STRIDE + 1
    idx = np.arange(n_cmp)[:, None] * CMP_STRIDE + np.arange(CMP_BLOCK)[None, :]
    blocks = jnp.take(x, jnp.asarray(idx.reshape(-1)), axis=2).reshape(B, Hk, n_cmp, CMP_BLOCK, Dh) + pos
    flat = blocks.reshape(B, Hk, n_cmp, CMP_BLOCK * Dh)
    return jax.nn.silu(flat @ w1) @ w2

def _nsa(q, kc, vc, ks, vs, kw, vw, gate_logits, cmp_pos, cmp_w1, cmp_w2, slopes):
    f32 = jnp.float32
    B, S, _ = q.shape
    dt = q.dtype
    qh = q.reshape(B, S, NSA_KV_HEADS, NSA_GROUP, HEAD_DIM).transpose(0, 2, 3, 1, 4) * (HEAD_DIM ** -0.5)

    def kvh(t):
        return t.reshape(B, S, NSA_KV_HEADS, HEAD_DIM).transpose(0, 2, 1, 3)

    gates = jax.nn.sigmoid(gate_logits.astype(f32)).reshape(B, S, NSA_KV_HEADS, NSA_GROUP, 3).transpose(0, 2, 3, 1, 4)
    k_cmp = _compress(kvh(kc), cmp_pos[0], cmp_w1[0], cmp_w2[0])
    v_cmp = _compress(kvh(vc), cmp_pos[1], cmp_w1[1], cmp_w2[1])
    n_cmp = k_cmp.shape[2]
    n_slc = S // SLC_BLOCK
    k_top = min(SLC_TOPN, n_slc)
    cmp_start = np.arange(n_cmp) * CMP_STRIDE
    cmp_end = jnp.asarray(cmp_start + CMP_BLOCK - 1)
    cmp_ctr = jnp.asarray(cmp_start + 0.5 * (CMP_BLOCK - 1), f32)
    slc_start = np.arange(n_slc) * SLC_BLOCK
    overlap = jnp.asarray(((cmp_start[:, None] < slc_start[None, :] + SLC_BLOCK)
                           & (cmp_start[:, None] + CMP_BLOCK > slc_start[None, :])).astype(np.float32))
    ks_blk = kvh(ks).reshape(B, NSA_KV_HEADS, n_slc, SLC_BLOCK, HEAD_DIM)
    vs_blk = kvh(vs).reshape(B, NSA_KV_HEADS, n_slc, SLC_BLOCK, HEAD_DIM)
    kw_pad = jnp.pad(kvh(kw), ((0, 0), (0, 0), (WIN, 0), (0, 0)))
    vw_pad = jnp.pad(kvh(vw), ((0, 0), (0, 0), (WIN, 0), (0, 0)))
    sl = slopes.reshape(1, NSA_KV_HEADS, NSA_GROUP, 1, 1)
    b_idx = jnp.arange(B)[:, None, None, None]
    h_idx = jnp.arange(NSA_KV_HEADS)[None, :, None, None]
    blk_ids = jnp.arange(n_slc)

    def block(i):
        q0 = i * NSA_QB
        t = q0 + jnp.arange(NSA_QB)
        tf = t.astype(f32)
        qi = lax.dynamic_slice_in_dim(qh, q0, NSA_QB, axis=3)
        gi = lax.dynamic_slice_in_dim(gates, q0, NSA_QB, axis=3)
        s_c = jnp.einsum('bkgqd,bknd->bkgqn', qi, k_cmp).astype(f32) - sl * jnp.abs(tf[:, None] - cmp_ctr[None, :])
        p_c, _ = _softmax_masked(s_c, cmp_end[None, :] <= t[:, None])
        o_c = jnp.einsum('bkgqn,bknd->bkgqd', p_c.astype(dt), v_cmp)
        imp = jnp.einsum('bkgqn,nm->bkqm', p_c, overlap)
        cur = (t // SLC_BLOCK)[:, None]
        forced = (blk_ids[None, :] == 0) | (blk_ids[None, :] == cur) | (blk_ids[None, :] == cur - 1)
        valid = blk_ids[None, :] <= cur
        score = jnp.where(valid, jnp.where(forced, FORCE_SCORE, imp), -FORCE_SCORE)
        top_s, top_i = lax.top_k(score, k_top)
        k_sel = ks_blk[b_idx, h_idx, top_i]
        v_sel = vs_blk[b_idx, h_idx, top_i]
        pos = top_i[..., None] * SLC_BLOCK + jnp.arange(SLC_BLOCK)
        m_s = (top_s >= 0)[..., None] & (pos <= t[:, None, None])
        dist = tf[:, None, None] - pos.astype(f32)
        s_s = jnp.einsum('bkgqd,bkqjld->bkgqjl', qi, k_sel).astype(f32) - sl[..., None] * dist[:, :, None]
        shp = s_s.shape
        p_s, _ = _softmax_masked(s_s.reshape(shp[0], shp[1], shp[2], shp[3], -1),
                                 m_s.reshape(shp[0], shp[1], 1, shp[3], -1))
        o_s = jnp.einsum('bkgqjl,bkqjld->bkgqd', p_s.reshape(shp).astype(dt), v_sel)
        kwi = lax.dynamic_slice_in_dim(kw_pad, q0, NSA_QB + WIN, axis=2)
        vwi = lax.dynamic_slice_in_dim(vw_pad, q0, NSA_QB + WIN, axis=2)
        kp = q0 - WIN + jnp.arange(NSA_QB + WIN)
        rel = t[:, None] - kp[None, :]
        m_w = (kp[None, :] >= 0) & (rel >= 0) & (rel < WIN)
        s_w = jnp.einsum('bkgqd,bknd->bkgqn', qi, kwi).astype(f32) - sl * rel.astype(f32)
        p_w, _ = _softmax_masked(s_w, m_w)
        o_w = jnp.einsum('bkgqn,bknd->bkgqd', p_w.astype(dt), vwi)
        o = gi[..., 0:1] * o_c + gi[..., 1:2] * o_s + gi[..., 2:3] * o_w
        return o.astype(dt)

    out = lax.map(block, jnp.arange(S // NSA_QB))
    return out.transpose(1, 0, 4, 2, 3, 5).reshape(B, S, NSA_Q_W)

def _dilated(q, k, v, slopes):
    f32 = jnp.float32
    B, S, _ = q.shape
    dt = q.dtype

    def heads(t):
        return t.reshape(B, S, DIL_HEADS, HEAD_DIM).transpose(0, 2, 1, 3)

    qh = heads(q) * (HEAD_DIM ** -0.5)
    kh = heads(k)
    vh = heads(v)
    groups = []
    for g, (w, d) in enumerate(DIL_PAIRS):
        hs = slice(g * DIL_HPG, (g + 1) * DIL_HPG)
        groups.append((qh[:, hs], kh[:, hs], vh[:, hs], slopes[hs], w, d))

    def block(i):
        q0 = i * DIL_QB
        t = q0 + jnp.arange(DIL_QB)
        outs, lses = [], []
        for qg, kg, vg, sg, w, d in groups:
            n_keys = w // d + 1
            dist = jnp.arange(n_keys) * d
            pos = t[:, None] - dist[None, :]
            idx = jnp.maximum(pos, 0).reshape(-1)
            qi = lax.dynamic_slice_in_dim(qg, q0, DIL_QB, axis=2)
            ki = jnp.take(kg, idx, axis=2).reshape(B, DIL_HPG, DIL_QB, n_keys, HEAD_DIM)
            vi = jnp.take(vg, idx, axis=2).reshape(B, DIL_HPG, DIL_QB, n_keys, HEAD_DIM)
            s = jnp.einsum('bhqd,bhqjd->bhqj', qi, ki).astype(f32) - sg[None, :, None, None] * dist.astype(f32)
            p, lse = _softmax_masked(s, pos >= 0)
            outs.append(jnp.einsum('bhqj,bhqjd->bhqd', p.astype(dt), vi))
            lses.append(lse)
        alpha = jax.nn.softmax(jnp.stack(lses), axis=0)
        return jnp.concatenate([outs[g] * alpha[g][..., None].astype(dt) for g in range(len(outs))], axis=1)

    out = lax.map(block, jnp.arange(S // DIL_QB))
    return out.transpose(1, 0, 3, 2, 4).reshape(B, S, DIL_W)

def _hgrn2(q, f_logit, inp, g, lb):
    f32 = jnp.float32
    B, S, _ = q.shape
    dt = q.dtype

    def heads(t):
        return t.astype(f32).reshape(B, S, HG_HEADS, HG_DIM).transpose(0, 2, 1, 3)

    qh, flh, vh = heads(q), heads(f_logit), heads(inp)
    lbh = lb.astype(f32).reshape(1, HG_HEADS, 1, HG_DIM)
    log_f = jnp.logaddexp(jnp.log(lbh + LB_TINY), jnp.log1p(-lbh) + jax.nn.log_sigmoid(flh))
    kh = -jnp.expm1(log_f)
    nc = S // HG_CHUNK

    def chunks(t):
        return t.reshape(B, HG_HEADS, nc, HG_CHUNK, HG_DIM).transpose(2, 0, 1, 3, 4)

    ar = jnp.arange(HG_CHUNK)
    causal = (ar[:, None] >= ar[None, :])[:, :, None]

    def step(state, xs):
        qc, kc, vc, lfc = xs
        b = jnp.cumsum(lfc, axis=2)
        diff = jnp.where(causal, b[:, :, :, None, :] - b[:, :, None, :, :], 0.0)
        decay = jnp.where(causal, jnp.exp(diff), 0.0)
        a = jnp.einsum('bhtd,bhsd,bhtsd->bhts', qc, kc, decay)
        o = jnp.einsum('bhts,bhse->bhte', a, vc) + jnp.einsum('bhtd,bhde->bhte', qc * jnp.exp(b), state)
        b_last = b[:, :, -1:, :]
        new_state = jnp.exp(b_last[:, :, 0, :])[..., None] * state + jnp.einsum('bhsd,bhse->bhde', kc * jnp.exp(b_last - b), vc)
        return new_state, o

    s0 = jnp.zeros((B, HG_HEADS, HG_DIM, HG_DIM), f32)
    _, o = lax.scan(step, s0, (chunks(qh), chunks(kh), chunks(vh), chunks(log_f)))
    o = o.transpose(1, 2, 0, 3, 4).reshape(B, HG_HEADS, S, HG_DIM)
    o = o * lax.rsqrt(jnp.mean(o * o, axis=-1, keepdims=True) + EPS)
    o = o.transpose(0, 2, 1, 3).reshape(B, S, HG_W) * jax.nn.silu(g.astype(f32))
    return o.astype(dt)

def setup_inputs(seed: int = 0) -> dict:
    key = jax.random.key(seed)
    ks = jax.random.split(key, 18)
    f32 = jnp.float32

    def nrm(k, shape, fan_in):
        return jax.random.normal(k, shape, f32) * (fan_in ** -0.5)

    def gain(k, shape):
        return 1.0 + 0.05 * jax.random.normal(k, shape, f32)

    return {
        'x': jax.random.normal(ks[0], (BATCH, SEQ, D_MODEL), f32),
        'p': jax.random.normal(ks[1], (DEPTH, BATCH, SEQ, PLE_DIM), f32),
        'w_in': nrm(ks[2], (DEPTH, D_MODEL, IN_TOTAL), D_MODEL),
        'w_out': nrm(ks[3], (DEPTH, MIX_W, D_MODEL), MIX_W),
        'cmp_pos': 0.02 * jax.random.normal(ks[4], (DEPTH, 2, CMP_BLOCK, HEAD_DIM), f32),
        'cmp_w1': nrm(ks[5], (DEPTH, 2, CMP_BLOCK * HEAD_DIM, CMP_HIDDEN), CMP_BLOCK * HEAD_DIM),
        'cmp_w2': nrm(ks[6], (DEPTH, 2, CMP_HIDDEN, HEAD_DIM), CMP_HIDDEN),
        'hg_lb': 0.1 * jax.random.normal(ks[7], (DEPTH, HG_W), f32),
        'g_pre_mix': gain(ks[8], (DEPTH, D_MODEL)),
        'g_post_mix': gain(ks[9], (DEPTH, D_MODEL)),
        'g_pre_mlp': gain(ks[10], (DEPTH, D_MODEL)),
        'g_post_mlp': gain(ks[11], (DEPTH, D_MODEL)),
        'w_up': nrm(ks[12], (DEPTH, D_MODEL, D_FF), D_MODEL),
        'w_down': nrm(ks[13], (DEPTH, D_FF, D_MODEL), D_FF),
        'g_ple': gain(ks[14], (DEPTH, D_MODEL)),
        'w_ple_gate': nrm(ks[15], (DEPTH, D_MODEL, D_MODEL), D_MODEL),
        'w_ple_proj': nrm(ks[16], (DEPTH, PLE_DIM, D_MODEL), PLE_DIM),
    }

def reference(x, p, w_in, w_out, cmp_pos, cmp_w1, cmp_w2, hg_lb, g_pre_mix, g_post_mix,
              g_pre_mlp, g_post_mlp, w_up, w_down, g_ple, w_ple_gate, w_ple_proj):
    nsa_slopes, dil_slopes = _alibi_slopes()
    sm = jax.nn.softmax(hg_lb.astype(jnp.float32), axis=0)
    lower_bounds = jnp.maximum(jnp.cumsum(sm, axis=0) - sm[0:1], 0.0)
    split_pts = [int(v) for v in np.cumsum(IN_WIDTHS)[:-1]]
    h = x
    for l in range(DEPTH):
        hn = _rmsnorm(h, g_pre_mix[l])
        proj = hn @ w_in[l]
        (nq, nkc, nvc, nks, nvs, nkw, nvw, ngate, dq, dk, dv, hq, hf, hi, hg) = jnp.split(proj, split_pts, axis=-1)
        o_nsa = _nsa(nq, nkc, nvc, nks, nvs, nkw, nvw, ngate, cmp_pos[l], cmp_w1[l], cmp_w2[l], nsa_slopes)
        o_dil = _dilated(dq, dk, dv, dil_slopes)
        o_hg = _hgrn2(hq, hf, hi, hg, lower_bounds[l])
        mix = jnp.concatenate([o_nsa, o_dil, o_hg], axis=-1) @ w_out[l]
        h = h + _rmsnorm(mix, g_post_mix[l])
        hn = _rmsnorm(h, g_pre_mlp[l])
        u = jnp.square(jax.nn.relu(hn @ w_up[l]))
        h = h + _rmsnorm(u @ w_down[l], g_post_mlp[l])
        gate = jax.nn.sigmoid(_rmsnorm(h, g_ple[l]) @ w_ple_gate[l])
        h = h + (p[l] @ w_ple_proj[l]) * gate
    return h


_drawn_inputs = setup_inputs


def setup_inputs(seed=0):
    import zlib

    import numpy as np

    out = dict(_drawn_inputs(seed))
    spreads = {}
    factors = {'cmp_pos': 6.727, 'g_ple': 23.925}
    for name, (base, spread) in spreads.items():
        noise = np.random.default_rng([zlib.crc32(name.encode()), seed]).standard_normal(out[name].shape)
        drawn = base * np.exp(spread * noise) if base else spread * noise
        out[name] = jnp.asarray(drawn.astype(out[name].dtype))
    for name, factor in factors.items():
        out[name] = (out[name] * factor).astype(out[name].dtype)
    return out
```

```python
import concourse.bass as bass
from concourse import mybir
from contextlib import ExitStack
import numpy as np

P = 128
SEQ, DM, DFF, PLE = 512, 1024, 4096, 256
TT = SEQ // P
KT = DM // P
HD = 64
NH, NKV, NG = 6, 2, 3
CB, CS, NC, NCP = 32, 16, 31, 32
DIL = 4
HGH = 4
PAN = 2048
EPS = 1e-6
NEG = -1e30
X_SPLIT = -40.0
LOG_TINY = float(np.log(1e-30))

N_IN = 18
G_OUT = N_IN
G_PLE = G_OUT + 4
G_MLP = G_PLE + 1
EIGHTHS = 8
G_GATE = G_MLP + 4 * EIGHTHS
N_PANELS = G_GATE + 4

C_NQ, C_KC, C_KS, C_VS, C_KW, C_VW, C_GT = 0, 384, 640, 768, 896, 1024, 1152
C_DQ, C_DK, C_DV, C_HQ, C_HF, C_HI, C_HG = 1170, 1554, 1938, 2322, 2578, 2834, 3090

D0W = SEQ + 4
TB_D0 = 0
TB_D12 = TB_D0 + 2 * D0W
TB_NSA = TB_D12 + 2 * 256
TB_CMP = TB_NSA + NH * SEQ
TB_RST = TB_CMP + NKV * TT * NG * NCP
TB_W = TB_RST + SEQ

LEVELS = (2, 4, 8, 16, 32, 64, 128)
HGC = 64


def slopes():
    n = 12
    s = (2.0 ** (-8.0 * np.arange(1, n + 1) / n)).reshape(-1, 4)
    return s[:, 2:].reshape(-1).astype(np.float32), s[:, :2].reshape(-1).astype(np.float32)


def constant_table():
    nsa, dil = slopes()
    t = np.zeros((P, TB_W), np.float32)
    p = np.arange(P)[:, None]
    rel = p + 384 - np.arange(SEQ)[None, :]
    for h in range(NH):
        t[:, TB_NSA + h * SEQ:TB_NSA + (h + 1) * SEQ] = np.where(rel >= 0, nsa[h] * rel.astype(np.float32), -NEG)
    for hh in range(2):
        rel = DIL * p + 3 - np.arange(D0W)[None, :]
        t[:, TB_D0 + hh * D0W:TB_D0 + (hh + 1) * D0W] = np.where(
            (rel >= 0) & (rel <= 128), dil[hh] * rel.astype(np.float32), -NEG)
        rel = DIL * (p - np.arange(P)[None, :])
        o = TB_D12 + hh * 256
        t[:, o:o + P] = np.where(rel >= 0, dil[2 + hh] * rel.astype(np.float32), -NEG)
        t[:, o + P:o + 256] = np.where((rel >= 0) & (rel % 16 == 0), dil[4 + hh] * rel.astype(np.float32), -NEG)
    for k in range(NKV):
        for i in range(TT):
            for g in range(NG):
                o = TB_CMP + ((k * TT + i) * NG + g) * NCP
                n = np.arange(NCP)[None, :]
                tok = i * P + p
                d = np.abs(tok - (n * CS + 0.5 * (CB - 1))).astype(np.float32)
                ok = (n * CS + CB - 1 <= tok) & (n < NC)
                t[:, o:o + NCP] = np.where(ok, nsa[k * NG + g] * d, -NEG)
    t[:, TB_RST:TB_RST + SEQ] = (np.arange(SEQ) % HGC != 0)
    return t


def level_masks():
    s, q = np.arange(P)[:, None], np.arange(P)[None, :]
    m = [(s // L == q // L) & (q // (L // 2) == s // (L // 2) + 1) for L in LEVELS]
    return np.stack(m, 1).astype(np.int32)


def build(nc, xT, xn, wst, pT, gpre, gvec, gpost, pos, w2, ctab, lmask, eye, out):
    fp32, f32r, i32 = mybir.dt.float32, mybir.dt.float32r, mybir.dt.int32
    ALU, ACT, AX = mybir.AluOpType, mybir.ActivationFunctionType, mybir.AxisListType
    ctx = ExitStack()
    with ctx:
        def sb(name, shape, dt):
            return ctx.enter_context(nc.sbuf_tensor(name, shape, dt))

        def sem(name):
            return ctx.enter_context(nc.semaphore(name))

        raw = sb("raw", [P, 2, PAN], fp32)
        Whi = sb("Whi", [P, 2, PAN], f32r)
        Wlo = sb("Wlo", [P, 2, PAN], f32r)
        Xhi = sb("Xhi", [P, KT, SEQ], f32r)
        Xlo = sb("Xlo", [P, KT, SEQ], f32r)
        Uhi = sb("Uhi", [P, 4, SEQ], f32r)
        Ulo = sb("Ulo", [P, 4, SEQ], f32r)
        AW = 26400
        arena = sb("arena", [P, AW], fp32)
        PB = [ctx.enter_context(nc.psum_tensor(f"bank{i}", [P, 512], fp32)) for i in range(8)]

        at = [0]

        def take(n):
            a = at[0]
            at[0] += n
            assert at[0] <= AW, at[0]
            return a

        def view(a, n):
            return arena[:, a:a + n]

        tab = view(take(TB_W), TB_W)
        aT = take(11 * SEQ)
        T = view(aT, 11 * SEQ).rearrange("p (j t) -> p j t", t=SEQ)
        Q0, KS, KW, DQ0, DK0 = 0, 3, 4, 5, 8
        V = view(take(5 * SEQ), 5 * SEQ).rearrange("p (v j e) -> p v j e", v=5, e=P)
        VS, VW, DV0 = 0, 1, 2
        HG = view(take(1024), 1024).rearrange("p (i c) -> p i c", i=TT)
        gates = view(take(72), 72)
        small = view(take(320), 320)
        kcT = view(take(NCP), NCP)
        vcR = view(take(128), 128).rearrange("p (k e) -> p k e", k=NKV)
        w2s = view(take(256), 256).rearrange("p (b j e) -> p b j e", b=2, j=2)
        aX = take(9728)
        HQ = view(aX, 1024).rearrange("p (j t) -> p j t", j=2)
        HF = view(aX + 1024, 1024).rearrange("p (j t) -> p j t", j=2)
        HI = view(aX + 2048, 1024).rearrange("p (i c) -> p i c", i=TT)
        tA, tB, tC, tD = (view(aX + 3072 + 1024 * n, 1024) for n in range(4))
        AD = view(aX + 7168, 2048).rearrange("p (h i t) -> p h i t", h=HGH, i=TT)
        AO = view(aT + DQ0 * SEQ, 3072).rearrange("p (h b t) -> p h b t", h=HGH, t=P)
        PT = view(aX, 8192).rearrange("p (a b j t) -> p a b j t", a=2, b=2, j=TT)
        SR = view(aX + 8192, 3 * SEQ).rearrange("p (a n) -> p a n", a=3)
        PC = view(aX, 768)
        PCT = HG.rearrange("p i c -> p (i c)").rearrange("p (k t) -> p k t", k=NKV)
        DPT = view(aX, 2 * 768).rearrange("p (a b t) -> p a b t", a=2, t=P)
        DSR = view(aX + 1536, 3 * 768).rearrange("p (a n) -> p a n", a=3)
        XT = view(aX, 4096).rearrange("p (k t) -> p k t", k=KT)
        sqs = view(aX + 4096, 1024).rearrange("p (a t) -> p a t", a=2)
        acc0 = view(aX + 5120, 512)
        rb = view(aX + 5632, 512)
        hn_t = view(aX + 6144, 1024).rearrange("p (a t) -> p a t", a=2)
        ones = view(aX + 7168, P)
        aC = aT + DQ0 * SEQ
        KCV = view(aC, 1024).rearrange("p (b t) -> p b t", b=2)
        KD = view(aC + 1024, 1024).rearrange("p (b a u) -> p b a u", b=2, a=2)
        CT = view(aC, 1984).rearrange("p (b m k n) -> p b m k n", b=2, m=16, k=NKV)
        CA = view(aC + 2048, 1024).rearrange("p (b k u) -> p b k u", b=2, k=NKV)
        CHa = take(2 * 2 * 62)
        CEXP = view(take(248), 248)
        CH = view(CHa, 248).rearrange("p (b j n) -> p b j n", b=2, j=2)
        assert 3 * 4096 + 2048 + 2048 + 3072 <= AW
        H = view(0, 4096).rearrange("p (i n) -> p i n", i=TT)
        Y = view(4096, 4096).rearrange("p (i n) -> p i n", i=TT)
        PR = view(8192, 4096).rearrange("p (i n) -> p i n", i=TT)
        GB = view(12288, 2048).rearrange("p (a n) -> p a n", a=2)
        tm = view(14336, 2048).rearrange("p (a n) -> p a n", a=2)
        junk = view(16384, 1024)
        relu = view(17408, 1024).rearrange("p (a n) -> p a n", a=2)
        usq = view(18432, 1024).rearrange("p (a n) -> p a n", a=2)
        pst = view(19456, 1024)
        Gsig = view(20480, 2048).rearrange("p (a n) -> p a n", a=4)

        masks = sb("masks", [P, len(LEVELS), P], i32)
        ident_s = sb("ident_s", [P, P], fp32)
        gpre_s = sb("gpre_s", [P, KT], fp32)
        gvec_s = sb("gvec_s", [P, 2, KT], fp32)
        pos_s = sb("pos_s", [P, 2, 16], fp32)
        st = sb("st", [P, 64], fp32)

        ident = ident_s[:, :]
        ntab = tab[:, TB_NSA:TB_NSA + NH * SEQ].rearrange("p (h n) -> p h n", h=NH)
        d0tab = tab[:, TB_D0:TB_D0 + 2 * D0W].rearrange("p (h n) -> p h n", h=2)
        d12tab = tab[:, TB_D12:TB_D12 + 512].rearrange("p (h n) -> p h n", h=2)
        ctb = tab[:, TB_CMP:TB_CMP + 768].rearrange("p (k n) -> p k n", k=NKV)
        rst = tab[:, TB_RST:TB_RST + SEQ]

        mneg = small[:, 0:64]
        den = small[:, 64:128]
        rden = small[:, 128:192]
        cst = small[:, 192:216]
        csum = small[:, 216:240]
        hgs = small[:, 240:256]
        blk = small[:, 256:288]
        boff = small[:, 288:304]

        raw_in = [sem("raw_in0"), sem("raw_in1")]
        x_in = [sem(f"x_in{k}") for k in range(4)]
        const_in = sem("const_in")
        tab_in = sem("tab_in")
        small_in = sem("small_in")
        cmp_in = sem("cmp_in")
        res_in = sem("res_in")
        out_sent = sem("out_sent")
        hi_done = sem("hi_done")
        lo_done = sem("lo_done")
        half_done = sem("half_done")
        act_seq = sem("act_seq")
        dve_seq = sem("dve_seq")
        ones_set = sem("ones_set")
        sq_done = sem("sq_done")
        acc_done = sem("acc_done")
        ss_done = sem("ss_done")
        ms_done = sem("ms_done")
        sqrt_done = sem("sqrt_done")
        hn_f = sem("hn_f")
        hn_hi = sem("hn_hi")
        hn_lo = sem("hn_lo")
        job_done = sem("job_done")
        job_evac = sem("job_evac")
        kd_done = sem("kd_done")
        ct_done = sem("ct_done")
        ct_hi = sem("ct_hi")
        ct_lo = sem("ct_lo")
        hx = sem("hx")
        hy = sem("hy")
        hg_k = sem("hg_k")
        arg_done = sem("arg_done")
        dec_done = sem("dec_done")
        qk_done = sem("qk_done")
        hg_mm = sem("hg_mm")
        hg_ev = sem("hg_ev")
        hgo_mm = sem("hgo_mm")
        hgo_ev = sem("hgo_ev")
        oh_done = sem("oh_done")
        mixT_mm = sem("mixT_mm")
        mix_hi = sem("mix_hi")
        mix_lo = sem("mix_lo")
        ce = sem("ce")
        ch_done = sem("ch_done")
        c2_mm = sem("c2_mm")
        c2_ev = sem("c2_ev")
        cs_mm = sem("cs_mm")
        cs_ev = sem("cs_ev")
        cs_exp = sem("cs_exp")
        cs_p = sem("cs_p")
        ct_mm = sem("ct_mm")
        ct_ev = sem("ct_ev")
        s_mm = sem("s_mm")
        s_ev = sem("s_ev")
        p_exp = sem("p_exp")
        p_done = sem("p_done")
        t_mm = sem("t_mm")
        t_ev = sem("t_ev")
        pv_done = sem("pv_done")
        ds_mm = sem("ds_mm")
        ds_ev = sem("ds_ev")
        dp_exp = sem("dp_exp")
        dp_done = sem("dp_done")
        dt_mm = sem("dt_mm")
        dt_ev = sem("dt_ev")
        dpv_done = sem("dpv_done")
        y_mm = sem("y_mm")
        y_ev = sem("y_ev")
        pt_hi = sem("pt_hi")
        pt_lo = sem("pt_lo")
        n_ss = sem("n_ss")
        n_ms = sem("n_ms")
        n_sq = sem("n_sq")
        n_h = sem("n_h")
        n_xs = sem("n_xs")
        n_rs = sem("n_rs")
        n_tr = sem("n_tr")
        n_g = sem("n_g")
        n_hi = sem("n_hi")
        n_lo = sem("n_lo")
        up_mm = sem("up_mm")
        up_relu = sem("up_relu")
        up_sq = sem("up_sq")
        up_hi = sem("up_hi")
        up_lo = sem("up_lo")
        dn_mm = sem("dn_mm")
        dn_ev = sem("dn_ev")
        z_done = sem("z_done")
        gt_mm = sem("gt_mm")
        gt_sig = sem("gt_sig")
        o_done = sem("o_done")

        jobs = []

        def t_job(g, c, dst, scale=1.0):
            jobs.append((g, "T", c, P, None, dst, scale))

        def b_job(g, w, t, parts):
            jobs.append((g, "B", 0, w, t, parts, 1.0))

        for j in range(2):
            t_job(0, j * P, HF[:, j, :])
        for j in range(2):
            t_job(1, j * P, HQ[:, j, :])
        for b in range(2):
            t_job(2, b * P, KCV[:, b, :])
        for t in range(TT):
            b_job(4, 512, t, [(0, 256, HI[:, t, :]), (256, 256, V[:, VS:VW + 1, t, :])])
        for t in range(TT):
            b_job(6, 402, t, [(0, 256, HG[:, t, :]), (256, P, V[:, DV0, t, :]), (384, 18, gates[:, 18 * t:18 * t + 18])])
        for j in range(2):
            t_job(7, j * P, T[:, Q0 + j, :], -HD ** -0.5)
        t_job(8, 0, T[:, Q0 + 2, :], -HD ** -0.5)
        t_job(8, P, T[:, KS, :])
        t_job(9, 0, T[:, KW, :])
        dv = [V[:, DV0 + g].rearrange("p j e -> p (j e)") for g in (1, 2)]
        t_job(9, P, dv[0])
        t_job(10, 0, dv[1])
        for g in range(2):
            jobs.append((11, "X", 0, P, g, V[:, DV0 + 1 + g], 1.0))
        for b in range(2):
            for j in range(2):
                jobs.append((12 + 2 * b, "H", j * P, b, None, CH[:, b, j, :], 1.0))
        for j in range(2):
            t_job(15, j * P, T[:, DQ0 + j, :], -HD ** -0.5)
        t_job(16, 0, T[:, DQ0 + 2, :], -HD ** -0.5)
        t_job(16, P, T[:, DK0, :])
        for j in range(2):
            t_job(17, j * P, T[:, DK0 + 1 + j, :])
        panel_jobs = {g: [n for n, j in enumerate(jobs) if j[0] == g] for g in range(N_IN)}
        jobs_by = [sum(1 for j in jobs if j[0] <= g) for g in range(N_IN)]

        LEVEL_AT = {0: 3, 1: 4, 2: 5, 3: 6, 4: 7, 5: 8, 6: 9, 7: 11, 8: 13, 9: 14}
        steps = [("norm0",), ("split", 0), ("scale0",), ("split", 1)]
        for g in range(N_IN):
            steps.append(("gemm", g))
            here = [lev for lev in LEVEL_AT if LEVEL_AT[lev] == g]
            if here:
                steps.append(("level_mm", here[0]))
            if g == 15:
                steps += [("hg_values",), ("cmp_mlp",)]
            if g == 16:
                steps.append(("cmp_scores",))
            steps.append(("split", g + 2))
            if g == 1:
                steps.append(("decay",))
            if g == 2:
                steps.append(("cmp_im2col",))
            if here and here[0] < 9:
                steps.append(("level", here[0] + 1))
        steps += [("hg_mix",), ("cmp_turn",), ("nsa",), ("dil",)]
        PAIRS = (3, 5, 11, 13)

        def last_use(g):
            if g in PAIRS:
                return half_done, PAIRS.index(g) + 1
            if g < N_IN:
                return job_done, jobs_by[g]
            if g < G_PLE:
                c = g - G_OUT
                return (half_done, 5 + c // 2) if c % 2 == 0 else (y_mm, 2 * c + 2)
            if g == G_PLE:
                return y_mm, 16
            if g < G_GATE:
                q = g - G_MLP
                e, c = q // 4, q % 4
                return (up_mm, 4 * e + 2 * c + 2) if c < 2 else (dn_mm, 8 * e + 4 * (c - 2) + 4)
            c = g - G_GATE
            return (half_done, 7 + c // 2) if c % 2 == 0 else (gt_mm, 2 * c + 2)

        NLEV = 10

        HGB = (4, 5, 6, 7)
        rows = [(h, b, i) for h in range(NH) for b in range(2) for i in range(TT)]
        ROWB, TRB, OB = (0, 1, 2), (3, 4, 5), (6, 7)
        drows = [(r, hh) for r in range(DIL) for hh in range(2)]

        block = ctx.enter_context(nc.Block())

        @block.sync
        def _(sp):
            def load_panel(g):
                if g >= 2:
                    sp.wait_ge(lo_done, g - 1)
                sp.dma_start(raw[:, g % 2, :], wst[g]).then_inc(raw_in[g % 2], 16)

            for k in range(4):
                sp.dma_start(XT[:, 2 * k:2 * k + 2, :], xT[:, 2 * k:2 * k + 2, :]).then_inc(x_in[k], 16)
            load_panel(0)
            load_panel(1)
            sp.dma_start(masks[:, :, :], lmask).then_inc(const_in, 16)
            sp.dma_start(ident, eye).then_inc(const_in, 16)
            for g in range(2, N_IN + 2):
                load_panel(g)
                if g == 4:
                    sp.wait_ge(kd_done, 1)
                    for b in range(2):
                        for par in range(2):
                            for k in range(NKV):
                                sp.dma_start(CA[par * HD:(par + 1) * HD, b, k, :],
                                             KD[k * HD:(k + 1) * HD, b, par, :]).then_inc(cmp_in, 16)
            sp.wait_ge(dpv_done, len(drows))
            sp.wait_ge(mix_lo, KT)
            sp.dma_start(H, xn.rearrange("(i p) n -> p i n", p=P)).then_inc(res_in, 16)
            sp.dma_start(pst, pT).then_inc(res_in, 16)
            for a in range(2):
                sp.dma_start(GB[:, a, :], gpost[a:a + 1, :].partition_broadcast(P)).then_inc(res_in, 16)
            for g in range(N_IN + 2, G_MLP + 2):
                load_panel(g)
            with sp.Fori(0, EIGHTHS // 2) as i:
                for c in range(8):
                    sp.wait_ge(lo_done, G_MLP + 2 + c - 1 + i * 8)
                    sp.dma_start(raw[:, (G_MLP + c) % 2, :],
                                 wst[bass.ds(G_MLP + 2 + c + i * 8, 1), :, :].rearrange("o p n -> (o p) n")
                                 ).then_inc(raw_in[(G_MLP + c) % 2], 16)
            for g in range(G_GATE + 2, N_PANELS):
                load_panel(g)
            for n in range(8):
                sp.wait_ge(o_done, n + 1)
                t, nh = n % TT, n // TT
                sp.dma_start(out[t * P:(t + 1) * P, nh * 512:(nh + 1) * 512],
                             H[:, t, nh * 512:(nh + 1) * 512]).then_inc(out_sent, 16)
            sp.wait_ge(out_sent, 128)

        @block.gpsimd
        def _(pool):
            pool.dma_start(gpre_s[:, :], gpre).then_inc(small_in, 16)
            pool.dma_start(gvec_s[:, :, :], gvec).then_inc(small_in, 16)
            pool.dma_start(pos_s[:, :, :], pos).then_inc(small_in, 16)
            pool.dma_start(w2s, w2).then_inc(small_in, 16)
            pool.dma_start(tab, ctab).then_inc(tab_in, 16)
            nc.gpsimd.memset(ones, 1.0).then_inc(ones_set, 1)
            nc.gpsimd.memset(kcT, 0.0).then_inc(z_done, 1)
            nc.gpsimd.memset(vcR, 0.0).then_inc(z_done, 1)
            pool.wait_ge(n_h, TT)
            nc.gpsimd.memset(Y, 0.0).then_inc(dn_ev, 1)

        @block.scalar
        def _(act):
            seq = [0]

            def link(ins):
                seq[0] += 1
                ins.then_inc(act_seq, 1)
                act.wait_ge(act_seq, seq[0])

            def hi(g, count=None):
                act.wait_ge(raw_in[g % 2], 16 * (g // 2 + 1) if count is None else count)
                if count is None and g >= 2:
                    act.wait_ge(*last_use(g - 2))
                nc.scalar.activation(Whi[:, g % 2, :], raw[:, g % 2, :], ACT.Copy).then_inc(hi_done, 1)

            for step in steps:
                if step[0] == "norm0":
                    for k in range(KT):
                        if k % 2 == 0:
                            act.wait_ge(x_in[k // 2], 16)
                        if k >= 2:
                            act.wait_ge(acc_done, k - 1)
                        nc.scalar.activation(sqs[:, k % 2, :], XT[:, k, :], ACT.Square).then_inc(sq_done, 1)
                elif step[0] == "scale0":
                    act.wait_ge(ms_done, 1)
                    nc.scalar.activation(rb, rb, ACT.Sqrt).then_inc(sqrt_done, 1)
                    for k in range(KT):
                        act.wait_ge(hn_f, k + 1)
                        nc.scalar.activation(Xhi[:, k, :], hn_t[:, k % 2, :], ACT.Copy).then_inc(hn_hi, 1)
                elif step[0] == "split":
                    hi(step[1])
                elif step[0] == "gemm":
                    for n in panel_jobs[step[1]]:
                        _, kind, _, w, tiles, dst, scale = jobs[n]
                        act.wait_ge(job_done, n + 1)
                        if step[1] == 15:
                            act.wait_ge(hgo_mm, 2)
                        src = PB[n % 4][:, :]
                        if kind == "B":
                            for a, (c, cw, part) in enumerate(dst):
                                piece = src[:, c:c + cw]
                                if cw == 256 and c:
                                    piece = piece.rearrange("p (v e) -> p v e", v=2)
                                ins = nc.scalar.activation(part, piece, ACT.Copy)
                            ins.then_inc(job_evac, 1)
                            continue
                        if kind == "H":
                            src = src[:, 0:2 * NC]
                        elif kind == "X":
                            src = src.rearrange("p (r e) -> p r e", e=P)
                        nc.scalar.activation(dst, src, ACT.Copy, scale=scale).then_inc(job_evac, 1)
                elif step[0] == "decay":
                    act.wait_ge(hx, 1)
                    nc.scalar.activation(tB, tA, ACT.Exp, scale=-1.0).then_inc(hy, 1)
                    act.wait_ge(hx, 2)
                    link(nc.scalar.activation(tA, tA, ACT.Exp))
                    nc.scalar.activation(tA, tA, ACT.Ln, bias=1.0).then_inc(hy, 1)
                    act.wait_ge(hy, 1)
                    nc.scalar.activation(tD, tB, ACT.Ln, bias=1.0).then_inc(hy, 1)
                elif step[0] == "level":
                    act.wait_ge(arg_done, step[1])
                    nc.scalar.activation(tA, tA, ACT.Exp).then_inc(dec_done, 1)
                elif step[0] == "cmp_im2col":
                    act.wait_ge(ct_done, 1)
                    nc.scalar.activation(Uhi[:, :, :].rearrange("p a t -> p (a t)")[:, 0:1984],
                                         view(aC, 1984), ACT.Copy).then_inc(ct_hi, 1)
                elif step[0] == "cmp_mlp":
                    act.wait_ge(job_evac, jobs_by[14])
                    nc.scalar.activation(CEXP, view(CHa, 248), ACT.Exp, scale=-1.0).then_inc(ce, 1)
                elif step[0] == "hg_values":
                    for a in range(2):
                        act.wait_ge(hgo_mm, a + 1)
                        nc.scalar.activation(tA[:, a * 512:(a + 1) * 512], PB[HGB[a]][:, :], ACT.Copy).then_inc(hgo_ev, 1)
                    act.wait_ge(hx, 4)
                    nc.scalar.activation(hgs, hgs, ACT.Sqrt).then_inc(hy, 1)
                    nc.scalar.activation(tC, HG.rearrange("p i c -> p (i c)"), ACT.Exp, scale=-1.0).then_inc(hy, 1)
                elif step[0] == "hg_mix":
                    for j in range(2):
                        act.wait_ge(mixT_mm, j + 1)
                        nc.scalar.activation(Xhi[:, 6 + j, :], PB[HGB[2 + j]][:, :], ACT.Copy).then_inc(mix_hi, 1)
                elif step[0] == "cmp_scores":
                    act.wait_ge(job_evac, jobs_by[6])
                    nc.scalar.activation(gates, gates, ACT.Exp, scale=-1.0).then_inc(ce, 1)
                    act.wait_ge(cs_ev, 1)
                    nc.scalar.activation(PC, PC, ACT.Exp, scale=-1.0).then_inc(cs_exp, 1)
                elif step[0] == "cmp_turn":
                    for k in range(NKV):
                        act.wait_ge(ct_mm, k + 1)
                        nc.scalar.activation(PCT[0:96, k, :], PB[4 + k][0:96, :], ACT.Copy).then_inc(ct_ev, 1)
                elif step[0] == "nsa":
                    def t_copy(n):
                        h, b, i = rows[n]
                        act.wait_ge(t_mm, n + 1)
                        if i == 0 and b == 0 and h >= 2:
                            act.wait_ge(pv_done, h - 1)
                        nc.scalar.activation(PT[:, h % 2, b, 0:i + 1, i * P:(i + 1) * P],
                                             PB[TRB[n % 3]][:, 0:(i + 1) * P].rearrange("p (j t) -> p j t", t=P),
                                             ACT.Copy).then_inc(t_ev, 1)

                    def mix_evac(j):
                        act.wait_ge(pv_done, 2 * j + 2)
                        nc.scalar.activation(Xhi[:, j, :], PB[OB[j % 2]][:, :], ACT.Copy).then_inc(mix_hi, 1)

                    for n in range(len(rows) + 4):
                        if n < len(rows):
                            w = (rows[n][2] + 1) * P
                            act.wait_ge(s_ev, n + 1)
                            nc.scalar.activation(SR[:, n % 3, 0:w], SR[:, n % 3, 0:w], ACT.Exp,
                                                 bias=mneg[:, n:n + 1], scale=-1.0,
                                                 accum_out=den[:, n:n + 1]).then_inc(p_exp, 1)
                        if 2 <= n < len(rows) + 2:
                            t_copy(n - 2)
                        if n >= 19 and (n - 19) % 16 == 0:
                            mix_evac((n - 19) // 16)
                elif step[0] == "dil":
                    def dt_copy(n):
                        if n >= 2:
                            act.wait_ge(dpv_done, n - 1)
                        act.wait_ge(dt_mm, n + 1)
                        nc.scalar.activation(DPT[:, n % 2, 0:4, :], PB[3][:, :].rearrange("p (j t) -> p j t", t=P), ACT.Copy
                                             ).then_inc(dt_ev, 1)
                        nc.scalar.activation(DPT[:, n % 2, 4:6, :], PB[4][:, 0:256].rearrange("p (j t) -> p j t", t=P),
                                             ACT.Copy).then_inc(dt_ev, 1)

                    for n in range(len(drows) + 1):
                        if n < len(drows):
                            act.wait_ge(ds_ev, n + 1)
                            nc.scalar.activation(DSR[:, n % 3, :], DSR[:, n % 3, :], ACT.Exp,
                                                 bias=mneg[:, 48 + n:49 + n], scale=-1.0,
                                                 accum_out=den[:, 48 + n:49 + n]).then_inc(dp_exp, 1)
                        if n >= 1:
                            dt_copy(n - 1)
                    act.wait_ge(dpv_done, len(drows))
                    for g in range(3):
                        nc.scalar.activation(Xhi[:, 3 + g, :].rearrange("p (i r) -> p i r", r=DIL),
                                             PB[5 + g][:, :].rearrange("p (r i) -> p i r", r=DIL),
                                             ACT.Copy).then_inc(mix_hi, 1)

            act.wait_ge(res_in, 64)
            for c in range(4):
                hi(G_OUT + 2 + c)
                if c == 1:
                    nc.scalar.activation(Uhi[:, 0:2, :], pst.rearrange("p (a t) -> p a t", a=2), ACT.Copy).then_inc(pt_hi, 1)

            def post_norm(a, first):
                for t in range(TT):
                    k = a * TT + t
                    if a == 0:
                        act.wait_ge(y_ev, 4 + t + 1)
                    else:
                        act.wait_ge(dn_ev, 1 + 8 * (EIGHTHS - 1) + 4 + t + 1)
                    nc.scalar.activation(junk, Y[:, t, :], ACT.Square, accum_out=st[:, k:k + 1]).then_inc(n_ss, 1)
                    act.wait_ge(n_ms, 2 * k + 1)
                    nc.scalar.activation(st[:, 8 + k:9 + k], st[:, 8 + k:9 + k], ACT.Sqrt).then_inc(n_sq, 1)
                    act.wait_ge(n_h, k + 1)
                    nc.scalar.activation(junk, H[:, t, :], ACT.Square, accum_out=st[:, 16 + k:17 + k]).then_inc(n_ss, 1)
                    act.wait_ge(n_ms, 2 * k + 2)
                    nc.scalar.activation(st[:, 24 + k:25 + k], st[:, 24 + k:25 + k], ACT.Sqrt).then_inc(n_sq, 1)
                    act.wait_ge(n_rs, k + 1)
                    if k >= 2:
                        act.wait_ge(n_tr, 2 * (k - 1))
                    nc.scalar.activation(tm[:, k % 2, :], H[:, t, :], ACT.Copy, scale=st[:, 24 + k:25 + k]).then_inc(n_xs, 1)
                    for b in range(2):
                        act.wait_ge(n_g, 2 * k + b + 1)
                        nc.scalar.activation(Xhi[:, 4 * b:4 * b + 4, t * P:(t + 1) * P],
                                             usq[:, b, :].rearrange("p (k t) -> p k t", t=P), ACT.Copy).then_inc(n_hi, 1)

            post_norm(0, True)

            act.wait_ge(y_mm, 16)
            hi(G_MLP + 1)
            with act.Fori(0, EIGHTHS // 2) as i:
                for e in range(2):
                    for c in range(4):
                        if c < 2:
                            for f in range(2 * c, 2 * c + 2):
                                u = 4 * e + f
                                act.wait_ge(up_mm, i * 8 + u + 1)
                                bank = PB[(0 if e == 0 else 4) + f]
                                nc.scalar.activation(relu[:, f % 2, :], bank[:, :], ACT.Relu).then_inc(up_relu, 1)
                                act.wait_ge(up_sq, i * 8 + u + 1)
                                nc.scalar.activation(Uhi[:, f, :], usq[:, f % 2, :], ACT.Copy).then_inc(up_hi, 1)
                        g = G_MLP + 2 + 4 * e + c
                        if c < 2:
                            act.wait_ge(up_mm, i * 8 + 4 * e + 2 * c + 2)
                        else:
                            act.wait_ge(dn_mm, i * 16 + 8 * e + 4 * (c - 2) + 4)
                        hi(g, i * 64 + 16 * (g // 2 + 1))

            post_norm(1, False)
            for g in range(G_GATE + 2, N_PANELS):
                hi(g)
            for n in range(8):
                act.wait_ge(gt_mm, n + 1)
                if n >= 4:
                    act.wait_ge(o_done, n - 3)
                nc.scalar.activation(Gsig[:, n % 4, :], PB[n][:, :], ACT.Sigmoid).then_inc(gt_sig, 1)

        @block.vector
        def _(dve):
            seq = [0]

            def link(ins):
                seq[0] += 1
                ins.then_inc(dve_seq, 1)
                dve.wait_ge(dve_seq, seq[0])

            def lo(g, count=None):
                dve.wait_ge(hi_done, g + 1 if count is None else count)
                nc.vector.tensor_tensor(Wlo[:, g % 2, :], raw[:, g % 2, :], Whi[:, g % 2, :].bitcast(fp32),
                                        ALU.subtract).then_inc(lo_done, 1)

            V2 = nc.vector
            for step in steps:
                if step[0] == "norm0":
                    for k in range(KT):
                        dve.wait_ge(sq_done, k + 1)
                        if k >= 1:
                            dve.wait_ge(acc_done, k)
                        if k == 0:
                            V2.tensor_copy(acc0, sqs[:, 0, :]).then_inc(acc_done, 1)
                        else:
                            V2.tensor_tensor(acc0, acc0, sqs[:, k % 2, :], ALU.add).then_inc(acc_done, 1)
                elif step[0] == "scale0":
                    dve.wait_ge(ss_done, 1)
                    V2.tensor_scalar(rb, PB[0][:, :], 1.0 / DM, EPS, ALU.mult, ALU.add).then_inc(ms_done, 1)
                    dve.wait_ge(sqrt_done, 1)
                    link(V2.reciprocal(rb, rb))
                    dve.wait_ge(small_in, 64)
                    for k in range(KT):
                        if k >= 2:
                            dve.wait_ge(hn_lo, k - 1)
                        V2.scalar_tensor_tensor(out=hn_t[:, k % 2, :], in0=XT[:, k, :], scalar=gpre_s[:, k:k + 1],
                                                in1=rb, op0=ALU.mult, op1=ALU.mult).then_inc(hn_f, 1)
                        if k >= 1:
                            dve.wait_ge(hn_hi, k)
                            V2.tensor_tensor(Xlo[:, k - 1, :], hn_t[:, (k - 1) % 2, :],
                                             Xhi[:, k - 1, :].bitcast(fp32), ALU.subtract).then_inc(hn_lo, 1)
                    dve.wait_ge(hn_hi, KT)
                    V2.tensor_tensor(Xlo[:, KT - 1, :], hn_t[:, (KT - 1) % 2, :],
                                     Xhi[:, KT - 1, :].bitcast(fp32), ALU.subtract).then_inc(hn_lo, 1)
                elif step[0] == "split":
                    lo(step[1])
                elif step[0] == "decay":
                    hf = HF.rearrange("p j t -> p (j t)")
                    dve.wait_ge(job_evac, jobs_by[0])
                    V2.tensor_scalar(tA, hf, X_SPLIT, None, ALU.max).then_inc(hx, 1)
                    dve.wait_ge(hy, 1)
                    V2.tensor_scalar(tA, hf, X_SPLIT, -LOG_TINY, ALU.min, ALU.add).then_inc(hx, 1)
                    V2.tensor_scalar(tC, hf, X_SPLIT, None, ALU.is_lt).then_inc(hx, 1)
                    dve.wait_ge(hx, 3)
                    link(V2.tensor_scalar(hf, tB, 1.0, None, ALU.add))
                    link(V2.reciprocal(hf, hf))
                    link(V2.tensor_tensor(hf, hf, tB, ALU.mult))
                    dve.wait_ge(hy, 2)
                    link(V2.scalar_tensor_tensor(out=tA, in0=tA, scalar=LOG_TINY - X_SPLIT, in1=tC,
                                                 op0=ALU.add, op1=ALU.mult))
                    dve.wait_ge(hy, 3)
                    link(V2.tensor_tensor(tA, tA, tD, ALU.subtract))
                    dve.wait_ge(const_in, 32)
                    dve.wait_ge(tab_in, 16)
                    for j in range(2):
                        link(V2.tensor_tensor_scan(tB[:, j * SEQ:(j + 1) * SEQ], rst, tA[:, j * SEQ:(j + 1) * SEQ],
                                                   0.0, ALU.mult, ALU.add))
                    V2.tensor_copy(blk[:, 0:16], tB.rearrange("p (c u) -> p c u", u=HGC)[:, :, HGC - 1]).then_inc(hg_k, 1)
                elif step[0] == "level":
                    lev = step[1]
                    dve.wait_ge(hg_k, 1)
                    if lev > 1:
                        dve.wait_ge(qk_done, lev - 1)
                    if lev <= 6:
                        L = LEVELS[lev - 1]
                        tb = tB.rearrange("p (n a u) -> p n a u", a=2, u=L // 2)
                        ta = tA.rearrange("p (n a u) -> p n a u", a=2, u=L // 2)
                        mid = tb[:, :, 0, L // 2 - 1:L // 2].broadcast_to([P, 1024 // L, L // 2])
                        V2.tensor_tensor(ta[:, :, 1, :], tb[:, :, 1, :], mid, ALU.subtract).then_inc(dve_seq, 1)
                        V2.tensor_tensor(ta[:, :, 0, :], mid, tb[:, :, 0, :], ALU.subtract).then_inc(arg_done, 1)
                        seq[0] += 1
                    else:
                        half = {7: 1, 8: 2, 9: 4}[lev]
                        bo = boff.rearrange("p (j c) -> p j c", j=2)
                        bl = blk[:, 0:16].rearrange("p (j c) -> p j c", j=2)
                        link(V2.memset(boff, 0.0))
                        for c0 in range(0, 8, 2 * half):
                            for c in range(c0 + half - 1, c0 - 1, -1):
                                nxt = bo[:, :, c + 1] if c < c0 + half - 1 else None
                                if nxt is None:
                                    link(V2.tensor_copy(bo[:, :, c], bl[:, :, c]))
                                else:
                                    link(V2.tensor_tensor(bo[:, :, c], bl[:, :, c], nxt, ALU.add))
                            for c in range(c0 + half + 1, c0 + 2 * half):
                                link(V2.tensor_tensor(bo[:, :, c], bl[:, :, c - 1], bo[:, :, c - 1], ALU.add))
                        tb = tB.rearrange("p (n a h u) -> p n a h u", a=2, h=half, u=HGC)
                        ta = tA.rearrange("p (n a h u) -> p n a h u", a=2, h=half, u=HGC)
                        ov = boff.rearrange("p (n a h) -> p n a h", a=2, h=half)
                        wide = [P, 8 // half, half, HGC]
                        V2.tensor_tensor(ta[:, :, 1], tb[:, :, 1], ov[:, :, 1, :].unsqueeze(3).broadcast_to(wide),
                                         ALU.add).then_inc(dve_seq, 1)
                        V2.tensor_tensor(ta[:, :, 0], ov[:, :, 0, :].unsqueeze(3).broadcast_to(wide), tb[:, :, 0],
                                         ALU.subtract).then_inc(arg_done, 1)
                        seq[0] += 1
                    dve.wait_ge(dec_done, lev)
                    dve.wait_ge(hg_mm, 4 * lev)
                    link(V2.tensor_tensor(tC, HQ.rearrange("p j t -> p (j t)"), tA, ALU.mult))
                    V2.tensor_tensor(tD, HF.rearrange("p j t -> p (j t)"), tA, ALU.mult).then_inc(qk_done, 1)
                elif step[0] == "level_mm":
                    lev = step[1]
                    for h in range(HGH):
                        n = 4 * lev + h
                        dve.wait_ge(hg_mm, n + 1)
                        pb = PB[HGB[h]][:, :]
                        pb3 = pb.rearrange("p (i t) -> p i t", t=P)
                        if lev == 0:
                            V2.tensor_tensor(AD[:, h], pb3, ident.unsqueeze(1).broadcast_to([P, TT, P]),
                                             ALU.mult).then_inc(hg_ev, 1)
                        elif lev <= 7:
                            dve.wait_ge(hg_ev, 4 * (lev - 1) + h + 1)
                            V2.copy_predicated(AD[:, h], masks[:, lev - 1, :].unsqueeze(1).broadcast_to([P, TT, P]),
                                               pb3).then_inc(hg_ev, 1)
                        elif lev == 8:
                            V2.tensor_copy(AO[:, h, 0:2, :], pb3[:, 0:2, :]).then_inc(hg_ev, 1)
                        else:
                            V2.tensor_copy(AO[:, h, 2:6, :], pb3).then_inc(hg_ev, 1)
                elif step[0] == "cmp_im2col":
                    dve.wait_ge(job_evac, jobs_by[2])
                    V2.tensor_copy(KD, KCV.rearrange("p b (u a) -> p b a u", a=2)).then_inc(kd_done, 1)
                    dve.wait_ge(cmp_in, 8 * 16)
                    last = None
                    for b in range(2):
                        for k in range(NKV):
                            for mh in range(2):
                                src = CA[:, b, k, :].rearrange("p (n m) -> p m n", m=8)[:, :, mh:mh + NC]
                                bias = pos_s[:, b, 8 * mh:8 * mh + 8].unsqueeze(2).broadcast_to([P, 8, NC])
                                ins = V2.tensor_tensor(CT[:, b, 8 * mh:8 * mh + 8, k, :], src, bias, ALU.add)
                                if b == 1 and k == 1 and mh == 1:
                                    ins.then_inc(ct_done, 1)
                    dve.wait_ge(ct_hi, 1)
                    dve.wait_ge(ct_done, 1)
                    V2.tensor_tensor(Ulo[:, :, :].rearrange("p a t -> p (a t)")[:, 0:1984], view(aC, 1984),
                                     Uhi[:, :, :].rearrange("p a t -> p (a t)")[:, 0:1984].bitcast(fp32),
                                     ALU.subtract).then_inc(ct_lo, 1)
                elif step[0] == "cmp_mlp":
                    dve.wait_ge(ce, 1)
                    link(V2.tensor_scalar(CEXP, CEXP, 1.0, None, ALU.add))
                    link(V2.reciprocal(CEXP, CEXP))
                    V2.tensor_tensor(view(CHa, 248), view(CHa, 248), CEXP, ALU.mult).then_inc(ch_done, 1)
                    dve.wait_ge(z_done, 2)
                    dve.wait_ge(c2_mm, 1)
                    V2.tensor_copy(kcT[:, 0:NC], PB[6][:, 0:NC]).then_inc(c2_ev, 1)
                    for g in range(NG):
                        V2.tensor_copy(vcR[32 * g:32 * g + NC], PB[7][32 * g:32 * g + NC, 0:128]
                                       .rearrange("p (k e) -> p k e", k=NKV)).then_inc(c2_ev, 1)
                elif step[0] == "hg_values":
                    dve.wait_ge(hgo_ev, 2)
                    link(V2.tensor_tensor(tB, tA, tA, ALU.mult))
                    link(V2.tensor_reduce(hgs, tB.rearrange("p (n e) -> p n e", e=HD), AX.X, ALU.add))
                    V2.tensor_scalar(hgs, hgs, 1.0 / HD, EPS, ALU.mult, ALU.add).then_inc(hx, 1)
                    dve.wait_ge(hy, 4)
                    link(V2.reciprocal(hgs, hgs))
                    link(V2.tensor_tensor(tA.rearrange("p (n e) -> p n e", e=HD), tA.rearrange("p (n e) -> p n e", e=HD),
                                          hgs.unsqueeze(2).broadcast_to([P, 16, HD]), ALU.mult))
                    dve.wait_ge(hy, 5)
                    link(V2.tensor_scalar(tC, tC, 1.0, None, ALU.add))
                    link(V2.reciprocal(tC, tC))
                    link(V2.tensor_tensor(tC, tC, HG.rearrange("p i c -> p (i c)"), ALU.mult))
                    V2.tensor_tensor(tD, tA, tC, ALU.mult).then_inc(oh_done, 1)
                elif step[0] == "hg_mix":
                    for j in range(2):
                        dve.wait_ge(mix_hi, j + 1)
                        V2.tensor_tensor(Xlo[:, 6 + j, :], PB[HGB[2 + j]][:, :], Xhi[:, 6 + j, :].bitcast(fp32),
                                         ALU.subtract).then_inc(mix_lo, 1)
                elif step[0] == "cmp_scores":
                    dve.wait_ge(ce, 2)
                    link(V2.tensor_scalar(gates, gates, 1.0, None, ALU.add))
                    link(V2.reciprocal(gates, gates))
                    for k in range(NKV):
                        dve.wait_ge(cs_mm, k + 1)
                        link(V2.tensor_tensor(PC[:, k * 384:(k + 1) * 384], PB[4 + k][:, 0:384], ctb[:, k, :], ALU.add))
                    pc3 = PC.rearrange("p (n c) -> p n c", c=NCP)
                    link(V2.tensor_reduce(cst, pc3, AX.X, ALU.min))
                    link(V2.tensor_scalar(cst, cst, 1e25, None, ALU.min))
                    V2.tensor_tensor(pc3, pc3, cst.unsqueeze(2).broadcast_to([P, 24, NCP]), ALU.subtract).then_inc(cs_ev, 1)
                    dve.wait_ge(cs_exp, 1)
                    link(V2.tensor_reduce(csum, pc3, AX.X, ALU.add))
                    link(V2.tensor_scalar(csum, csum, 1e-30, None, ALU.max))
                    link(V2.reciprocal(csum, csum))
                    for k in range(NKV):
                        gv = gates.rearrange("p (i k g b) -> p i k g b", i=TT, k=NKV, b=3)[:, :, k, :, 0]
                        cv = csum[:, k * 12:(k + 1) * 12].rearrange("p (i g) -> p i g", g=NG)
                        link(V2.tensor_tensor(cv, cv, gv, ALU.mult))
                    V2.tensor_tensor(pc3, pc3, csum.unsqueeze(2).broadcast_to([P, 24, NCP]), ALU.mult).then_inc(cs_p, 1)
                elif step[0] == "nsa":
                    gv = gates.rearrange("p (i h b) -> p i h b", h=NH, b=3)

                    def normalise(n):
                        h, b, i = rows[n]
                        w = (i + 1) * P
                        dve.wait_ge(p_exp, n + 1)
                        link(V2.reciprocal(rden[:, n:n + 1], den[:, n:n + 1]))
                        V2.tensor_scalar(SR[:, n % 3, 0:w], SR[:, n % 3, 0:w], rden[:, n:n + 1],
                                         gv[:, i, h, 1 + b:2 + b], ALU.mult, ALU.mult).then_inc(p_done, 1)

                    def mix_lo_part(j):
                        dve.wait_ge(mix_hi, 2 + j + 1)
                        V2.tensor_tensor(Xlo[:, j, :], PB[OB[j % 2]][:, :], Xhi[:, j, :].bitcast(fp32),
                                         ALU.subtract).then_inc(mix_lo, 1)

                    for n in range(len(rows) + 4):
                        if n < len(rows):
                            h, b, i = rows[n]
                            w = (i + 1) * P
                            dve.wait_ge(s_mm, n + 1)
                            if n >= 3:
                                dve.wait_ge(t_mm, n - 2)
                            V2.tensor_tensor_reduce(out=SR[:, n % 3, 0:w], in0=ntab[:, h, SEQ - w:SEQ],
                                                    in1=PB[ROWB[n % 3]][:, 0:w], scale=1.0, scalar=3e38,
                                                    op0=ALU.add, op1=ALU.min,
                                                    accum_out=mneg[:, n:n + 1]).then_inc(s_ev, 1)
                        if 1 <= n < len(rows) + 1:
                            normalise(n - 1)
                        if n >= 19 and (n - 19) % 16 == 0:
                            mix_lo_part((n - 19) // 16)
                elif step[0] == "dil":
                    def normalise(n):
                        dve.wait_ge(dp_exp, n + 1)
                        link(V2.reciprocal(rden[:, 48 + n:49 + n], den[:, 48 + n:49 + n]))
                        V2.tensor_scalar(DSR[:, n % 3, :], DSR[:, n % 3, :], rden[:, 48 + n:49 + n], None,
                                         ALU.mult).then_inc(dp_done, 1)

                    for n in range(len(drows) + 1):
                        if n < len(drows):
                            r, hh = drows[n]
                            dve.wait_ge(ds_mm, n + 1)
                            if n >= 3:
                                dve.wait_ge(dt_mm, n - 2)
                            link(V2.tensor_tensor_reduce(out=DSR[:, n % 3, 0:SEQ], in0=d0tab[:, hh, 3 - r:3 - r + SEQ],
                                                         in1=PB[n % 2][:, :],
                                                         scale=1.0, scalar=3e38, op0=ALU.add, op1=ALU.min,
                                                         accum_out=st[:, 32 + n:33 + n]))
                            link(V2.tensor_tensor_reduce(out=DSR[:, n % 3, SEQ:768], in0=d12tab[:, hh, :],
                                                         in1=PB[2][:, (n % 2) * 256:(n % 2 + 1) * 256],
                                                         scale=1.0, scalar=3e38, op0=ALU.add, op1=ALU.min,
                                                         accum_out=st[:, 40 + n:41 + n]))
                            V2.tensor_tensor(mneg[:, 48 + n:49 + n], st[:, 32 + n:33 + n], st[:, 40 + n:41 + n],
                                             ALU.min).then_inc(ds_ev, 1)
                        if n >= 1:
                            normalise(n - 1)
                    for g in range(3):
                        dve.wait_ge(mix_hi, 5 + g + 1)
                        V2.tensor_tensor(Xlo[:, 3 + g, :].rearrange("p (i r) -> p i r", r=DIL),
                                         PB[5 + g][:, :].rearrange("p (r i) -> p i r", r=DIL),
                                         Xhi[:, 3 + g, :].bitcast(fp32).rearrange("p (i r) -> p i r", r=DIL),
                                         ALU.subtract).then_inc(mix_lo, 1)

            dve.wait_ge(res_in, 64)
            for c in range(4):
                lo(G_OUT + 2 + c)
                if c == 1:
                    dve.wait_ge(pt_hi, 1)
                    V2.tensor_tensor(Ulo[:, 0:2, :], pst.rearrange("p (a t) -> p a t", a=2),
                                     Uhi[:, 0:2, :].bitcast(fp32), ALU.subtract).then_inc(pt_lo, 1)
                if c in (1, 3):
                    nh = c // 2
                    for t in range(TT):
                        dve.wait_ge(y_mm, 4 * nh + t + 1)
                        V2.tensor_copy(Y[:, t, nh * 512:(nh + 1) * 512], PB[4 * nh + t][:, :]).then_inc(y_ev, 1)

            def post_norm(a):
                for t in range(TT):
                    k = a * TT + t
                    dve.wait_ge(n_ss, 2 * k + 1)
                    V2.tensor_scalar(st[:, 8 + k:9 + k], st[:, k:k + 1], 1.0 / DM, EPS, ALU.mult, ALU.add).then_inc(n_ms, 1)
                    dve.wait_ge(n_sq, 2 * k + 1)
                    link(V2.reciprocal(st[:, 8 + k:9 + k], st[:, 8 + k:9 + k]))
                    link(V2.scalar_tensor_tensor(out=Y[:, t, :], in0=Y[:, t, :], scalar=st[:, 8 + k:9 + k],
                                                 in1=GB[:, a, :], op0=ALU.mult, op1=ALU.mult))
                    V2.tensor_tensor(H[:, t, :], H[:, t, :], Y[:, t, :], ALU.add).then_inc(n_h, 1)
                    dve.wait_ge(n_ss, 2 * k + 2)
                    V2.tensor_scalar(st[:, 24 + k:25 + k], st[:, 16 + k:17 + k], 1.0 / DM, EPS,
                                     ALU.mult, ALU.add).then_inc(n_ms, 1)
                    dve.wait_ge(n_sq, 2 * k + 2)
                    V2.reciprocal(st[:, 24 + k:25 + k], st[:, 24 + k:25 + k]).then_inc(n_rs, 1)
                    for b in range(2):
                        dve.wait_ge(n_tr, 2 * k + b + 1)
                        if k >= 1:
                            dve.wait_ge(n_hi, 2 * (k - 1) + b + 1)
                        V2.tensor_tensor(usq[:, b, :].rearrange("p (k t) -> p k t", t=P),
                                         PB[2 * (k % 2) + b][:, :].rearrange("p (k t) -> p k t", t=P),
                                         gvec_s[:, a, 4 * b:4 * b + 4].unsqueeze(2).broadcast_to([P, 4, P]),
                                         ALU.mult).then_inc(n_g, 1)
                        dve.wait_ge(n_hi, 2 * k + b + 1)
                        V2.tensor_tensor(Xlo[:, 4 * b:4 * b + 4, t * P:(t + 1) * P],
                                         usq[:, b, :].rearrange("p (k t) -> p k t", t=P),
                                         Xhi[:, 4 * b:4 * b + 4, t * P:(t + 1) * P].bitcast(fp32),
                                         ALU.subtract).then_inc(n_lo, 1)

            post_norm(0)
            for n in range(8):
                t, nh = n % TT, n // TT
                dve.wait_ge(y_mm, 8 + n + 1)
                V2.tensor_copy(PR[:, t, nh * 512:(nh + 1) * 512], PB[4 + n % 4][:, :]).then_inc(y_ev, 1)
            lo(G_MLP + 1)
            with dve.Fori(0, EIGHTHS // 2) as i:
                for e in range(2):
                    for c in range(4):
                        if c < 2:
                            for f in range(2 * c, 2 * c + 2):
                                u = 4 * e + f
                                dve.wait_ge(up_relu, i * 8 + u + 1)
                                if u:
                                    dve.wait_ge(up_lo, i * 8 + u)
                                V2.tensor_tensor(usq[:, f % 2, :], relu[:, f % 2, :], relu[:, f % 2, :],
                                                 ALU.mult).then_inc(up_sq, 1)
                                dve.wait_ge(up_hi, i * 8 + u + 1)
                                dve.wait_ge(up_sq, i * 8 + u + 1)
                                V2.tensor_tensor(Ulo[:, f, :], usq[:, f % 2, :], Uhi[:, f, :].bitcast(fp32),
                                                 ALU.subtract).then_inc(up_lo, 1)
                        else:
                            nh = c - 2
                            for t in range(TT):
                                bank = PB[(4 if (nh == 0) == (e == 0) else 0) + t]
                                dve.wait_ge(dn_mm, i * 16 + 8 * e + 4 * nh + t + 1)
                                yv = Y[:, t, nh * 512:(nh + 1) * 512]
                                dve.wait_ge(dn_ev, i * 16 + 8 * e + 1)
                                V2.tensor_tensor(yv, yv, bank[:, :], ALU.add).then_inc(dn_ev, 1)
                        g = G_MLP + 2 + 4 * e + c
                        lo(g, i * 8 + g + 1)
                dve.wait_ge(up_lo, i * 8 + 8)
            post_norm(1)
            for g in range(G_GATE + 2, N_PANELS):
                lo(g)
            for n in range(8):
                t, nh = n % TT, n // TT
                dve.wait_ge(gt_sig, n + 1)
                link(V2.tensor_tensor(Gsig[:, n % 4, :], Gsig[:, n % 4, :], PR[:, t, nh * 512:(nh + 1) * 512], ALU.mult))
                hv = H[:, t, nh * 512:(nh + 1) * 512]
                V2.tensor_tensor(hv, hv, Gsig[:, n % 4, :], ALU.add).then_inc(o_done, 1)

        @block.tensor
        def _(pe):
            mm = nc.tensor.matmul

            def three(out_ap, w, x, start, stop):
                mm(out_ap, w[0], x[0], start=start, stop=False)
                mm(out_ap, w[0], x[1], start=False, stop=False)
                return mm(out_ap, w[1], x[0], start=False, stop=stop)

            def W(g, a, b):
                return Whi[:, g % 2, a:b], Wlo[:, g % 2, a:b]

            def X(k, sl):
                return Xhi[:, k, sl], Xlo[:, k, sl]

            for step in steps:
                if step[0] == "norm0":
                    pe.wait_ge(ones_set, 1)
                    pe.wait_ge(acc_done, KT)
                    mm(PB[0][:, :], ones, acc0, start=True, stop=True).then_inc(ss_done, 1)
                elif step[0] == "gemm":
                    g = step[1]
                    pe.wait_ge(lo_done, g + 1)
                    mine = panel_jobs[g]
                    second = g - 1 in PAIRS
                    if g in PAIRS or second:
                        mine = panel_jobs[g if second else g + 1]
                    if g == 11:
                        mine = panel_jobs[11] + mine
                    if g == 0:
                        pe.wait_ge(ms_done, 1)
                        for k in range(KT):
                            pe.wait_ge(hn_lo, k + 1)
                            for n in mine:
                                c = jobs[n][2]
                                last = three(PB[n][:, :], W(g, k * 256 + c, k * 256 + c + P), X(k, slice(0, SEQ)),
                                             k == 0, k == KT - 1)
                                if k == KT - 1:
                                    last.then_inc(job_done, 1)
                        continue
                    for n in mine:
                        _, kind, c, w, t, dst, _ = jobs[n]
                        bank = PB[n % 4]
                        if n >= 4 and not second:
                            pe.wait_ge(job_evac, n - 3)
                        if kind == "T":
                            for k in range(KT):
                                last = three(bank[:, :], W(g, k * 256 + c, k * 256 + c + P), X(k, slice(0, SEQ)),
                                             k == 0, k == KT - 1)
                        elif kind == "B":
                            for k in range(4):
                                last = three(bank[:, 0:w], X(4 * second + k, slice(t * P, (t + 1) * P)),
                                             W(g, k * 512, k * 512 + w), not second and k == 0, second and k == 3)
                        elif kind == "H":
                            b = w
                            pe.wait_ge(ct_lo, 1)
                            uh = Uhi[:, :, :].rearrange("p a t -> p (a t)")
                            ul = Ulo[:, :, :].rearrange("p a t -> p (a t)")
                            for m in range(8):
                                o = b * 992 + (8 * second + m) * 62
                                last = three(bank[:, 0:62], W(g, m * 256 + c, m * 256 + c + P),
                                             (uh[:, o:o + 62], ul[:, o:o + 62]),
                                             not second and m == 0, second and m == 7)
                        else:
                            pe.wait_ge(job_evac, jobs_by[10])
                            pe.wait_ge(const_in, 32)
                            flat = dst.rearrange("p j e -> p (j e)")
                            for r in range(DIL):
                                last = nc.tensor.transpose(bank[:, r * P:(r + 1) * P], flat[:, r:SEQ:DIL], ident)
                        if kind in "TX" or second:
                            last.then_inc(job_done, 1)
                        elif n == mine[-1]:
                            last.then_inc(half_done, 1)
                elif step[0] == "level_mm":
                    lev = step[1]
                    if lev == 0:
                        pe.wait_ge(hg_k, 1)
                        Qs, Ks = HQ, HF
                    else:
                        pe.wait_ge(qk_done, lev)
                        Qs = tC.rearrange("p (j t) -> p j t", j=2)
                        Ks = tD.rearrange("p (j t) -> p j t", j=2)
                    for h in range(HGH):
                        j, r = h // 2, slice((h % 2) * HD, (h % 2 + 1) * HD)
                        bank = PB[HGB[h]]
                        if lev:
                            pe.wait_ge(hg_ev, 4 * (lev - 1) + h + 1)
                        if lev <= 7:
                            for i in range(TT):
                                last = mm(bank[:, i * P:(i + 1) * P], Ks[r, j, i * P:(i + 1) * P], Qs[r, j, i * P:(i + 1) * P],
                                          start=True, stop=True)
                        elif lev == 8:
                            for b, s in enumerate((0, 2)):
                                last = mm(bank[:, b * P:(b + 1) * P], Ks[r, j, s * P:(s + 1) * P],
                                          Qs[r, j, (s + 1) * P:(s + 2) * P], start=True, stop=True)
                        else:
                            for s in range(2):
                                last = mm(bank[:, s * 256:(s + 1) * 256], Ks[r, j, s * P:(s + 1) * P], Qs[r, j, 256:512],
                                          start=True, stop=True)
                        last.then_inc(hg_mm, 1)
                elif step[0] == "cmp_mlp":
                    pe.wait_ge(ch_done, 1)
                    pe.wait_ge(small_in, 64)
                    pe.wait_ge(hgo_ev, 2)
                    for k in range(NKV):
                        for j in range(2):
                            mm(PB[6][k * HD:(k + 1) * HD, 0:NC], w2s[:, 0, j, :], CH[:, 0, j, k * NC:(k + 1) * NC],
                               start=(j == 0), stop=(j == 1))
                    for g in range(NG):
                        for k in range(NKV):
                            for j in range(2):
                                last = mm(PB[7][32 * g:32 * g + NC, k * HD:(k + 1) * HD], CH[:, 1, j, k * NC:(k + 1) * NC],
                                          w2s[:, 1, j, :], start=(j == 0), stop=(j == 1))
                    last.then_inc(c2_mm, 1)
                elif step[0] == "hg_values":
                    pe.wait_ge(hg_ev, 4 * NLEV)
                    pe.wait_ge(job_evac, jobs_by[4])
                    OFF = {(0, 1): 0, (2, 3): 1, (0, 2): 2, (0, 3): 3, (1, 2): 4, (1, 3): 5}
                    for a in range(2):
                        for i in (2 * a, 2 * a + 1):
                            for h in range(HGH):
                                o = (i % 2) * 256 + h * HD
                                for s in range(i + 1):
                                    lhs = AD[:, h, i, :] if s == i else AO[:, h, OFF[(s, i)], :]
                                    last = mm(PB[HGB[a]][:, o:o + HD], lhs, HI[:, s, h * HD:(h + 1) * HD],
                                              start=(s == 0), stop=(s == i))
                        last.then_inc(hgo_mm, 1)
                elif step[0] == "hg_mix":
                    pe.wait_ge(oh_done, 1)
                    pe.wait_ge(c2_ev, 4)
                    for j in range(2):
                        for i in range(TT):
                            last = nc.tensor.transpose(PB[HGB[2 + j]][:, i * P:(i + 1) * P],
                                                       tD[:, i * 256 + j * P:i * 256 + (j + 1) * P], ident)
                        last.then_inc(mixT_mm, 1)
                elif step[0] == "cmp_scores":
                    pe.wait_ge(job_evac, jobs_by[8])
                    pe.wait_ge(hgo_ev, 2)
                    pe.wait_ge(c2_ev, 4)
                    for k in range(NKV):
                        r = slice(k * HD, (k + 1) * HD)
                        for i in range(TT):
                            for g in range(NG):
                                o = (i * NG + g) * NCP
                                last = mm(PB[4 + k][:, o:o + NCP], T[r, Q0 + g, i * P:(i + 1) * P], kcT[r, :],
                                          start=True, stop=True)
                        last.then_inc(cs_mm, 1)
                elif step[0] == "cmp_turn":
                    pe.wait_ge(cs_p, 1)
                    for k in range(NKV):
                        for i in range(TT):
                            last = nc.tensor.transpose(PB[4 + k][0:96, i * P:(i + 1) * P],
                                                       PC[:, k * 384 + i * 96:k * 384 + (i + 1) * 96], ident)
                        last.then_inc(ct_mm, 1)
                elif step[0] == "nsa":
                    pe.wait_ge(job_evac, len(jobs))
                    pe.wait_ge(ct_ev, 2)
                    pe.wait_ge(mix_lo, 2)

                    def transposes(n):
                        h, b, i = rows[n]
                        pe.wait_ge(p_done, n + 1)
                        if n >= 3:
                            pe.wait_ge(t_ev, n - 2)
                        for j in range(i + 1):
                            last = nc.tensor.transpose(PB[TRB[n % 3]][:, j * P:(j + 1) * P],
                                                       SR[:, n % 3, j * P:(j + 1) * P], ident)
                        last.then_inc(t_mm, 1)

                    def values(h):
                        k, g, half = h // NG, h % NG, h % 2
                        j2 = h // 2
                        pe.wait_ge(t_ev, 8 * h + 8)
                        if half == 0 and j2 >= 2:
                            pe.wait_ge(mix_lo, 2 + j2 - 1)
                        o = PB[OB[j2 % 2]][half * HD:(half + 1) * HD, :]
                        mm(o, vcR[32 * g:32 * g + NCP, k, :], PCT[32 * g:32 * g + NCP, k, :], start=True, stop=False)
                        for b in range(2):
                            for s in range(TT):
                                last = mm(o[:, s * P:SEQ], V[:, (VS, VW)[b], s, k * HD:(k + 1) * HD],
                                          PT[:, h % 2, b, s, s * P:SEQ], start=False, stop=(b == 1 and s == TT - 1))
                        last.then_inc(pv_done, 1)

                    for n in range(len(rows) + 4):
                        if n < len(rows):
                            h, b, i = rows[n]
                            k, g = h // NG, h % NG
                            if n >= 3:
                                pe.wait_ge(s_ev, n - 2)
                            r = slice(k * HD, (k + 1) * HD)
                            mm(PB[ROWB[n % 3]][:, 0:(i + 1) * P], T[r, Q0 + g, i * P:(i + 1) * P],
                               T[r, (KS, KW)[b], 0:(i + 1) * P], start=True, stop=True).then_inc(s_mm, 1)
                        if 2 <= n < len(rows) + 2:
                            transposes(n - 2)
                        if n >= 11 and (n - 11) % 8 == 0:
                            values((n - 11) // 8)
                elif step[0] == "dil":
                    pe.wait_ge(t_ev, len(rows))
                    pe.wait_ge(s_ev, len(rows))
                    pe.wait_ge(mix_lo, 5)

                    def transposes(n):
                        pe.wait_ge(dp_done, n + 1)
                        if n >= 1:
                            pe.wait_ge(dt_ev, 2 * n)
                        for j in range(6):
                            bank = PB[3 + j // 4]
                            last = nc.tensor.transpose(bank[:, (j % 4) * P:(j % 4 + 1) * P],
                                                       DSR[:, n % 3, j * P:(j + 1) * P], ident)
                        last.then_inc(dt_mm, 1)

                    def values(n):
                        r, hh = drows[n]
                        pe.wait_ge(dt_ev, 2 * n + 2)
                        c = slice(hh * HD, (hh + 1) * HD)
                        for s in range(TT):
                            mm(PB[5][c, r * P:(r + 1) * P], V[:, DV0, s, c], DPT[:, n % 2, s, :], start=(s == 0), stop=(s == TT - 1))
                        for g in range(1, 3):
                            last = mm(PB[5 + g][c, r * P:(r + 1) * P], V[:, DV0 + g, r, c], DPT[:, n % 2, 3 + g, :],
                                      start=True, stop=True)
                        last.then_inc(dpv_done, 1)

                    for n in range(len(drows) + 2):
                        if n < len(drows):
                            r, hh = drows[n]
                            if n >= 1:
                                pe.wait_ge(ds_ev, n)
                            p = slice(hh * HD, (hh + 1) * HD)
                            mm(PB[n % 2][:, :], T[p, DQ0, r:SEQ:DIL], T[p, DK0, :], start=True, stop=True)
                            for g in range(1, 3):
                                last = mm(PB[2][:, (n % 2) * 256 + (g - 1) * P:(n % 2) * 256 + g * P],
                                          T[p, DQ0 + g, r:SEQ:DIL], T[p, DK0 + g, r:SEQ:DIL], start=True, stop=True)
                            last.then_inc(ds_mm, 1)
                        if 1 <= n < len(drows) + 1:
                            transposes(n - 1)
                        if n >= 2:
                            values(n - 2)

            pe.wait_ge(mix_lo, KT)
            for c in range(4):
                g = G_OUT + c
                nh, kh = c // 2, c % 2
                pe.wait_ge(lo_done, g + 1)
                for t in range(TT):
                    for k in range(4):
                        last = three(PB[4 * nh + t][:, :], X(4 * kh + k, slice(t * P, (t + 1) * P)), W(g, k * 512, (k + 1) * 512),
                                     kh == 0 and k == 0, kh == 1 and k == 3)
                    if kh == 1:
                        last.then_inc(y_mm, 1)
                if kh == 0:
                    last.then_inc(half_done, 1)

            def norm_transposes(a):
                for t in range(TT):
                    k = a * TT + t
                    pe.wait_ge(n_xs, k + 1)
                    for b in range(2):
                        if k >= 2:
                            pe.wait_ge(n_lo, 2 * (k - 2) + b + 1)
                        for kk in range(4):
                            c = (4 * b + kk) * P
                            last = nc.tensor.transpose(PB[2 * (k % 2) + b][:, kk * P:(kk + 1) * P], tm[:, k % 2, c:c + P], ident)
                        last.then_inc(n_tr, 1)

            pe.wait_ge(y_ev, 4)
            norm_transposes(0)
            g = G_PLE
            pe.wait_ge(lo_done, g + 1)
            pe.wait_ge(pt_lo, 1)
            for n in range(8):
                t, nh = n % TT, n // TT
                pe.wait_ge(y_ev, 8 + (n - 3 if n >= 4 else 0))
                for k in range(2):
                    last = three(PB[4 + n % 4][:, :], (Uhi[:, k, t * P:(t + 1) * P], Ulo[:, k, t * P:(t + 1) * P]),
                                 W(g, k * 1024 + nh * 512, k * 1024 + (nh + 1) * 512), k == 0, k == 1)
                last.then_inc(y_mm, 1)
            pe.wait_ge(n_lo, 8)
            pe.wait_ge(y_ev, 16)
            with pe.Fori(0, EIGHTHS // 2) as i:
                for e in range(2):
                    up0 = 0 if e == 0 else 4
                    for c in range(2):
                        g = G_MLP + 4 * e + c
                        pe.wait_ge(lo_done, i * 8 + g + 1)
                        for f in range(2 * c, 2 * c + 2):
                            if e == 1:
                                pe.wait_ge(dn_ev, i * 16 + 5)
                            for k in range(KT):
                                o = k * 256 + (f % 2) * P
                                last = three(PB[up0 + f][:, :], W(g, o, o + P), X(k, slice(0, SEQ)), k == 0, k == KT - 1)
                            last.then_inc(up_mm, 1)
                    for nh in range(2):
                        g = G_MLP + 4 * e + 2 + nh
                        b0 = 4 if (nh == 0) == (e == 0) else 0
                        pe.wait_ge(lo_done, i * 8 + g + 1)
                        if nh == 1:
                            pe.wait_ge(up_lo, i * 8 + 4 * e + 4)
                        else:
                            pe.wait_ge(dn_ev, i * 16 + 8 * e + 1)
                        for k in range(4):
                            if nh == 0:
                                pe.wait_ge(up_lo, i * 8 + 4 * e + k + 1)
                            for t in range(TT):
                                last = three(PB[b0 + t][:, :], (Uhi[:, k, t * P:(t + 1) * P], Ulo[:, k, t * P:(t + 1) * P]),
                                             W(g, k * 512, (k + 1) * 512), k == 0, k == 3)
                                if k == 3:
                                    last.then_inc(dn_mm, 1)
                pe.wait_ge(dn_ev, i * 16 + 13)
            norm_transposes(1)
            pe.wait_ge(n_lo, 16)
            for c in range(4):
                g = G_GATE + c
                nh, kh = c // 2, c % 2
                pe.wait_ge(lo_done, g + 1)
                for t in range(TT):
                    for k in range(4):
                        last = three(PB[4 * nh + t][:, :], X(4 * kh + k, slice(t * P, (t + 1) * P)), W(g, k * 512, (k + 1) * 512),
                                     kh == 0 and k == 0, kh == 1 and k == 3)
                    if kh == 1:
                        last.then_inc(gt_mm, 1)
                    elif t == TT - 1:
                        last.then_inc(half_done, 1)


def panels(w_in, w_out, cmp_w1, w_up, w_down, w_gate, w_ple):
    out = np.zeros((N_PANELS, P, PAN), np.float32)

    def cols(g, parts):
        v = out[g].reshape(P, KT, 256)
        o = 0
        for c, n in parts:
            v[:, :, o:o + n] = w_in[:, c:c + n].reshape(KT, P, n).transpose(1, 0, 2)
            o += n

    def block(g, w):
        out[g] = w.reshape(4, P, 512).transpose(1, 0, 2).reshape(P, PAN)

    cols(0, [(C_HF, 256)])
    cols(1, [(C_HQ, 256)])
    cols(2, [(C_KC, 256)])
    def pair(g, parts):
        o = 0
        for c, n in parts:
            for m in range(2):
                out[g + m].reshape(P, 4, 512)[:, :, o:o + n] = \
                    w_in[m * 512:(m + 1) * 512, c:c + n].reshape(4, P, n).transpose(1, 0, 2)
            o += n

    pair(3, [(C_HI, 256), (C_VS, 128), (C_VW, 128)])
    pair(5, [(C_HG, 256), (C_DV, 128), (C_GT, 18)])
    q = [(C_NQ + h * HD, HD) for h in (0, 3, 1, 4, 2, 5)]
    cols(7, q[:4])
    cols(8, q[4:] + [(C_KS, 128)])
    cols(9, [(C_KW, 128), (C_DV + 128, 128)])
    cols(10, [(C_DV + 256, 128)])
    for b in range(2):
        for m in range(2):
            out[11 + 2 * b + m] = cmp_w1[b, m * 1024:(m + 1) * 1024].reshape(8, P, 256).transpose(1, 0, 2).reshape(P, PAN)
    cols(15, [(C_DQ, 256)])
    cols(16, [(C_DQ + 256, 256)])
    cols(17, [(C_DK + 128, 256)])
    for c in range(4):
        nh, kh = c // 2, c % 2
        block(G_OUT + c, w_out[kh * 512:(kh + 1) * 512, nh * 512:(nh + 1) * 512])
        block(G_GATE + c, w_gate[kh * 512:(kh + 1) * 512, nh * 512:(nh + 1) * 512])
    out[G_PLE] = w_ple.reshape(2, P, DM).transpose(1, 0, 2).reshape(P, PAN)
    for e in range(EIGHTHS):
        for c in range(2):
            f = e * 512 + c * 256
            out[G_MLP + 4 * e + c] = w_up[:, f:f + 256].reshape(KT, P, 256).transpose(1, 0, 2).reshape(P, PAN)
            block(G_MLP + 4 * e + 2 + c, w_down[e * 512:(e + 1) * 512, c * 512:(c + 1) * 512])
    return out


def kernel(**inputs):
    import numpy as _np
    import concourse.bacc as _bacc
    from concourse import mybir as _mybir
    from concourse.bass_utils import run_bass_kernel_spmd as _run

    a = {k: _np.asarray(v) for k, v in inputs.items()}
    x = a["x"][0]
    tiles = lambda v: v.reshape(-1, P).T
    arrays = {
        "xT": x.T.reshape(KT, P, SEQ).transpose(1, 0, 2),
        "xn": x,
        "wst": panels(a["w_in"][0], a["w_out"][0], a["cmp_w1"][0], a["w_up"][0], a["w_down"][0],
                      a["w_ple_gate"][0], a["w_ple_proj"][0]),
        "pT": a["p"][0, 0].T.reshape(2, P, SEQ).transpose(1, 0, 2).reshape(P, 1024),
        "gpre": tiles(a["g_pre_mix"][0]),
        "gvec": _np.stack([tiles(a["g_pre_mlp"][0]), tiles(a["g_ple"][0])], 1),
        "gpost": _np.stack([a["g_post_mix"][0], a["g_post_mlp"][0]]),
        "pos": a["cmp_pos"][0].reshape(2, 16, P).transpose(2, 0, 1),
        "w2": a["cmp_w2"][0].reshape(2, 2, P, HD).transpose(2, 0, 1, 3),
        "ctab": constant_table(),
        "lmask": level_masks(),
        "eye": _np.eye(P, dtype=_np.float32),
    }
    nc = _bacc.Bacc("TRN2", target_bir_lowering=False, num_devices=1)
    args = []
    for name in arrays:
        arrays[name] = _np.ascontiguousarray(arrays[name])
        args.append(nc.dram_tensor(name, arrays[name].shape, _mybir.dt.from_np(arrays[name].dtype),
                                   kind="ExternalInput").ap())
    args.append(nc.dram_tensor("out", (SEQ, DM), _mybir.dt.float32, kind="ExternalOutput").ap())
    build(nc, *args)
    r = _run(nc, [arrays], core_ids=[0])
    return r.results[0]["out"].reshape(1, SEQ, DM)
```

```python
import concourse.bass as bass
from concourse import mybir
from contextlib import ExitStack
import numpy as np

P = 128
SEQ, DM, DFF, PLE = 512, 1024, 4096, 256
TT = SEQ // P
KT = DM // P
HD = 64
NH, NKV, NG = 6, 2, 3
CB, CS, NC, NCP = 32, 16, 31, 32
DIL = 4
HGH = 4
MIX_ORDER = (0, 1, 2, 6, 7, 3, 4, 5)
PAN = 2048
EPS = 1e-6
NEG = -1e30
X_SPLIT = -40.0
LOG_TINY = float(np.log(1e-30))

N_IN = 18
G_PT = N_IN
G_PLE = G_PT + 1
G_OUT = G_PLE + 1
G_MLP = G_OUT + 4
EIGHTHS = 8
G_GATE = G_MLP + 4 * EIGHTHS
N_PANELS = G_GATE + 4

C_NQ, C_KC, C_KS, C_VS, C_KW, C_VW, C_GT = 0, 384, 640, 768, 896, 1024, 1152
C_DQ, C_DK, C_DV, C_HQ, C_HF, C_HI, C_HG = 1170, 1554, 1938, 2322, 2578, 2834, 3090

D0W = SEQ + 4
TB_D0 = 0
TB_D12 = TB_D0 + 2 * D0W
TB_NSA = TB_D12 + 2 * 256
TB_CMP = TB_NSA + NH * SEQ
TB_RST = TB_CMP + NKV * TT * NG * NCP
TB_W = TB_RST + SEQ

LEVELS = (2, 4, 8, 16, 32, 64, 128)
HGC = 64


def slopes():
    n = 12
    s = (2.0 ** (-8.0 * np.arange(1, n + 1) / n)).reshape(-1, 4)
    return s[:, 2:].reshape(-1).astype(np.float32), s[:, :2].reshape(-1).astype(np.float32)


def constant_table():
    nsa, dil = slopes()
    t = np.zeros((P, TB_W), np.float32)
    p = np.arange(P)[:, None]
    rel = p + 384 - np.arange(SEQ)[None, :]
    for h in range(NH):
        t[:, TB_NSA + h * SEQ:TB_NSA + (h + 1) * SEQ] = np.where(rel >= 0, nsa[h] * rel.astype(np.float32), -NEG)
    for hh in range(2):
        rel = DIL * p + 3 - np.arange(D0W)[None, :]
        t[:, TB_D0 + hh * D0W:TB_D0 + (hh + 1) * D0W] = np.where(
            (rel >= 0) & (rel <= 128), dil[hh] * rel.astype(np.float32), -NEG)
        rel = DIL * (p - np.arange(P)[None, :])
        o = TB_D12 + hh * 256
        t[:, o:o + P] = np.where(rel >= 0, dil[2 + hh] * rel.astype(np.float32), -NEG)
        t[:, o + P:o + 256] = np.where((rel >= 0) & (rel % 16 == 0), dil[4 + hh] * rel.astype(np.float32), -NEG)
    for k in range(NKV):
        for i in range(TT):
            for g in range(NG):
                o = TB_CMP + ((k * TT + i) * NG + g) * NCP
                n = np.arange(NCP)[None, :]
                tok = i * P + p
                d = np.abs(tok - (n * CS + 0.5 * (CB - 1))).astype(np.float32)
                ok = (n * CS + CB - 1 <= tok) & (n < NC)
                t[:, o:o + NCP] = np.where(ok, nsa[k * NG + g] * d, -NEG)
    t[:, TB_RST:TB_RST + SEQ] = (np.arange(SEQ) % HGC != 0)
    return t


def level_masks():
    s, q = np.arange(P)[:, None], np.arange(P)[None, :]
    m = [(s // L == q // L) & (q // (L // 2) == s // (L // 2) + 1) for L in LEVELS]
    return np.stack(m, 1).astype(np.int32)


def build(nc, xT, xn, wst, gpre, gvec, gpost, pos, w2, ctab, lmask, eye, out):
    fp32, f32r, i32 = mybir.dt.float32, mybir.dt.float32r, mybir.dt.int32
    ALU, ACT, AX = mybir.AluOpType, mybir.ActivationFunctionType, mybir.AxisListType
    ctx = ExitStack()
    with ctx:
        def sb(name, shape, dt):
            return ctx.enter_context(nc.sbuf_tensor(name, shape, dt))

        def sem(name):
            return ctx.enter_context(nc.semaphore(name))

        raw = sb("raw", [P, 2, PAN], fp32)
        Whi = sb("Whi", [P, 2, PAN], f32r)
        Wlo = sb("Wlo", [P, 2, PAN], f32r)
        Xhi = sb("Xhi", [P, KT, SEQ], f32r)
        Xlo = sb("Xlo", [P, KT, SEQ], f32r)
        Uhi = sb("Uhi", [P, 4, SEQ], f32r)
        Ulo = sb("Ulo", [P, 4, SEQ], f32r)
        AW = 26500
        arena = sb("arena", [P, AW], fp32)
        PB = [ctx.enter_context(nc.psum_tensor(f"bank{i}", [P, 512], fp32)) for i in range(8)]

        at = [0]

        def take(n):
            a = at[0]
            at[0] += n
            assert at[0] <= AW, at[0]
            return a

        def view(a, n):
            return arena[:, a:a + n]

        tab = view(take(TB_W), TB_W)
        aT = take(11 * SEQ)
        T = view(aT, 11 * SEQ).rearrange("p (j t) -> p j t", t=SEQ)
        Q0, KS, KW, DQ0, DK0 = 0, 3, 4, 5, 8
        V = view(take(5 * SEQ), 5 * SEQ).rearrange("p (v j e) -> p v j e", v=5, e=P)
        VS, VW, DV0 = 0, 1, 2
        HG = view(take(1024), 1024).rearrange("p (i c) -> p i c", i=TT)
        gates = view(take(72), 72)
        small = view(take(320), 320)
        kcT = view(take(NCP), NCP)
        vcR = view(take(128), 128).rearrange("p (k e) -> p k e", k=NKV)
        w2s = view(take(256), 256).rearrange("p (b j e) -> p b j e", b=2, j=2)
        aX = take(9728)
        HQ = view(aX, 1024).rearrange("p (j t) -> p j t", j=2)
        HF = view(aX + 1024, 1024).rearrange("p (j t) -> p j t", j=2)
        HI = view(aX + 2048, 1024).rearrange("p (i c) -> p i c", i=TT)
        tA, tB, tC, tD = (view(aX + 3072 + 1024 * n, 1024) for n in range(4))
        AD = view(aX + 7168, 2048).rearrange("p (h i t) -> p h i t", h=HGH, i=TT)
        AO = view(aT + DQ0 * SEQ, 3072).rearrange("p (h b t) -> p h b t", h=HGH, t=P)
        PT = view(aX, 8192).rearrange("p (a b j t) -> p a b j t", a=2, b=2, j=TT)
        SR = view(aX + 8192, 3 * SEQ).rearrange("p (a n) -> p a n", a=3)
        PC = view(aX, 768)
        PCT = HG.rearrange("p i c -> p (i c)").rearrange("p (k t) -> p k t", k=NKV)
        DPT = view(aX, 2 * 768).rearrange("p (a b t) -> p a b t", a=2, t=P)
        DSR = view(aX + 1536, 3 * 768).rearrange("p (a n) -> p a n", a=3)
        XT = view(aX, 4096).rearrange("p (k t) -> p k t", k=KT)
        sqs = view(aX + 4096, 1024).rearrange("p (a t) -> p a t", a=2)
        acc0 = view(aX + 5120, 512)
        rb = view(aX + 5632, 512)
        hn_t = view(aX + 6144, 1024).rearrange("p (a t) -> p a t", a=2)
        ones = view(aX + 7168, P)
        aC = aT + DQ0 * SEQ
        KCV = view(aC, 1024).rearrange("p (b t) -> p b t", b=2)
        KD = view(aC + 1024, 1024).rearrange("p (b a u) -> p b a u", b=2, a=2)
        CT = view(aC, 1984).rearrange("p (b m k n) -> p b m k n", b=2, m=16, k=NKV)
        CA = view(aC + 2048, 1024).rearrange("p (b k u) -> p b k u", b=2, k=NKV)
        CEXP = view(aC, 512)
        CHa = take(2 * 2 * 62)
        CHN = view(take(512), 512).rearrange("p (b j) -> p b j", b=2)
        CH = view(CHa, 248).rearrange("p (b j n) -> p b j n", b=2, j=2)
        PR = view(TB_NSA, 4096).rearrange("p (i n) -> p i n", i=TT)
        assert TB_NSA + 4096 <= TB_W
        at[0] = TB_W
        H = view(take(4096), 4096).rearrange("p (i n) -> p i n", i=TT)
        Y = view(take(4096), 4096).rearrange("p (i n) -> p i n", i=TT)
        GB = view(take(2048), 2048).rearrange("p (a n) -> p a n", a=2)
        diag = view(take(512), 512).rearrange("p (t n) -> p t n", t=TT)
        squares = view(take(2048), 2048).rearrange("p (a n) -> p a n", a=4)
        relu = view(take(1024), 1024).rearrange("p (a n) -> p a n", a=2)
        usq = view(take(1024), 1024).rearrange("p (a n) -> p a n", a=2)
        Gsig = view(take(2048), 2048).rearrange("p (a n) -> p a n", a=4)

        masks = sb("masks", [P, len(LEVELS), P], i32)
        ident_s = sb("ident_s", [P, P], fp32)
        gpre_s = sb("gpre_s", [P, KT], fp32)
        gvec_s = sb("gvec_s", [P, 2, KT], fp32)
        pos_s = sb("pos_s", [P, 2, 16], fp32)
        st = sb("st", [P, 64], fp32)

        ident = ident_s[:, :]
        ss_a, bias_a, rs_y, rs_h, ss_h = (st[:, o:o + 8] for o in (0, 8, 16, 24, 48))
        eps, warm = st[:, 56:57], st[:, 57:58]
        ntab = tab[:, TB_NSA:TB_NSA + NH * SEQ].rearrange("p (h n) -> p h n", h=NH)
        d0tab = tab[:, TB_D0:TB_D0 + 2 * D0W].rearrange("p (h n) -> p h n", h=2)
        d12tab = tab[:, TB_D12:TB_D12 + 512].rearrange("p (h n) -> p h n", h=2)
        ctb = tab[:, TB_CMP:TB_CMP + 768].rearrange("p (k n) -> p k n", k=NKV)
        rst = tab[:, TB_RST:TB_RST + SEQ]

        mneg = small[:, 0:64]
        den = small[:, 64:128]
        rden = small[:, 128:192]
        cst = small[:, 192:216]
        csum = small[:, 216:240]
        hgs = small[:, 240:256]
        blk = small[:, 256:288]
        boff = small[:, 288:304]

        raw_in = [sem("raw_in0"), sem("raw_in1")]
        x_in = [sem(f"x_in{k}") for k in range(4)]
        const_in = sem("const_in")
        tab_in = sem("tab_in")
        small_in = sem("small_in")
        cmp_in = sem("cmp_in")
        res_in = sem("res_in")
        out_sent = sem("out_sent")
        hi_done = sem("hi_done")
        lo_done = sem("lo_done")
        half_done = sem("half_done")
        act_seq = sem("act_seq")
        dve_seq = sem("dve_seq")
        ones_set = sem("ones_set")
        sq_done = sem("sq_done")
        acc_done = sem("acc_done")
        ss_done = sem("ss_done")
        ms_done = sem("ms_done")
        sqrt_done = sem("sqrt_done")
        hn_f = sem("hn_f")
        hn_hi = sem("hn_hi")
        hn_lo = sem("hn_lo")
        job_done = sem("job_done")
        job_evac = sem("job_evac")
        kd_done = sem("kd_done")
        ct_done = sem("ct_done")
        ct_hi = sem("ct_hi")
        ct_lo = sem("ct_lo")
        hx = sem("hx")
        hy = sem("hy")
        hg_k = sem("hg_k")
        arg_done = sem("arg_done")
        dec_done = sem("dec_done")
        qk_done = sem("qk_done")
        hg_mm = sem("hg_mm")
        hg_ev = sem("hg_ev")
        hgo_mm = sem("hgo_mm")
        hgo_ev = sem("hgo_ev")
        oh_done = sem("oh_done")
        mixT_mm = sem("mixT_mm")
        mix_hi = sem("mix_hi")
        mix_lo = sem("mix_lo")
        ce = sem("ce")
        ch_done = sem("ch_done")
        chT_mm = sem("chT_mm")
        chT_ev = sem("chT_ev")
        c2_mm = sem("c2_mm")
        c2_ev = sem("c2_ev")
        cs_mm = sem("cs_mm")
        cs_ev = sem("cs_ev")
        cs_exp = sem("cs_exp")
        cs_p = sem("cs_p")
        ct_mm = sem("ct_mm")
        ct_ev = sem("ct_ev")
        s_mm = sem("s_mm")
        s_ev = sem("s_ev")
        p_exp = sem("p_exp")
        p_done = sem("p_done")
        t_mm = sem("t_mm")
        t_ev = sem("t_ev")
        pv_done = sem("pv_done")
        ds_mm = sem("ds_mm")
        ds_ev = sem("ds_ev")
        dp_exp = sem("dp_exp")
        dp_done = sem("dp_done")
        dt_mm = sem("dt_mm")
        dt_ev = sem("dt_ev")
        dpv_done = sem("dpv_done")
        y_mm = sem("y_mm")
        y_ev = sem("y_ev")
        eps_set = sem("eps_set")
        y_sq = sem("y_sq")
        y_first = sem("y_first")
        y_gain = sem("y_gain")
        y_rms = sem("y_rms")
        h_done = sem("h_done")
        h_sq = sem("h_sq")
        h_rms = sem("h_rms")
        h_rs = sem("h_rs")
        diag_done = sem("diag_done")
        h_turned = sem("h_turned")
        x_hi = sem("x_hi")
        x_lo = sem("x_lo")
        up_mm = sem("up_mm")
        up_relu = sem("up_relu")
        up_sq = sem("up_sq")
        up_hi = sem("up_hi")
        up_lo = sem("up_lo")
        dn_mm = sem("dn_mm")
        dn_ev = sem("dn_ev")
        z_done = sem("z_done")
        gt_mm = sem("gt_mm")
        gt_sig = sem("gt_sig")
        o_done = sem("o_done")

        jobs = []

        def t_job(g, c, dst, scale=1.0):
            jobs.append((g, "T", c, P, None, dst, scale))

        def b_job(g, w, t, parts):
            jobs.append((g, "B", 0, w, t, parts, 1.0))

        for j in range(2):
            t_job(0, j * P, HF[:, j, :])
        for j in range(2):
            t_job(1, j * P, HQ[:, j, :])
        for b in range(2):
            t_job(2, b * P, KCV[:, b, :])
        for t in range(TT):
            b_job(4, 512, t, [(0, 256, HI[:, t, :]), (256, 256, V[:, VS:VW + 1, t, :])])
        for b in range(2):
            jobs.append((6 + 2 * b, "H", 0, b, None, CHN[0:2 * NC, b, :], 1.0))
        for t in range(TT):
            b_job(10, 402, t, [(0, 256, HG[:, t, :]), (256, P, V[:, DV0, t, :]), (384, 18, gates[:, 18 * t:18 * t + 18])])
        for j in range(2):
            t_job(11, j * P, T[:, Q0 + j, :], -HD ** -0.5)
        t_job(12, 0, T[:, Q0 + 2, :], -HD ** -0.5)
        t_job(12, P, T[:, KS, :])
        t_job(13, 0, T[:, KW, :])
        dv = [V[:, DV0 + g].rearrange("p j e -> p (j e)") for g in (1, 2)]
        t_job(13, P, dv[0])
        t_job(14, 0, dv[1])
        for g in range(2):
            jobs.append((15, "X", 0, P, g, V[:, DV0 + 1 + g], 1.0))
        for j in range(2):
            t_job(15, j * P, T[:, DQ0 + j, :], -HD ** -0.5)
        t_job(16, 0, T[:, DQ0 + 2, :], -HD ** -0.5)
        t_job(16, P, T[:, DK0, :])
        for j in range(2):
            t_job(17, j * P, T[:, DK0 + 1 + j, :])
        panel_jobs = {g: [n for n, j in enumerate(jobs) if j[0] == g] for g in range(N_IN)}
        jobs_by = [sum(1 for j in jobs if j[0] <= g) for g in range(N_IN)]

        LEVEL_AT = {0: 4, 1: 6, 2: 8, 3: 9, 4: 10, 5: 11, 6: 12, 7: 13, 8: 14, 9: 15}
        steps = [("norm0",), ("split", 0), ("scale0",), ("split", 1)]
        for g in range(N_IN):
            steps.append(("gemm", g))
            here = [lev for lev in LEVEL_AT if LEVEL_AT[lev] == g]
            if here:
                steps.append(("level_mm", here[0]))
            if g == 9:
                steps.append(("cmp_silu",))
            if g == 10:
                steps.append(("cmp_mlp",))
            if g == 15:
                steps.append(("hg_values",))
            if g == 16:
                steps.append(("cmp_scores",))
            steps.append(("split", g + 2))
            if g == 1:
                steps.append(("decay",))
            if g == 2:
                steps.append(("cmp_kd",))
            if g == 3:
                steps.append(("cmp_im2col",))
            if here and here[0] < 9:
                steps.append(("level", here[0] + 1))
        steps += [("hg_mix",), ("cmp_turn",), ("nsa",), ("dil",)]
        PAIRS = (3, 5, 7, 9)

        def last_use(g):
            if g in PAIRS:
                return half_done, PAIRS.index(g) + 1
            if g < N_IN:
                return job_done, jobs_by[g]
            if g < G_OUT:
                return y_mm, 8
            if g < G_MLP:
                c = g - G_OUT
                return (half_done, 5 + c // 2) if c % 2 == 0 else (y_mm, 8 + 2 * c + 2)
            if g < G_GATE:
                q = g - G_MLP
                e, c = q // 4, q % 4
                return (up_mm, 4 * e + 2 * c + 2) if c < 2 else (dn_mm, 8 * e + 4 * (c - 2) + 4)
            c = g - G_GATE
            return (half_done, 7 + c // 2) if c % 2 == 0 else (gt_mm, 2 * c + 2)

        NLEV = 10

        HGB = (4, 5, 6, 7)
        rows = [(h, b, i) for h in range(NH) for b in range(2) for i in range(TT)]
        ROWB, TRB, OB = (0, 1, 2), (3, 4, 5), (6, 7)
        drows = [(r, hh) for r in range(DIL) for hh in range(2)]

        block = ctx.enter_context(nc.Block())

        @block.sync
        def _(sp):
            def load_panel(g):
                if g >= 2:
                    sp.wait_ge(lo_done, g - 1)
                sp.dma_start(raw[:, g % 2, :], wst[g]).then_inc(raw_in[g % 2], 16)

            for k in range(4):
                sp.dma_start(XT[:, 2 * k:2 * k + 2, :], xT[:, 2 * k:2 * k + 2, :]).then_inc(x_in[k], 16)
            load_panel(0)
            load_panel(1)
            sp.dma_start(masks[:, :, :], lmask).then_inc(const_in, 16)
            sp.dma_start(ident, eye).then_inc(const_in, 16)
            for g in range(2, G_OUT + 2):
                load_panel(g)
                if g == 4:
                    sp.wait_ge(kd_done, 1)
                    for b in range(2):
                        for par in range(2):
                            for k in range(NKV):
                                sp.dma_start(CA[par * HD:(par + 1) * HD, b, k, :],
                                             KD[k * HD:(k + 1) * HD, b, par, :]).then_inc(cmp_in, 16)
            sp.wait_ge(dpv_done, len(drows))
            sp.wait_ge(mix_lo, KT)
            sp.dma_start(H, xn.rearrange("(i p) n -> p i n", p=P)).then_inc(res_in, 16)
            for a in range(2):
                sp.dma_start(GB[:, a, :], gpost[a:a + 1, :].partition_broadcast(P)).then_inc(res_in, 16)
            for g in range(G_OUT + 2, G_MLP + 2):
                load_panel(g)
            with sp.Fori(0, EIGHTHS // 2) as i:
                for c in range(8):
                    sp.wait_ge(lo_done, G_MLP + 2 + c - 1 + i * 8)
                    sp.dma_start(raw[:, (G_MLP + c) % 2, :],
                                 wst[bass.ds(G_MLP + 2 + c + i * 8, 1), :, :].rearrange("o p n -> (o p) n")
                                 ).then_inc(raw_in[(G_MLP + c) % 2], 16)
            for g in range(G_GATE + 2, N_PANELS):
                load_panel(g)
            for n in range(8):
                sp.wait_ge(o_done, n + 1)
                t, nh = n % TT, n // TT
                sp.dma_start(out[t * P:(t + 1) * P, nh * 512:(nh + 1) * 512],
                             H[:, t, nh * 512:(nh + 1) * 512]).then_inc(out_sent, 16)
            sp.wait_ge(out_sent, 128)

        @block.gpsimd
        def _(pool):
            pool.dma_start(gpre_s[:, :], gpre).then_inc(small_in, 16)
            pool.dma_start(gvec_s[:, :, :], gvec).then_inc(small_in, 16)
            pool.dma_start(pos_s[:, :, :], pos).then_inc(small_in, 16)
            pool.dma_start(w2s, w2).then_inc(small_in, 16)
            pool.dma_start(tab, ctab).then_inc(tab_in, 16)
            nc.gpsimd.memset(ones, 1.0).then_inc(ones_set, 1)
            nc.gpsimd.memset(eps, EPS).then_inc(eps_set, 1)
            for u in (Uhi, Ulo):
                nc.gpsimd.memset(u[:, 3, 448:512].bitcast(fp32), 0.0).then_inc(z_done, 1)
            nc.gpsimd.memset(kcT, 0.0).then_inc(z_done, 1)
            nc.gpsimd.memset(vcR, 0.0).then_inc(z_done, 1)
            pool.wait_ge(h_done, TT)
            nc.gpsimd.memset(Y, 0.0).then_inc(dn_ev, 1)

        @block.scalar
        def _(act):
            seq = [0]

            def link(ins):
                seq[0] += 1
                ins.then_inc(act_seq, 1)
                act.wait_ge(act_seq, seq[0])

            def hi(g, count=None):
                act.wait_ge(raw_in[g % 2], 16 * (g // 2 + 1) if count is None else count)
                if count is None and g >= 2:
                    act.wait_ge(*last_use(g - 2))
                nc.scalar.activation(Whi[:, g % 2, :], raw[:, g % 2, :], ACT.Copy).then_inc(hi_done, 1)

            for step in steps:
                if step[0] == "norm0":
                    for k in range(KT):
                        if k % 2 == 0:
                            act.wait_ge(x_in[k // 2], 16)
                        if k >= 2:
                            act.wait_ge(acc_done, k - 1)
                        nc.scalar.activation(sqs[:, k % 2, :], XT[:, k, :], ACT.Square).then_inc(sq_done, 1)
                elif step[0] == "scale0":
                    act.wait_ge(ms_done, 1)
                    nc.scalar.activation(rb, rb, ACT.Sqrt).then_inc(sqrt_done, 1)
                    for k in range(KT):
                        act.wait_ge(hn_f, k + 1)
                        nc.scalar.activation(Xhi[:, k, :], hn_t[:, k % 2, :], ACT.Copy).then_inc(hn_hi, 1)
                elif step[0] == "split":
                    hi(step[1])
                elif step[0] == "gemm":
                    for n in panel_jobs[step[1]]:
                        _, kind, _, w, tiles, dst, scale = jobs[n]
                        act.wait_ge(job_done, n + 1)
                        if step[1] == 15:
                            act.wait_ge(hgo_mm, 2)
                        src = PB[n % 4][:, :]
                        if kind == "B":
                            for a, (c, cw, part) in enumerate(dst):
                                piece = src[:, c:c + cw]
                                if cw == 256 and c:
                                    piece = piece.rearrange("p (v e) -> p v e", v=2)
                                ins = nc.scalar.activation(part, piece, ACT.Copy)
                            ins.then_inc(job_evac, 1)
                            continue
                        if kind == "H":
                            src = src[0:2 * NC, 0:256]
                        elif kind == "X":
                            src = src.rearrange("p (r e) -> p r e", e=P)
                        nc.scalar.activation(dst, src, ACT.Copy, scale=scale).then_inc(job_evac, 1)
                elif step[0] == "decay":
                    act.wait_ge(hx, 1)
                    nc.scalar.activation(tB, tA, ACT.Exp, scale=-1.0).then_inc(hy, 1)
                    act.wait_ge(hx, 2)
                    link(nc.scalar.activation(tA, tA, ACT.Exp))
                    nc.scalar.activation(tA, tA, ACT.Ln, bias=1.0).then_inc(hy, 1)
                    act.wait_ge(hy, 1)
                    nc.scalar.activation(tD, tB, ACT.Ln, bias=1.0).then_inc(hy, 1)
                elif step[0] == "level":
                    act.wait_ge(arg_done, step[1])
                    nc.scalar.activation(tA, tA, ACT.Exp).then_inc(dec_done, 1)
                elif step[0] == "cmp_im2col":
                    act.wait_ge(ct_done, 1)
                    nc.scalar.activation(Uhi[:, :, :].rearrange("p a t -> p (a t)")[:, 0:1984],
                                         view(aC, 1984), ACT.Copy).then_inc(ct_hi, 1)
                elif step[0] == "cmp_silu":
                    act.wait_ge(job_evac, jobs_by[8])
                    nc.scalar.activation(CEXP[0:2 * NC, :], CHN[0:2 * NC, :, :].rearrange("p b j -> p (b j)"), ACT.Exp,
                                         scale=-1.0).then_inc(ce, 1)
                elif step[0] == "cmp_mlp":
                    act.wait_ge(chT_mm, 1)
                    nc.scalar.activation(view(CHa, 248), PB[7][:, 0:248], ACT.Copy).then_inc(chT_ev, 1)
                elif step[0] == "hg_values":
                    for a in range(2):
                        act.wait_ge(hgo_mm, a + 1)
                        nc.scalar.activation(tA[:, a * 512:(a + 1) * 512], PB[HGB[a]][:, :], ACT.Copy).then_inc(hgo_ev, 1)
                    act.wait_ge(hx, 4)
                    nc.scalar.activation(hgs, hgs, ACT.Sqrt).then_inc(hy, 1)
                    nc.scalar.activation(tC, HG.rearrange("p i c -> p (i c)"), ACT.Exp, scale=-1.0).then_inc(hy, 1)
                elif step[0] == "hg_mix":
                    for j in range(2):
                        act.wait_ge(mixT_mm, j + 1)
                        nc.scalar.activation(Xhi[:, 6 + j, :], PB[HGB[2 + j]][:, :], ACT.Copy).then_inc(mix_hi, 1)
                elif step[0] == "cmp_scores":
                    act.wait_ge(job_evac, jobs_by[10])
                    nc.scalar.activation(gates, gates, ACT.Exp, scale=-1.0).then_inc(ce, 1)
                    act.wait_ge(cs_ev, 1)
                    nc.scalar.activation(PC, PC, ACT.Exp, scale=-1.0).then_inc(cs_exp, 1)
                elif step[0] == "cmp_turn":
                    for k in range(NKV):
                        act.wait_ge(ct_mm, k + 1)
                        nc.scalar.activation(PCT[0:96, k, :], PB[4 + k][0:96, :], ACT.Copy).then_inc(ct_ev, 1)
                elif step[0] == "nsa":
                    def t_copy(n):
                        h, b, i = rows[n]
                        act.wait_ge(t_mm, n + 1)
                        if i == 0 and b == 0 and h >= 2:
                            act.wait_ge(pv_done, h - 1)
                        nc.scalar.activation(PT[:, h % 2, b, 0:i + 1, i * P:(i + 1) * P],
                                             PB[TRB[n % 3]][:, 0:(i + 1) * P].rearrange("p (j t) -> p j t", t=P),
                                             ACT.Copy).then_inc(t_ev, 1)

                    def mix_evac(j):
                        act.wait_ge(pv_done, 2 * j + 2)
                        nc.scalar.activation(Xhi[:, j, :], PB[OB[j % 2]][:, :], ACT.Copy).then_inc(mix_hi, 1)

                    for n in range(len(rows) + 4):
                        if n < len(rows):
                            w = (rows[n][2] + 1) * P
                            act.wait_ge(s_ev, n + 1)
                            nc.scalar.activation(SR[:, n % 3, 0:w], SR[:, n % 3, 0:w], ACT.Exp,
                                                 bias=mneg[:, n:n + 1], scale=-1.0,
                                                 accum_out=den[:, n:n + 1]).then_inc(p_exp, 1)
                        if 2 <= n < len(rows) + 2:
                            t_copy(n - 2)
                        if n >= 19 and (n - 19) % 16 == 0:
                            mix_evac((n - 19) // 16)
                elif step[0] == "dil":
                    def dt_copy(n):
                        if n >= 2:
                            act.wait_ge(dpv_done, n - 1)
                        act.wait_ge(dt_mm, n + 1)
                        nc.scalar.activation(DPT[:, n % 2, 0:4, :], PB[3][:, :].rearrange("p (j t) -> p j t", t=P),
                                             ACT.Copy).then_inc(dt_ev, 1)
                        nc.scalar.activation(DPT[:, n % 2, 4:6, :], PB[4][:, 0:256].rearrange("p (j t) -> p j t", t=P),
                                             ACT.Copy).then_inc(dt_ev, 1)

                    for n in range(len(drows) + 2):
                        if n < len(drows):
                            act.wait_ge(ds_ev, n + 1)
                            nc.scalar.activation(DSR[:, n % 3, :], DSR[:, n % 3, :], ACT.Exp,
                                                 bias=mneg[:, 48 + n:49 + n], scale=-1.0,
                                                 accum_out=den[:, 48 + n:49 + n]).then_inc(dp_exp, 1)
                        if n >= 2:
                            dt_copy(n - 2)
                    act.wait_ge(dpv_done, len(drows))
                    for g in range(3):
                        nc.scalar.activation(Xhi[:, 3 + g, :].rearrange("p (i r) -> p i r", r=DIL),
                                             PB[5 + g][:, :].rearrange("p (r i) -> p i r", r=DIL),
                                             ACT.Copy).then_inc(mix_hi, 1)

            def y_half(a, nh, t):
                if a == 0:
                    act.wait_ge(y_mm, 8 + 4 * nh + t + 1)
                    return PB[4 * nh + t][:, :]
                act.wait_ge(dn_ev, 1 + 8 * (EIGHTHS - 1) + 4 * nh + t + 1)
                return Y[:, t, nh * 512:(nh + 1) * 512]

            def first_halves(a):
                for t in range(TT):
                    src = y_half(a, 0, t)
                    if a:
                        act.wait_ge(y_sq, 4 + t + 1)
                    nc.scalar.activation(squares[:, t % 2, :], src, ACT.Square,
                                         accum_out=ss_a[:, 4 * a + t:4 * a + t + 1]).then_inc(y_sq, 1)
                    act.wait_ge(y_sq, 8 * a + t + 1)

            def post_norm(a):
                for s in range(TT + 1):
                    if s < TT:
                        k = TT * a + s
                        src = y_half(a, 1, s)
                        nc.scalar.activation(squares[:, s % 2, :], src, ACT.Square,
                                             accum_out=rs_y[:, k:k + 1]).then_inc(y_sq, 1)
                        act.wait_ge(y_sq, 8 * a + 4 + s + 1)
                        act.wait_ge(y_first, a + 1)
                        nc.scalar.activation(rs_y[:, k:k + 1], rs_y[:, k:k + 1], ACT.Sqrt, scale=1.0 / DM,
                                             bias=bias_a[:, k:k + 1]).then_inc(y_rms, 1)
                    if s >= 1:
                        k = TT * a + s - 1
                        act.wait_ge(h_done, k + 1)
                        nc.scalar.activation(squares[:, 2:4, :].rearrange("p a n -> p (a n)"), H[:, s - 1, :], ACT.Square,
                                             accum_out=ss_h[:, k:k + 1]).then_inc(h_sq, 1)
                        act.wait_ge(h_sq, k + 1)
                        act.wait_ge(eps_set, 1)
                        nc.scalar.activation(rs_h[:, k:k + 1], ss_h[:, k:k + 1], ACT.Sqrt, scale=1.0 / DM,
                                             bias=eps).then_inc(h_rms, 1)
                for k in range(KT):
                    act.wait_ge(h_turned, KT * a + k + 1)
                    nc.scalar.activation(Xhi[:, k, :], PB[k][:, :], ACT.Copy,
                                         scale=gvec_s[:, a, k:k + 1]).then_inc(x_hi, 1)

            act.wait_ge(const_in, 32)
            nc.scalar.activation(warm, ident[:, 0:1], ACT.Sqrt)
            for g in range(G_OUT, G_OUT + 4):
                hi(g)
            first_halves(0)
            hi(G_MLP)
            post_norm(0)
            hi(G_MLP + 1)

            def mlp_turn(i, last):
                for e in range(2):
                    for c in range(4):
                        if c < 2:
                            for f in range(2 * c, 2 * c + 2):
                                u = 4 * e + f
                                act.wait_ge(up_mm, i * 8 + u + 1)
                                bank = PB[(0 if e == 0 else 4) + f]
                                nc.scalar.activation(relu[:, f % 2, :], bank[:, :], ACT.Relu).then_inc(up_relu, 1)
                                act.wait_ge(up_sq, i * 8 + u + 1)
                                nc.scalar.activation(Uhi[:, f, :], usq[:, f % 2, :], ACT.Copy).then_inc(up_hi, 1)
                        if last and e == 1 and c == 3:
                            continue
                        g = G_MLP + 2 + 4 * e + c
                        if c < 2:
                            act.wait_ge(up_mm, i * 8 + 4 * e + 2 * c + 2)
                        else:
                            act.wait_ge(dn_mm, i * 16 + 8 * e + 4 * (c - 2) + 4)
                        hi(g, i * 64 + 16 * (g // 2 + 1))

            with act.Fori(0, EIGHTHS // 2 - 1) as i:
                mlp_turn(i, False)
            mlp_turn(EIGHTHS // 2 - 1, True)
            first_halves(1)
            post_norm(1)
            for g in range(G_GATE + 1, G_GATE + 2):
                hi(g)
            for g in range(G_GATE + 2, N_PANELS):
                hi(g)
            act.wait_ge(h_rs, 2 * TT)
            for n in range(8):
                act.wait_ge(gt_mm, n + 1)
                if n >= 4:
                    act.wait_ge(o_done, n - 3)
                nc.scalar.activation(Gsig[:, n % 4, :], PB[n][:, :], ACT.Sigmoid,
                                     scale=rs_h[:, TT + n % TT:TT + n % TT + 1]).then_inc(gt_sig, 1)

        @block.vector
        def _(dve):
            seq = [0]

            def link(ins):
                seq[0] += 1
                ins.then_inc(dve_seq, 1)
                dve.wait_ge(dve_seq, seq[0])

            def lo(g, count=None):
                dve.wait_ge(hi_done, g + 1 if count is None else count)
                nc.vector.tensor_tensor(Wlo[:, g % 2, :], raw[:, g % 2, :], Whi[:, g % 2, :].bitcast(fp32),
                                        ALU.subtract).then_inc(lo_done, 1)

            V2 = nc.vector
            for step in steps:
                if step[0] == "norm0":
                    for k in range(KT):
                        dve.wait_ge(sq_done, k + 1)
                        if k >= 1:
                            dve.wait_ge(acc_done, k)
                        if k == 0:
                            V2.tensor_copy(acc0, sqs[:, 0, :]).then_inc(acc_done, 1)
                        else:
                            V2.tensor_tensor(acc0, acc0, sqs[:, k % 2, :], ALU.add).then_inc(acc_done, 1)
                elif step[0] == "scale0":
                    dve.wait_ge(ss_done, 1)
                    V2.tensor_scalar(rb, PB[0][:, :], 1.0 / DM, EPS, ALU.mult, ALU.add).then_inc(ms_done, 1)
                    dve.wait_ge(sqrt_done, 1)
                    link(V2.reciprocal(rb, rb))
                    dve.wait_ge(small_in, 64)
                    for k in range(KT):
                        if k >= 2:
                            dve.wait_ge(hn_lo, k - 1)
                        V2.scalar_tensor_tensor(out=hn_t[:, k % 2, :], in0=XT[:, k, :], scalar=gpre_s[:, k:k + 1],
                                                in1=rb, op0=ALU.mult, op1=ALU.mult).then_inc(hn_f, 1)
                        if k >= 1:
                            dve.wait_ge(hn_hi, k)
                            V2.tensor_tensor(Xlo[:, k - 1, :], hn_t[:, (k - 1) % 2, :],
                                             Xhi[:, k - 1, :].bitcast(fp32), ALU.subtract).then_inc(hn_lo, 1)
                    dve.wait_ge(hn_hi, KT)
                    V2.tensor_tensor(Xlo[:, KT - 1, :], hn_t[:, (KT - 1) % 2, :],
                                     Xhi[:, KT - 1, :].bitcast(fp32), ALU.subtract).then_inc(hn_lo, 1)
                elif step[0] == "split":
                    lo(step[1])
                elif step[0] == "decay":
                    hf = HF.rearrange("p j t -> p (j t)")
                    dve.wait_ge(job_evac, jobs_by[0])
                    V2.tensor_scalar(tA, hf, X_SPLIT, None, ALU.max).then_inc(hx, 1)
                    dve.wait_ge(hy, 1)
                    V2.tensor_scalar(tA, hf, X_SPLIT, -LOG_TINY, ALU.min, ALU.add).then_inc(hx, 1)
                    V2.tensor_scalar(tC, hf, X_SPLIT, None, ALU.is_lt).then_inc(hx, 1)
                    dve.wait_ge(hx, 3)
                    link(V2.tensor_scalar(hf, tB, 1.0, None, ALU.add))
                    link(V2.reciprocal(hf, hf))
                    link(V2.tensor_tensor(hf, hf, tB, ALU.mult))
                    dve.wait_ge(hy, 2)
                    link(V2.scalar_tensor_tensor(out=tA, in0=tA, scalar=LOG_TINY - X_SPLIT, in1=tC,
                                                 op0=ALU.add, op1=ALU.mult))
                    dve.wait_ge(hy, 3)
                    link(V2.tensor_tensor(tA, tA, tD, ALU.subtract))
                    dve.wait_ge(const_in, 32)
                    dve.wait_ge(tab_in, 16)
                    for j in range(2):
                        link(V2.tensor_tensor_scan(tB[:, j * SEQ:(j + 1) * SEQ], rst, tA[:, j * SEQ:(j + 1) * SEQ],
                                                   0.0, ALU.mult, ALU.add))
                    V2.tensor_copy(blk[:, 0:16], tB.rearrange("p (c u) -> p c u", u=HGC)[:, :, HGC - 1]).then_inc(hg_k, 1)
                elif step[0] == "level":
                    lev = step[1]
                    dve.wait_ge(hg_k, 1)
                    if lev > 1:
                        dve.wait_ge(qk_done, lev - 1)
                    if lev <= 6:
                        L = LEVELS[lev - 1]
                        tb = tB.rearrange("p (n a u) -> p n a u", a=2, u=L // 2)
                        ta = tA.rearrange("p (n a u) -> p n a u", a=2, u=L // 2)
                        mid = tb[:, :, 0, L // 2 - 1:L // 2].broadcast_to([P, 1024 // L, L // 2])
                        V2.tensor_tensor(ta[:, :, 1, :], tb[:, :, 1, :], mid, ALU.subtract).then_inc(dve_seq, 1)
                        V2.tensor_tensor(ta[:, :, 0, :], mid, tb[:, :, 0, :], ALU.subtract).then_inc(arg_done, 1)
                        seq[0] += 1
                    else:
                        half = {7: 1, 8: 2, 9: 4}[lev]
                        bo = boff.rearrange("p (j c) -> p j c", j=2)
                        bl = blk[:, 0:16].rearrange("p (j c) -> p j c", j=2)
                        link(V2.memset(boff, 0.0))
                        for c0 in range(0, 8, 2 * half):
                            for c in range(c0 + half - 1, c0 - 1, -1):
                                nxt = bo[:, :, c + 1] if c < c0 + half - 1 else None
                                if nxt is None:
                                    link(V2.tensor_copy(bo[:, :, c], bl[:, :, c]))
                                else:
                                    link(V2.tensor_tensor(bo[:, :, c], bl[:, :, c], nxt, ALU.add))
                            for c in range(c0 + half + 1, c0 + 2 * half):
                                link(V2.tensor_tensor(bo[:, :, c], bl[:, :, c - 1], bo[:, :, c - 1], ALU.add))
                        tb = tB.rearrange("p (n a h u) -> p n a h u", a=2, h=half, u=HGC)
                        ta = tA.rearrange("p (n a h u) -> p n a h u", a=2, h=half, u=HGC)
                        ov = boff.rearrange("p (n a h) -> p n a h", a=2, h=half)
                        wide = [P, 8 // half, half, HGC]
                        V2.tensor_tensor(ta[:, :, 1], tb[:, :, 1], ov[:, :, 1, :].unsqueeze(3).broadcast_to(wide),
                                         ALU.add).then_inc(dve_seq, 1)
                        V2.tensor_tensor(ta[:, :, 0], ov[:, :, 0, :].unsqueeze(3).broadcast_to(wide), tb[:, :, 0],
                                         ALU.subtract).then_inc(arg_done, 1)
                        seq[0] += 1
                    dve.wait_ge(dec_done, lev)
                    dve.wait_ge(hg_mm, 4 * lev)
                    link(V2.tensor_tensor(tC, HQ.rearrange("p j t -> p (j t)"), tA, ALU.mult))
                    V2.tensor_tensor(tD, HF.rearrange("p j t -> p (j t)"), tA, ALU.mult).then_inc(qk_done, 1)
                elif step[0] == "level_mm":
                    lev = step[1]
                    for h in range(HGH):
                        n = 4 * lev + h
                        dve.wait_ge(hg_mm, n + 1)
                        pb = PB[HGB[h]][:, :]
                        pb3 = pb.rearrange("p (i t) -> p i t", t=P)
                        if lev == 0:
                            V2.tensor_tensor(AD[:, h], pb3, ident.unsqueeze(1).broadcast_to([P, TT, P]),
                                             ALU.mult).then_inc(hg_ev, 1)
                        elif lev <= 7:
                            dve.wait_ge(hg_ev, 4 * (lev - 1) + h + 1)
                            V2.copy_predicated(AD[:, h], masks[:, lev - 1, :].unsqueeze(1).broadcast_to([P, TT, P]),
                                               pb3).then_inc(hg_ev, 1)
                        elif lev == 8:
                            V2.tensor_copy(AO[:, h, 0:2, :], pb3[:, 0:2, :]).then_inc(hg_ev, 1)
                        else:
                            V2.tensor_copy(AO[:, h, 2:6, :], pb3).then_inc(hg_ev, 1)
                elif step[0] == "cmp_kd":
                    dve.wait_ge(job_evac, jobs_by[2])
                    V2.tensor_copy(KD, KCV.rearrange("p b (u a) -> p b a u", a=2)).then_inc(kd_done, 1)
                elif step[0] == "cmp_im2col":
                    dve.wait_ge(cmp_in, 8 * 16)
                    last = None
                    for b in range(2):
                        for k in range(NKV):
                            for mh in range(2):
                                src = CA[:, b, k, :].rearrange("p (n m) -> p m n", m=8)[:, :, mh:mh + NC]
                                bias = pos_s[:, b, 8 * mh:8 * mh + 8].unsqueeze(2).broadcast_to([P, 8, NC])
                                ins = V2.tensor_tensor(CT[:, b, 8 * mh:8 * mh + 8, k, :], src, bias, ALU.add)
                                if b == 1 and k == 1 and mh == 1:
                                    ins.then_inc(ct_done, 1)
                    dve.wait_ge(ct_hi, 1)
                    dve.wait_ge(ct_done, 1)
                    V2.tensor_tensor(Ulo[:, :, :].rearrange("p a t -> p (a t)")[:, 0:1984], view(aC, 1984),
                                     Uhi[:, :, :].rearrange("p a t -> p (a t)")[:, 0:1984].bitcast(fp32),
                                     ALU.subtract).then_inc(ct_lo, 1)
                elif step[0] == "cmp_silu":
                    dve.wait_ge(ce, 1)
                    cx, chn = CEXP[0:2 * NC, :], CHN[0:2 * NC, :, :].rearrange("p b j -> p (b j)")
                    link(V2.tensor_scalar(cx, cx, 1.0, None, ALU.add))
                    link(V2.reciprocal(cx, cx))
                    V2.tensor_tensor(chn, chn, cx, ALU.mult).then_inc(ch_done, 1)
                elif step[0] == "cmp_mlp":
                    dve.wait_ge(z_done, 4)
                    dve.wait_ge(c2_mm, 1)
                    V2.tensor_copy(kcT[:, 0:NC], PB[4][:, 0:NC]).then_inc(c2_ev, 1)
                    for g in range(NG):
                        V2.tensor_copy(vcR[32 * g:32 * g + NC], PB[5][32 * g:32 * g + NC, 0:128]
                                       .rearrange("p (k e) -> p k e", k=NKV)).then_inc(c2_ev, 1)
                elif step[0] == "hg_values":
                    dve.wait_ge(hgo_ev, 2)
                    link(V2.tensor_tensor(tB, tA, tA, ALU.mult))
                    link(V2.tensor_reduce(hgs, tB.rearrange("p (n e) -> p n e", e=HD), AX.X, ALU.add))
                    V2.tensor_scalar(hgs, hgs, 1.0 / HD, EPS, ALU.mult, ALU.add).then_inc(hx, 1)
                    dve.wait_ge(hy, 4)
                    link(V2.reciprocal(hgs, hgs))
                    link(V2.tensor_tensor(tA.rearrange("p (n e) -> p n e", e=HD), tA.rearrange("p (n e) -> p n e", e=HD),
                                          hgs.unsqueeze(2).broadcast_to([P, 16, HD]), ALU.mult))
                    dve.wait_ge(hy, 5)
                    link(V2.tensor_scalar(tC, tC, 1.0, None, ALU.add))
                    link(V2.reciprocal(tC, tC))
                    link(V2.tensor_tensor(tC, tC, HG.rearrange("p i c -> p (i c)"), ALU.mult))
                    V2.tensor_tensor(tD, tA, tC, ALU.mult).then_inc(oh_done, 1)
                elif step[0] == "hg_mix":
                    for j in range(2):
                        dve.wait_ge(mix_hi, j + 1)
                        V2.tensor_tensor(Xlo[:, 6 + j, :], PB[HGB[2 + j]][:, :], Xhi[:, 6 + j, :].bitcast(fp32),
                                         ALU.subtract).then_inc(mix_lo, 1)
                elif step[0] == "cmp_scores":
                    dve.wait_ge(ce, 2)
                    link(V2.tensor_scalar(gates, gates, 1.0, None, ALU.add))
                    link(V2.reciprocal(gates, gates))
                    for k in range(NKV):
                        dve.wait_ge(cs_mm, k + 1)
                        link(V2.tensor_tensor(PC[:, k * 384:(k + 1) * 384], PB[4 + k][:, 0:384], ctb[:, k, :], ALU.add))
                    pc3 = PC.rearrange("p (n c) -> p n c", c=NCP)
                    link(V2.tensor_reduce(cst, pc3, AX.X, ALU.min))
                    link(V2.tensor_scalar(cst, cst, 1e25, None, ALU.min))
                    V2.tensor_tensor(pc3, pc3, cst.unsqueeze(2).broadcast_to([P, 24, NCP]), ALU.subtract).then_inc(cs_ev, 1)
                    dve.wait_ge(cs_exp, 1)
                    link(V2.tensor_reduce(csum, pc3, AX.X, ALU.add))
                    link(V2.tensor_scalar(csum, csum, 1e-30, None, ALU.max))
                    link(V2.reciprocal(csum, csum))
                    for k in range(NKV):
                        gv = gates.rearrange("p (i k g b) -> p i k g b", i=TT, k=NKV, b=3)[:, :, k, :, 0]
                        cv = csum[:, k * 12:(k + 1) * 12].rearrange("p (i g) -> p i g", g=NG)
                        link(V2.tensor_tensor(cv, cv, gv, ALU.mult))
                    V2.tensor_tensor(pc3, pc3, csum.unsqueeze(2).broadcast_to([P, 24, NCP]), ALU.mult).then_inc(cs_p, 1)
                elif step[0] == "nsa":
                    gv = gates.rearrange("p (i h b) -> p i h b", h=NH, b=3)

                    def normalise(n):
                        h, b, i = rows[n]
                        w = (i + 1) * P
                        dve.wait_ge(p_exp, n + 1)
                        link(V2.reciprocal(rden[:, n:n + 1], den[:, n:n + 1]))
                        V2.tensor_scalar(SR[:, n % 3, 0:w], SR[:, n % 3, 0:w], rden[:, n:n + 1],
                                         gv[:, i, h, 1 + b:2 + b], ALU.mult, ALU.mult).then_inc(p_done, 1)

                    def mix_lo_part(j):
                        dve.wait_ge(mix_hi, 2 + j + 1)
                        V2.tensor_tensor(Xlo[:, j, :], PB[OB[j % 2]][:, :], Xhi[:, j, :].bitcast(fp32),
                                         ALU.subtract).then_inc(mix_lo, 1)

                    for n in range(len(rows) + 4):
                        if n < len(rows):
                            h, b, i = rows[n]
                            w = (i + 1) * P
                            dve.wait_ge(s_mm, n + 1)
                            if n >= 3:
                                dve.wait_ge(t_mm, n - 2)
                            V2.tensor_tensor_reduce(out=SR[:, n % 3, 0:w], in0=ntab[:, h, SEQ - w:SEQ],
                                                    in1=PB[ROWB[n % 3]][:, 0:w], scale=1.0, scalar=3e38,
                                                    op0=ALU.add, op1=ALU.min,
                                                    accum_out=mneg[:, n:n + 1]).then_inc(s_ev, 1)
                        if 1 <= n < len(rows) + 1:
                            normalise(n - 1)
                        if n >= 19 and (n - 19) % 16 == 0:
                            mix_lo_part((n - 19) // 16)
                elif step[0] == "dil":
                    def normalise(n):
                        dve.wait_ge(dp_exp, n + 1)
                        link(V2.reciprocal(rden[:, 48 + n:49 + n], den[:, 48 + n:49 + n]))
                        V2.tensor_scalar(DSR[:, n % 3, :], DSR[:, n % 3, :], rden[:, 48 + n:49 + n], None,
                                         ALU.mult).then_inc(dp_done, 1)

                    for n in range(len(drows) + 1):
                        if n < len(drows):
                            r, hh = drows[n]
                            dve.wait_ge(ds_mm, n + 1)
                            if n >= 3:
                                dve.wait_ge(dt_mm, n - 2)
                            link(V2.tensor_tensor_reduce(out=DSR[:, n % 3, 0:SEQ], in0=d0tab[:, hh, 3 - r:3 - r + SEQ],
                                                         in1=PB[0][:, :],
                                                         scale=1.0, scalar=3e38, op0=ALU.add, op1=ALU.min,
                                                         accum_out=st[:, 32 + n:33 + n]))
                            link(V2.tensor_tensor_reduce(out=DSR[:, n % 3, SEQ:768], in0=d12tab[:, hh, :],
                                                         in1=PB[1][:, 0:256],
                                                         scale=1.0, scalar=3e38, op0=ALU.add, op1=ALU.min,
                                                         accum_out=st[:, 40 + n:41 + n]))
                            V2.tensor_tensor(mneg[:, 48 + n:49 + n], st[:, 32 + n:33 + n], st[:, 40 + n:41 + n],
                                             ALU.min).then_inc(ds_ev, 1)
                        if n >= 1:
                            normalise(n - 1)
                        if n < len(drows):
                            dve.wait_ge(y_mm, n + 1)
                            V2.tensor_copy(PR[:, n % TT, (n // TT) * 512:(n // TT + 1) * 512], PB[2][:, :]).then_inc(y_ev, 1)
                    for g in range(3):
                        dve.wait_ge(mix_hi, 5 + g + 1)
                        V2.tensor_tensor(Xlo[:, 3 + g, :].rearrange("p (i r) -> p i r", r=DIL),
                                         PB[5 + g][:, :].rearrange("p (r i) -> p i r", r=DIL),
                                         Xhi[:, 3 + g, :].bitcast(fp32).rearrange("p (i r) -> p i r", r=DIL),
                                         ALU.subtract).then_inc(mix_lo, 1)

            def first_halves(a):
                if a == 0:
                    dve.wait_ge(res_in, 48)
                for t in range(TT):
                    dve.wait_ge(y_sq, 8 * a + t + 1)
                    V2.tensor_tensor(Y[:, t, 0:512], PB[t][:, :] if a == 0 else Y[:, t, 0:512], GB[:, a, 0:512],
                                     ALU.mult).then_inc(y_gain, 1)
                V2.tensor_scalar(bias_a[:, TT * a:TT * a + TT], ss_a[:, TT * a:TT * a + TT], 1.0 / DM, EPS,
                                 ALU.mult, ALU.add).then_inc(y_first, 1)

            def post_norm(a):
                for s in range(TT + 1):
                    if s < TT:
                        k, yv = TT * a + s, Y[:, s, 512:1024]
                        if a == 1:
                            dve.wait_ge(dn_mm, 8 * EIGHTHS - 4 + s + 1)
                            dve.wait_ge(dn_ev, 8 * (EIGHTHS - 1) + 1)
                            V2.tensor_tensor(yv, yv, PB[4 + s][:, :], ALU.add).then_inc(dn_ev, 1)
                        dve.wait_ge(y_sq, 8 * a + 4 + s + 1)
                        V2.tensor_tensor(yv, PB[4 + s][:, :] if a == 0 else yv, GB[:, a, 512:1024],
                                         ALU.mult).then_inc(y_gain, 1)
                        dve.wait_ge(y_rms, k + 1)
                        link(V2.reciprocal(rs_y[:, k:k + 1], rs_y[:, k:k + 1]))
                        dve.wait_ge(y_gain, 8 * a + 4 + s + 1)
                        V2.scalar_tensor_tensor(out=H[:, s, :], in0=Y[:, s, :], scalar=rs_y[:, k:k + 1],
                                                in1=H[:, s, :], op0=ALU.mult, op1=ALU.add).then_inc(h_done, 1)
                    if s >= 1:
                        k = TT * a + s - 1
                        dve.wait_ge(h_rms, k + 1)
                        V2.reciprocal(rs_h[:, k:k + 1], rs_h[:, k:k + 1]).then_inc(h_rs, 1)
                        if a == 0:
                            dve.wait_ge(h_rs, k + 1)
                            V2.tensor_scalar(diag[:, s - 1, :], ident, rs_h[:, k:k + 1], None, ALU.mult).then_inc(diag_done, 1)
                for k in range(KT):
                    dve.wait_ge(x_hi, KT * a + k + 1)
                    V2.scalar_tensor_tensor(out=Xlo[:, k, :], in0=PB[k][:, :], scalar=gvec_s[:, a, k:k + 1],
                                            in1=Xhi[:, k, :].bitcast(fp32), op0=ALU.mult,
                                            op1=ALU.subtract).then_inc(x_lo, 1)

            for g in range(G_OUT, G_OUT + 4):
                lo(g)
            first_halves(0)
            lo(G_MLP)
            post_norm(0)
            lo(G_MLP + 1)

            def mlp_turn(i, last):
                for e in range(2):
                    for c in range(4):
                        if c < 2:
                            for f in range(2 * c, 2 * c + 2):
                                u = 4 * e + f
                                dve.wait_ge(up_relu, i * 8 + u + 1)
                                if u:
                                    dve.wait_ge(up_lo, i * 8 + u)
                                V2.tensor_tensor(usq[:, f % 2, :], relu[:, f % 2, :], relu[:, f % 2, :],
                                                 ALU.mult).then_inc(up_sq, 1)
                                dve.wait_ge(up_hi, i * 8 + u + 1)
                                dve.wait_ge(up_sq, i * 8 + u + 1)
                                V2.tensor_tensor(Ulo[:, f, :], usq[:, f % 2, :], Uhi[:, f, :].bitcast(fp32),
                                                 ALU.subtract).then_inc(up_lo, 1)
                        elif not (last and e == 1 and c == 3):
                            nh = c - 2
                            for t in range(TT):
                                bank = PB[(4 if (nh == 0) == (e == 0) else 0) + t]
                                dve.wait_ge(dn_mm, i * 16 + 8 * e + 4 * nh + t + 1)
                                yv = Y[:, t, nh * 512:(nh + 1) * 512]
                                dve.wait_ge(dn_ev, i * 16 + 8 * e + 1)
                                V2.tensor_tensor(yv, yv, bank[:, :], ALU.add).then_inc(dn_ev, 1)
                        if last and e == 1 and c == 3:
                            continue
                        g = G_MLP + 2 + 4 * e + c
                        lo(g, i * 8 + g + 1)
                dve.wait_ge(up_lo, i * 8 + 8)

            with dve.Fori(0, EIGHTHS // 2 - 1) as i:
                mlp_turn(i, False)
            mlp_turn(EIGHTHS // 2 - 1, True)
            first_halves(1)
            post_norm(1)
            lo(G_GATE + 1)
            for g in range(G_GATE + 2, N_PANELS):
                lo(g)
            for n in range(8):
                t, nh = n % TT, n // TT
                dve.wait_ge(gt_sig, n + 1)
                link(V2.tensor_tensor(Gsig[:, n % 4, :], Gsig[:, n % 4, :], PR[:, t, nh * 512:(nh + 1) * 512], ALU.mult))
                hv = H[:, t, nh * 512:(nh + 1) * 512]
                V2.tensor_tensor(hv, hv, Gsig[:, n % 4, :], ALU.add).then_inc(o_done, 1)

        @block.tensor
        def _(pe):
            mm = nc.tensor.matmul

            def three(out_ap, w, x, start, stop):
                mm(out_ap, w[0], x[0], start=start, stop=False)
                mm(out_ap, w[0], x[1], start=False, stop=False)
                return mm(out_ap, w[1], x[0], start=False, stop=stop)

            def W(g, a, b):
                return Whi[:, g % 2, a:b], Wlo[:, g % 2, a:b]

            def X(k, sl):
                return Xhi[:, k, sl], Xlo[:, k, sl]

            for step in steps:
                if step[0] == "norm0":
                    pe.wait_ge(ones_set, 1)
                    pe.wait_ge(acc_done, KT)
                    mm(PB[0][:, :], ones, acc0, start=True, stop=True).then_inc(ss_done, 1)
                elif step[0] == "gemm":
                    g = step[1]
                    pe.wait_ge(lo_done, g + 1)
                    mine = panel_jobs[g]
                    second = g - 1 in PAIRS
                    if g in PAIRS or second:
                        mine = panel_jobs[g if second else g + 1]
                    if g == 0:
                        pe.wait_ge(ms_done, 1)
                        for k in range(KT):
                            pe.wait_ge(hn_lo, k + 1)
                            for n in mine:
                                c = jobs[n][2]
                                last = three(PB[n][:, :], W(g, k * 256 + c, k * 256 + c + P), X(k, slice(0, SEQ)),
                                             k == 0, k == KT - 1)
                                if k == KT - 1:
                                    last.then_inc(job_done, 1)
                        continue
                    for n in mine:
                        _, kind, c, w, t, dst, _ = jobs[n]
                        bank = PB[n % 4]
                        if n >= 4 and not second:
                            pe.wait_ge(job_evac, n - 3)
                        if kind == "T":
                            for k in range(KT):
                                last = three(bank[:, :], W(g, k * 256 + c, k * 256 + c + P), X(k, slice(0, SEQ)),
                                             k == 0, k == KT - 1)
                        elif kind == "B":
                            for k in range(4):
                                last = three(bank[:, 0:w], X(4 * second + k, slice(t * P, (t + 1) * P)),
                                             W(g, k * 512, k * 512 + w), not second and k == 0, second and k == 3)
                        elif kind == "H":
                            b = w
                            pe.wait_ge(ct_lo, 1)
                            pe.wait_ge(z_done, 2)
                            uh = Uhi[:, :, :].rearrange("p a t -> p (a t)")
                            ul = Ulo[:, :, :].rearrange("p a t -> p (a t)")
                            for m in range(8):
                                o = b * 992 + (8 * second + m) * 62
                                last = three(bank[0:124, 0:256], (uh[:, o:o + 124], ul[:, o:o + 124]),
                                             W(g, m * 256, (m + 1) * 256), not second and m == 0, second and m == 7)
                        else:
                            pe.wait_ge(job_evac, jobs_by[14])
                            flat = dst.rearrange("p j e -> p (j e)")
                            for r in range(DIL):
                                last = nc.tensor.transpose(bank[:, r * P:(r + 1) * P], flat[:, r:SEQ:DIL], ident)
                        if kind in "TX" or second:
                            last.then_inc(job_done, 1)
                        elif n == mine[-1]:
                            last.then_inc(half_done, 1)
                elif step[0] == "level_mm":
                    lev = step[1]
                    if lev == 0:
                        pe.wait_ge(hg_k, 1)
                        Qs, Ks = HQ, HF
                    else:
                        pe.wait_ge(qk_done, lev)
                        Qs = tC.rearrange("p (j t) -> p j t", j=2)
                        Ks = tD.rearrange("p (j t) -> p j t", j=2)
                    for h in range(HGH):
                        j, r = h // 2, slice((h % 2) * HD, (h % 2 + 1) * HD)
                        bank = PB[HGB[h]]
                        if lev:
                            pe.wait_ge(hg_ev, 4 * (lev - 1) + h + 1)
                        if lev == 5:
                            pe.wait_ge(c2_ev, 4)
                        if lev <= 7:
                            for i in range(TT):
                                last = mm(bank[:, i * P:(i + 1) * P], Ks[r, j, i * P:(i + 1) * P], Qs[r, j, i * P:(i + 1) * P],
                                          start=True, stop=True)
                        elif lev == 8:
                            for b, s in enumerate((0, 2)):
                                last = mm(bank[:, b * P:(b + 1) * P], Ks[r, j, s * P:(s + 1) * P],
                                          Qs[r, j, (s + 1) * P:(s + 2) * P], start=True, stop=True)
                        else:
                            for s in range(2):
                                last = mm(bank[:, s * 256:(s + 1) * 256], Ks[r, j, s * P:(s + 1) * P], Qs[r, j, 256:512],
                                          start=True, stop=True)
                        last.then_inc(hg_mm, 1)
                elif step[0] == "cmp_mlp":
                    pe.wait_ge(ch_done, 1)
                    pe.wait_ge(small_in, 64)
                    pe.wait_ge(const_in, 32)
                    pe.wait_ge(hg_ev, 4 * 5)
                    for b in range(2):
                        for j in range(2):
                            last = nc.tensor.transpose(PB[7][:, (2 * b + j) * 62:(2 * b + j + 1) * 62],
                                                       CHN[0:2 * NC, b, j * P:(j + 1) * P], ident[0:2 * NC, 0:2 * NC])
                    last.then_inc(chT_mm, 1)
                    pe.wait_ge(chT_ev, 1)
                    for k in range(NKV):
                        for j in range(2):
                            mm(PB[4][k * HD:(k + 1) * HD, 0:NC], w2s[:, 0, j, :], CH[:, 0, j, k * NC:(k + 1) * NC],
                               start=(j == 0), stop=(j == 1))
                    for g in range(NG):
                        for k in range(NKV):
                            for j in range(2):
                                last = mm(PB[5][32 * g:32 * g + NC, k * HD:(k + 1) * HD], CH[:, 1, j, k * NC:(k + 1) * NC],
                                          w2s[:, 1, j, :], start=(j == 0), stop=(j == 1))
                    last.then_inc(c2_mm, 1)
                elif step[0] == "hg_values":
                    pe.wait_ge(hg_ev, 4 * NLEV)
                    pe.wait_ge(job_evac, jobs_by[4])
                    OFF = {(0, 1): 0, (2, 3): 1, (0, 2): 2, (0, 3): 3, (1, 2): 4, (1, 3): 5}
                    for a in range(2):
                        for i in (2 * a, 2 * a + 1):
                            for h in range(HGH):
                                o = (i % 2) * 256 + h * HD
                                for s in range(i + 1):
                                    lhs = AD[:, h, i, :] if s == i else AO[:, h, OFF[(s, i)], :]
                                    last = mm(PB[HGB[a]][:, o:o + HD], lhs, HI[:, s, h * HD:(h + 1) * HD],
                                              start=(s == 0), stop=(s == i))
                        last.then_inc(hgo_mm, 1)
                elif step[0] == "hg_mix":
                    pe.wait_ge(oh_done, 1)
                    for j in range(2):
                        for i in range(TT):
                            last = nc.tensor.transpose(PB[HGB[2 + j]][:, i * P:(i + 1) * P],
                                                       tD[:, i * 256 + j * P:i * 256 + (j + 1) * P], ident)
                        last.then_inc(mixT_mm, 1)
                elif step[0] == "cmp_scores":
                    pe.wait_ge(job_evac, jobs_by[12])
                    pe.wait_ge(hgo_ev, 2)
                    pe.wait_ge(c2_ev, 4)
                    for k in range(NKV):
                        r = slice(k * HD, (k + 1) * HD)
                        for i in range(TT):
                            for g in range(NG):
                                o = (i * NG + g) * NCP
                                last = mm(PB[4 + k][:, o:o + NCP], T[r, Q0 + g, i * P:(i + 1) * P], kcT[r, :],
                                          start=True, stop=True)
                        last.then_inc(cs_mm, 1)
                elif step[0] == "cmp_turn":
                    pe.wait_ge(cs_p, 1)
                    for k in range(NKV):
                        for i in range(TT):
                            last = nc.tensor.transpose(PB[4 + k][0:96, i * P:(i + 1) * P],
                                                       PC[:, k * 384 + i * 96:k * 384 + (i + 1) * 96], ident)
                        last.then_inc(ct_mm, 1)
                elif step[0] == "nsa":
                    pe.wait_ge(job_evac, len(jobs))
                    pe.wait_ge(ct_ev, 2)
                    pe.wait_ge(mix_lo, 2)

                    def transposes(n):
                        h, b, i = rows[n]
                        pe.wait_ge(p_done, n + 1)
                        if n >= 3:
                            pe.wait_ge(t_ev, n - 2)
                        for j in range(i + 1):
                            last = nc.tensor.transpose(PB[TRB[n % 3]][:, j * P:(j + 1) * P],
                                                       SR[:, n % 3, j * P:(j + 1) * P], ident)
                        last.then_inc(t_mm, 1)

                    def values(h):
                        k, g, half = h // NG, h % NG, h % 2
                        j2 = h // 2
                        pe.wait_ge(t_ev, 8 * h + 8)
                        if half == 0 and j2 >= 2:
                            pe.wait_ge(mix_lo, 2 + j2 - 1)
                        o = PB[OB[j2 % 2]][half * HD:(half + 1) * HD, :]
                        mm(o, vcR[32 * g:32 * g + NCP, k, :], PCT[32 * g:32 * g + NCP, k, :], start=True, stop=False)
                        for b in range(2):
                            for s in range(TT):
                                last = mm(o[:, s * P:SEQ], V[:, (VS, VW)[b], s, k * HD:(k + 1) * HD],
                                          PT[:, h % 2, b, s, s * P:SEQ], start=False, stop=(b == 1 and s == TT - 1))
                        last.then_inc(pv_done, 1)

                    for n in range(len(rows) + 4):
                        if n < len(rows):
                            h, b, i = rows[n]
                            k, g = h // NG, h % NG
                            if n >= 3:
                                pe.wait_ge(s_ev, n - 2)
                            r = slice(k * HD, (k + 1) * HD)
                            mm(PB[ROWB[n % 3]][:, 0:(i + 1) * P], T[r, Q0 + g, i * P:(i + 1) * P],
                               T[r, (KS, KW)[b], 0:(i + 1) * P], start=True, stop=True).then_inc(s_mm, 1)
                        if 2 <= n < len(rows) + 2:
                            transposes(n - 2)
                        if n >= 11 and (n - 11) % 8 == 0:
                            values((n - 11) // 8)
                elif step[0] == "dil":
                    pe.wait_ge(t_ev, len(rows))
                    pe.wait_ge(s_ev, len(rows))
                    pe.wait_ge(mix_lo, 5)

                    def product(n):
                        t, c = n % TT, (n // TT) * 512
                        pe.wait_ge(lo_done, G_PLE + 1)
                        if n:
                            pe.wait_ge(y_ev, n)
                        for k in range(2):
                            last = three(PB[2][:, :], W(G_PT, k * SEQ + t * P, k * SEQ + (t + 1) * P),
                                         W(G_PLE, k * DM + c, k * DM + c + 512), k == 0, k == 1)
                        last.then_inc(y_mm, 1)

                    def transposes(n):
                        pe.wait_ge(dp_done, n + 1)
                        if n >= 1:
                            pe.wait_ge(dt_ev, 2 * n)
                        for j in range(6):
                            bank = PB[3 + j // 4]
                            last = nc.tensor.transpose(bank[:, (j % 4) * P:(j % 4 + 1) * P],
                                                       DSR[:, n % 3, j * P:(j + 1) * P], ident)
                        last.then_inc(dt_mm, 1)

                    def values(n):
                        r, hh = drows[n]
                        pe.wait_ge(dt_ev, 2 * n + 2)
                        c = slice(hh * HD, (hh + 1) * HD)
                        for s in range(TT):
                            mm(PB[5][c, r * P:(r + 1) * P], V[:, DV0, s, c], DPT[:, n % 2, s, :], start=(s == 0), stop=(s == TT - 1))
                        for g in range(1, 3):
                            last = mm(PB[5 + g][c, r * P:(r + 1) * P], V[:, DV0 + g, r, c], DPT[:, n % 2, 3 + g, :],
                                      start=True, stop=True)
                        last.then_inc(dpv_done, 1)

                    for n in range(len(drows) + 3):
                        if n < len(drows):
                            r, hh = drows[n]
                            if n >= 1:
                                pe.wait_ge(ds_ev, n)
                            p = slice(hh * HD, (hh + 1) * HD)
                            mm(PB[0][:, :], T[p, DQ0, r:SEQ:DIL], T[p, DK0, :], start=True, stop=True)
                            for g in range(1, 3):
                                last = mm(PB[1][:, (g - 1) * P:g * P],
                                          T[p, DQ0 + g, r:SEQ:DIL], T[p, DK0 + g, r:SEQ:DIL], start=True, stop=True)
                            last.then_inc(ds_mm, 1)
                            product(n)
                        if 2 <= n < len(drows) + 2:
                            transposes(n - 2)
                        if n >= 3:
                            values(n - 3)

            pe.wait_ge(y_ev, 8)
            for c in range(4):
                g = G_OUT + c
                nh, kh = c // 2, c % 2
                pe.wait_ge(mix_lo, KT if kh else 5)
                pe.wait_ge(lo_done, g + 1)
                for t in range(TT):
                    for k in range(4):
                        last = three(PB[4 * nh + t][:, :], X(MIX_ORDER[4 * kh + k], slice(t * P, (t + 1) * P)),
                                     W(g, k * 512, (k + 1) * 512), kh == 0 and k == 0, kh == 1 and k == 3)
                    if kh == 1:
                        last.then_inc(y_mm, 1)
                if kh == 0:
                    last.then_inc(half_done, 1)

            def turn_h(a):
                pe.wait_ge(y_gain, 8 * a + 4)
                for t in range(TT):
                    if a == 0:
                        pe.wait_ge(diag_done, t + 1)
                    else:
                        pe.wait_ge(h_done, TT + t + 1)
                    todo = [(k, t) for k in range(4 + t)] + [(4 + t, u) for u in range(t + 1)]
                    for k, u in todo:
                        dst, src = PB[k][:, u * P:(u + 1) * P], H[:, u, k * P:(k + 1) * P]
                        if a == 0:
                            last = mm(dst, src, diag[:, u, :], start=True, stop=True)
                        else:
                            last = nc.tensor.transpose(dst, src, ident)
                        if t == TT - 1 and u == TT - 1:
                            last.then_inc(h_turned, 1)

            turn_h(0)
            with pe.Fori(0, EIGHTHS // 2) as i:
                for e in range(2):
                    up0 = 0 if e == 0 else 4
                    for c in range(2):
                        g = G_MLP + 4 * e + c
                        pe.wait_ge(lo_done, i * 8 + g + 1)
                        for f in range(2 * c, 2 * c + 2):
                            if e == 1:
                                pe.wait_ge(dn_ev, i * 16 + 5)
                            for k in range(KT):
                                if e == 0 and f == 0:
                                    pe.wait_ge(x_lo, k + 1)
                                o = k * 256 + (f % 2) * P
                                last = three(PB[up0 + f][:, :], W(g, o, o + P), X(k, slice(0, SEQ)), k == 0, k == KT - 1)
                            last.then_inc(up_mm, 1)
                    for nh in range(2):
                        g = G_MLP + 4 * e + 2 + nh
                        b0 = 4 if (nh == 0) == (e == 0) else 0
                        pe.wait_ge(lo_done, i * 8 + g + 1)
                        if nh == 1:
                            pe.wait_ge(up_lo, i * 8 + 4 * e + 4)
                        else:
                            pe.wait_ge(dn_ev, i * 16 + 8 * e + 1)
                        for k in range(4):
                            if nh == 0:
                                pe.wait_ge(up_lo, i * 8 + 4 * e + k + 1)
                            for t in range(TT):
                                last = three(PB[b0 + t][:, :], (Uhi[:, k, t * P:(t + 1) * P], Ulo[:, k, t * P:(t + 1) * P]),
                                             W(g, k * 512, (k + 1) * 512), k == 0, k == 3)
                                if k == 3:
                                    last.then_inc(dn_mm, 1)
                pe.wait_ge(dn_ev, i * 16 + 13)
            turn_h(1)
            for c in range(4):
                g = G_GATE + c
                nh, kh = c // 2, c % 2
                pe.wait_ge(lo_done, g + 1)
                for t in range(TT):
                    for k in range(4):
                        if nh == 0 and t == 0:
                            pe.wait_ge(x_lo, KT + 4 * kh + k + 1)
                        last = three(PB[4 * nh + t][:, :], X(4 * kh + k, slice(t * P, (t + 1) * P)), W(g, k * 512, (k + 1) * 512),
                                     kh == 0 and k == 0, kh == 1 and k == 3)
                    if kh == 1:
                        last.then_inc(gt_mm, 1)
                    elif t == TT - 1:
                        last.then_inc(half_done, 1)


def panels(w_in, w_out, cmp_w1, w_up, w_down, w_gate, w_ple, p):
    out = np.zeros((N_PANELS, P, PAN), np.float32)

    def cols(g, parts):
        v = out[g].reshape(P, KT, 256)
        o = 0
        for c, n in parts:
            v[:, :, o:o + n] = w_in[:, c:c + n].reshape(KT, P, n).transpose(1, 0, 2)
            o += n

    def block(g, w):
        out[g] = w.reshape(4, P, 512).transpose(1, 0, 2).reshape(P, PAN)

    cols(0, [(C_HF, 256)])
    cols(1, [(C_HQ, 256)])
    cols(2, [(C_KC, 256)])
    def pair(g, parts):
        o = 0
        for c, n in parts:
            for m in range(2):
                out[g + m].reshape(P, 4, 512)[:, :, o:o + n] = \
                    w_in[m * 512:(m + 1) * 512, c:c + n].reshape(4, P, n).transpose(1, 0, 2)
            o += n

    pair(3, [(C_HI, 256), (C_VS, 128), (C_VW, 128)])
    for b in range(2):
        for m in range(2):
            out[5 + 2 * b + m] = cmp_w1[b, m * 1024:(m + 1) * 1024].reshape(8, P, 256).transpose(1, 0, 2).reshape(P, PAN)
    pair(9, [(C_HG, 256), (C_DV, 128), (C_GT, 18)])
    q = [(C_NQ + h * HD, HD) for h in (0, 3, 1, 4, 2, 5)]
    cols(11, q[:4])
    cols(12, q[4:] + [(C_KS, 128)])
    cols(13, [(C_KW, 128), (C_DV + 128, 128)])
    cols(14, [(C_DV + 256, 128)])
    cols(15, [(C_DQ, 256)])
    cols(16, [(C_DQ + 256, 256)])
    cols(17, [(C_DK + 128, 256)])
    for c in range(4):
        nh, kh = c // 2, c % 2
        rows = np.concatenate([np.arange(k * P, (k + 1) * P) for k in MIX_ORDER[4 * kh:4 * kh + 4]])
        block(G_OUT + c, w_out[rows, nh * 512:(nh + 1) * 512])
        block(G_GATE + c, w_gate[kh * 512:(kh + 1) * 512, nh * 512:(nh + 1) * 512])
    out[G_PT, :, :2 * SEQ] = p.T.reshape(2, P, SEQ).transpose(1, 0, 2).reshape(P, 2 * SEQ)
    out[G_PLE] = w_ple.reshape(2, P, DM).transpose(1, 0, 2).reshape(P, PAN)
    for e in range(EIGHTHS):
        for c in range(2):
            f = e * 512 + c * 256
            out[G_MLP + 4 * e + c] = w_up[:, f:f + 256].reshape(KT, P, 256).transpose(1, 0, 2).reshape(P, PAN)
            block(G_MLP + 4 * e + 2 + c, w_down[e * 512:(e + 1) * 512, c * 512:(c + 1) * 512])
    return out


def kernel(**inputs):
    import numpy as _np
    import concourse.bacc as _bacc
    from concourse import mybir as _mybir
    from concourse.bass_utils import run_bass_kernel_spmd as _run

    a = {k: _np.asarray(v) for k, v in inputs.items()}
    x = a["x"][0]
    tiles = lambda v: v.reshape(-1, P).T
    arrays = {
        "xT": x.T.reshape(KT, P, SEQ).transpose(1, 0, 2),
        "xn": x,
        "wst": panels(a["w_in"][0], a["w_out"][0], a["cmp_w1"][0], a["w_up"][0], a["w_down"][0],
                      a["w_ple_gate"][0], a["w_ple_proj"][0], a["p"][0, 0]),
        "gpre": tiles(a["g_pre_mix"][0]),
        "gvec": _np.stack([tiles(a["g_pre_mlp"][0]), tiles(a["g_ple"][0])], 1),
        "gpost": _np.stack([a["g_post_mix"][0], a["g_post_mlp"][0]]),
        "pos": a["cmp_pos"][0].reshape(2, 16, P).transpose(2, 0, 1),
        "w2": a["cmp_w2"][0].reshape(2, 2, P, HD).transpose(2, 0, 1, 3),
        "ctab": constant_table(),
        "lmask": level_masks(),
        "eye": _np.eye(P, dtype=_np.float32),
    }
    nc = _bacc.Bacc("TRN2", target_bir_lowering=False, num_devices=1)
    args = []
    for name in arrays:
        arrays[name] = _np.ascontiguousarray(arrays[name])
        args.append(nc.dram_tensor(name, arrays[name].shape, _mybir.dt.from_np(arrays[name].dtype),
                                   kind="ExternalInput").ap())
    args.append(nc.dram_tensor("out", (SEQ, DM), _mybir.dt.float32, kind="ExternalOutput").ap())
    build(nc, *args)
    r = _run(nc, [arrays], core_ids=[0])
    return r.results[0]["out"].reshape(1, SEQ, DM)
```

```python
import concourse.bass as bass
from concourse import mybir
from contextlib import ExitStack
import numpy as np

P = 128
SEQ, DM, DFF, PLE = 512, 1024, 4096, 256
TT = SEQ // P
KT = DM // P
HD = 64
NH, NKV, NG = 6, 2, 3
CB, CS, NC, NCP = 32, 16, 31, 32
DIL = 4
HGH = 4
MIX_ORDER = (0, 1, 2, 6, 7, 3, 4, 5)
PAN = 2048
EPS = 1e-6
NEG = -1e30
X_SPLIT = -40.0
LOG_TINY = float(np.log(1e-30))

N_IN = 18
G_PT = N_IN
G_PLE = G_PT + 1
G_OUT = G_PLE + 1
G_MLP = G_OUT + 4
EIGHTHS = 8
G_GATE = G_MLP + 4 * EIGHTHS
N_PANELS = G_GATE + 4

C_NQ, C_KC, C_KS, C_VS, C_KW, C_VW, C_GT = 0, 384, 640, 768, 896, 1024, 1152
C_DQ, C_DK, C_DV, C_HQ, C_HF, C_HI, C_HG = 1170, 1554, 1938, 2322, 2578, 2834, 3090

D0W = SEQ + 4
TB_D0 = 0
TB_D12 = TB_D0 + 2 * D0W
TB_NSA = TB_D12 + 2 * 256
TB_CMP = TB_NSA + NH * SEQ
TB_RST = TB_CMP + NKV * TT * NG * NCP
TB_W = TB_RST + SEQ

LEVELS = (2, 4, 8, 16, 32, 64, 128)
HGC = 64


def slopes():
    n = 12
    s = (2.0 ** (-8.0 * np.arange(1, n + 1) / n)).reshape(-1, 4)
    return s[:, 2:].reshape(-1).astype(np.float32), s[:, :2].reshape(-1).astype(np.float32)


def constant_table():
    nsa, dil = slopes()
    t = np.zeros((P, TB_W), np.float32)
    p = np.arange(P)[:, None]
    rel = p + 384 - np.arange(SEQ)[None, :]
    for h in range(NH):
        t[:, TB_NSA + h * SEQ:TB_NSA + (h + 1) * SEQ] = np.where(rel >= 0, nsa[h] * rel.astype(np.float32), -NEG)
    for hh in range(2):
        rel = DIL * p + 3 - np.arange(D0W)[None, :]
        t[:, TB_D0 + hh * D0W:TB_D0 + (hh + 1) * D0W] = np.where(
            (rel >= 0) & (rel <= 128), dil[hh] * rel.astype(np.float32), -NEG)
        rel = DIL * (p - np.arange(P)[None, :])
        o = TB_D12 + hh * 256
        t[:, o:o + P] = np.where(rel >= 0, dil[2 + hh] * rel.astype(np.float32), -NEG)
        t[:, o + P:o + 256] = np.where((rel >= 0) & (rel % 16 == 0), dil[4 + hh] * rel.astype(np.float32), -NEG)
    for k in range(NKV):
        for i in range(TT):
            for g in range(NG):
                o = TB_CMP + ((k * TT + i) * NG + g) * NCP
                n = np.arange(NCP)[None, :]
                tok = i * P + p
                d = np.abs(tok - (n * CS + 0.5 * (CB - 1))).astype(np.float32)
                ok = (n * CS + CB - 1 <= tok) & (n < NC)
                t[:, o:o + NCP] = np.where(ok, nsa[k * NG + g] * d, -NEG)
    t[:, TB_RST:TB_RST + SEQ] = (np.arange(SEQ) % HGC != 0)
    return t


def level_masks():
    s, q = np.arange(P)[:, None], np.arange(P)[None, :]
    m = [(s // L == q // L) & (q // (L // 2) == s // (L // 2) + 1) for L in LEVELS]
    return np.stack(m, 1).astype(np.int32)


def build(nc, xn, wst, gpre, gvec, gpost, pos, w2, ctab, lmask, eye, out):
    fp32, f32r, i32 = mybir.dt.float32, mybir.dt.float32r, mybir.dt.int32
    ALU, ACT, AX = mybir.AluOpType, mybir.ActivationFunctionType, mybir.AxisListType
    ctx = ExitStack()
    with ctx:
        def sb(name, shape, dt):
            return ctx.enter_context(nc.sbuf_tensor(name, shape, dt))

        def sem(name):
            return ctx.enter_context(nc.semaphore(name))

        raw = sb("raw", [P, 2, PAN], fp32)
        Whi = sb("Whi", [P, 2, PAN], f32r)
        Wlo = sb("Wlo", [P, 2, PAN], f32r)
        Xhi = sb("Xhi", [P, KT, SEQ], f32r)
        Xlo = sb("Xlo", [P, KT, SEQ], f32r)
        Uhi = sb("Uhi", [P, 4, SEQ], f32r)
        Ulo = sb("Ulo", [P, 4, SEQ], f32r)
        AW = 26500
        arena = sb("arena", [P, AW], fp32)
        PB = [ctx.enter_context(nc.psum_tensor(f"bank{i}", [P, 512], fp32)) for i in range(8)]

        at = [0]

        def take(n):
            a = at[0]
            at[0] += n
            assert at[0] <= AW, at[0]
            return a

        def view(a, n):
            return arena[:, a:a + n]

        tab = view(take(TB_W), TB_W)
        aT = take(11 * SEQ)
        T = view(aT, 11 * SEQ).rearrange("p (j t) -> p j t", t=SEQ)
        Q0, KS, KW, DQ0, DK0 = 0, 3, 4, 5, 8
        V = view(take(5 * SEQ), 5 * SEQ).rearrange("p (v j e) -> p v j e", v=5, e=P)
        VS, VW, DV0 = 0, 1, 2
        HG = view(take(1024), 1024).rearrange("p (i c) -> p i c", i=TT)
        gates = view(take(72), 72)
        small = view(take(320), 320)
        kcT = view(take(NCP), NCP)
        vcR = view(take(128), 128).rearrange("p (k e) -> p k e", k=NKV)
        w2s = view(take(256), 256).rearrange("p (b j e) -> p b j e", b=2, j=2)
        aX = take(9728)
        CHN = view(take(512), 512).rearrange("p (b j) -> p b j", b=2)
        HQ = view(aX, 1024).rearrange("p (j t) -> p j t", j=2)
        HF = view(aX + 1024, 1024).rearrange("p (j t) -> p j t", j=2)
        HI = view(aX + 2048, 1024).rearrange("p (i c) -> p i c", i=TT)
        tA, tB, tC, tD = (view(aX + 3072 + 1024 * n, 1024) for n in range(4))
        AD = view(aX + 7168, 2048).rearrange("p (h i t) -> p h i t", h=HGH, i=TT)
        AO = view(aT + DQ0 * SEQ, 3072).rearrange("p (h b t) -> p h b t", h=HGH, t=P)
        PT = view(aX, 8192).rearrange("p (a b j t) -> p a b j t", a=2, b=2, j=TT)
        SR = view(aX + 8192, 4 * SEQ).rearrange("p (a n) -> p a n", a=4)
        PC = view(aX, 768)
        PCT = HG.rearrange("p i c -> p (i c)").rearrange("p (k t) -> p k t", k=NKV)
        DPT = view(aX, 2 * 768).rearrange("p (a b t) -> p a b t", a=2, t=P)
        DSR = view(aX + 1536, 3 * 768).rearrange("p (a n) -> p a n", a=3)
        XN = view(aX, 4096).rearrange("p (i n) -> p i n", i=TT)
        sqs = view(aX + 4096, 2048).rearrange("p (a n) -> p a n", a=2)
        diag0 = view(aX + 6144, 512).rearrange("p (t n) -> p t n", t=TT)
        aC = aT + DQ0 * SEQ
        KCV = view(aC, 1024).rearrange("p (b t) -> p b t", b=2)
        KD = view(aC + 1024, 1024).rearrange("p (b a u) -> p b a u", b=2, a=2)
        CT = view(aC, 1984).rearrange("p (b m k n) -> p b m k n", b=2, m=16, k=NKV)
        CA = view(aC + 2048, 1024).rearrange("p (b k u) -> p b k u", b=2, k=NKV)
        GS = view(aC, 1024)
        CHS = view(aC + 1024, 512)
        CHa = take(2 * 2 * 62)
        CH = view(CHa, 248).rearrange("p (b j n) -> p b j n", b=2, j=2)
        PR = view(TB_NSA, 4096).rearrange("p (i n) -> p i n", i=TT)
        assert TB_NSA + 4096 <= TB_W
        at[0] = TB_W
        H = view(take(4096), 4096).rearrange("p (i n) -> p i n", i=TT)
        Y = view(take(4096), 4096).rearrange("p (i n) -> p i n", i=TT)
        GB = view(take(2048), 2048).rearrange("p (a n) -> p a n", a=2)
        diag = view(take(512), 512).rearrange("p (t n) -> p t n", t=TT)
        squares = view(take(2048), 2048).rearrange("p (a n) -> p a n", a=4)
        relu = view(take(1024), 1024).rearrange("p (a n) -> p a n", a=2)
        usq = view(take(1024), 1024).rearrange("p (a n) -> p a n", a=2)
        Gsig = view(take(2048), 2048).rearrange("p (a n) -> p a n", a=4)

        masks = sb("masks", [P, len(LEVELS), P], i32)
        ident_s = sb("ident_s", [P, P], fp32)
        gpre_s = sb("gpre_s", [P, KT], fp32)
        gvec_s = sb("gvec_s", [P, 2, KT], fp32)
        pos_s = sb("pos_s", [P, 2, 16], fp32)
        st = sb("st", [P, 64], fp32)

        ident = ident_s[:, :]
        ss_a, bias_a, rs_y, rs_h, ss_h = (st[:, o:o + 8] for o in (0, 8, 16, 24, 48))
        eps, warm = st[:, 56:57], st[:, 57:58]
        ntab = tab[:, TB_NSA:TB_NSA + NH * SEQ].rearrange("p (h n) -> p h n", h=NH)
        d0tab = tab[:, TB_D0:TB_D0 + 2 * D0W].rearrange("p (h n) -> p h n", h=2)
        d12tab = tab[:, TB_D12:TB_D12 + 512].rearrange("p (h n) -> p h n", h=2)
        ctb = tab[:, TB_CMP:TB_CMP + 768].rearrange("p (k n) -> p k n", k=NKV)
        rst = tab[:, TB_RST:TB_RST + SEQ]

        mneg = small[:, 0:64]
        den = small[:, 64:128]
        rden = small[:, 128:192]
        cst = small[:, 192:216]
        csum = small[:, 216:240]
        hgs = small[:, 240:256]
        blk = small[:, 256:272]
        boff = small[:, 272:320]

        raw_in = [sem("raw_in0"), sem("raw_in1")]
        x_in = [sem(f"x_in{k}") for k in range(4)]
        mask_in = sem("mask_in")
        eye_in = sem("eye_in")
        tab_in = sem("tab_in")
        small_in = sem("small_in")
        gain_in = sem("gain_in")
        cmp_in = sem("cmp_in")
        res_in = sem("res_in")
        out_sent = sem("out_sent")
        hi_done = sem("hi_done")
        lo_done = sem("lo_done")
        half_done = sem("half_done")
        act_seq = sem("act_seq")
        dve_seq = sem("dve_seq")
        x_sq = sem("x_sq")
        x_rms = sem("x_rms")
        x_diag = sem("x_diag")
        x_turned = sem("x_turned")
        w_hi = sem("w_hi")
        w_lo = sem("w_lo")
        hn_hi = sem("hn_hi")
        hn_lo = sem("hn_lo")
        job_done = sem("job_done")
        job_evac = sem("job_evac")
        kd_done = sem("kd_done")
        ct_done = sem("ct_done")
        ct_hi = sem("ct_hi")
        ct_lo = sem("ct_lo")
        dec_in = sem("dec_in")
        dec_act = sem("dec_act")
        hg_k = sem("hg_k")
        off_seq = sem("off_seq")
        off_done = sem("off_done")
        arg_done = sem("arg_done")
        dec_done = sem("dec_done")
        qk_done = sem("qk_done")
        hg_mm = sem("hg_mm")
        hg_ev = sem("hg_ev")
        hgo_mm = sem("hgo_mm")
        hgo_ev = sem("hgo_ev")
        oh_done = sem("oh_done")
        mixT_mm = sem("mixT_mm")
        mix_hi = sem("mix_hi")
        mix_lo = sem("mix_lo")
        gate_sig = sem("gate_sig")
        silu_done = sem("silu_done")
        ch_done = sem("ch_done")
        chT_mm = sem("chT_mm")
        chT_ev = sem("chT_ev")
        c2_mm = sem("c2_mm")
        c2_ev = sem("c2_ev")
        cs_mm = sem("cs_mm")
        cs_ev = sem("cs_ev")
        cs_exp = sem("cs_exp")
        cs_p = sem("cs_p")
        ct_mm = sem("ct_mm")
        ct_ev = sem("ct_ev")
        s_mm = sem("s_mm")
        s_ev = sem("s_ev")
        p_exp = sem("p_exp")
        p_done = sem("p_done")
        t_mm = sem("t_mm")
        t_ev = sem("t_ev")
        pv_done = sem("pv_done")
        ds_mm = sem("ds_mm")
        ds_ev = sem("ds_ev")
        dp_exp = sem("dp_exp")
        dp_done = sem("dp_done")
        dt_mm = sem("dt_mm")
        dt_ev = sem("dt_ev")
        dpv_done = sem("dpv_done")
        y_mm = sem("y_mm")
        y_ev = sem("y_ev")
        eps_set = sem("eps_set")
        y_sq = sem("y_sq")
        y_first = sem("y_first")
        y_gain = sem("y_gain")
        y_rms = sem("y_rms")
        h_done = sem("h_done")
        h_sq = sem("h_sq")
        h_rms = sem("h_rms")
        h_rs = sem("h_rs")
        diag_done = sem("diag_done")
        h_turned = sem("h_turned")
        x_hi = sem("x_hi")
        x_lo = sem("x_lo")
        up_mm = sem("up_mm")
        up_relu = sem("up_relu")
        up_sq = sem("up_sq")
        up_hi = sem("up_hi")
        up_lo = sem("up_lo")
        dn_mm = sem("dn_mm")
        dn_ev = sem("dn_ev")
        z_done = sem("z_done")
        gt_mm = sem("gt_mm")
        gt_sig = sem("gt_sig")
        o_done = sem("o_done")

        jobs = []

        def t_job(g, c, dst, scale=1.0):
            jobs.append((g, "T", c, P, None, dst, scale))

        def b_job(g, w, t, parts):
            jobs.append((g, "B", 0, w, t, parts, 1.0))

        for j in range(2):
            t_job(0, j * P, HF[:, j, :])
        for j in range(2):
            t_job(1, j * P, HQ[:, j, :])
        for b in range(2):
            t_job(2, b * P, KCV[:, b, :])
        for t in range(TT):
            b_job(4, 512, t, [(0, 256, HI[:, t, :]), (256, 256, V[:, VS:VW + 1, t, :])])
        jobs.append((6, "H", 0, 0, None, CHN[0:2 * NC, 0, :], 1.0))
        for t in range(TT):
            b_job(8, 402, t, [(0, 256, HG[:, t, :]), (256, P, V[:, DV0, t, :]), (384, 18, gates[:, 18 * t:18 * t + 18])])
        jobs.append((10, "H", 0, 1, None, CHN[0:2 * NC, 1, :], 1.0))
        for j in range(2):
            t_job(11, j * P, T[:, Q0 + j, :], -HD ** -0.5)
        t_job(12, 0, T[:, Q0 + 2, :], -HD ** -0.5)
        t_job(12, P, T[:, KS, :])
        t_job(13, 0, T[:, KW, :])
        dv = [V[:, DV0 + g].rearrange("p j e -> p (j e)") for g in (1, 2)]
        t_job(13, P, dv[0])
        t_job(14, 0, dv[1])
        for g in range(2):
            jobs.append((15, "X", 0, P, g, V[:, DV0 + 1 + g], 1.0))
        for j in range(2):
            t_job(15, j * P, T[:, DQ0 + j, :], -HD ** -0.5)
        t_job(16, 0, T[:, DQ0 + 2, :], -HD ** -0.5)
        t_job(16, P, T[:, DK0, :])
        for j in range(2):
            t_job(17, j * P, T[:, DK0 + 1 + j, :])
        panel_jobs = {g: [n for n, j in enumerate(jobs) if j[0] == g] for g in range(N_IN)}
        jobs_by = [sum(1 for j in jobs if j[0] <= g) for g in range(N_IN)]

        LEVEL_AT = {0: 4, 1: 5, 2: 7, 3: 8, 4: 10, 5: 11, 6: 12, 7: 13, 8: 14, 9: 15}
        steps = [("norm0",), ("scale0",), ("split", 1)]
        for g in range(N_IN):
            steps.append(("gemm", g))
            here = [lev for lev in LEVEL_AT if LEVEL_AT[lev] == g]
            if g == 11:
                steps.append(("cmp_turn_hidden",))
            if g == 12:
                steps.append(("cmp_mlp",))
            if here:
                steps.append(("level_mm", here[0]))
            if g == 10:
                steps.append(("gates",))
            if g == 15:
                steps.append(("hg_values",))
            if g == 16:
                steps.append(("cmp_scores",))
            if g == 3:
                steps.append(("cmp_im2col",))
            if g + 2 < G_PLE:
                steps.append(("split", g + 2))
            if g == 1:
                steps.append(("decay",))
            if g == 15:
                steps.append(("hg_norm",))
            if g == 2:
                steps.append(("level_start",))
            if here and 0 < here[0] < 9:
                steps.append(("level", here[0] + 1))
        steps += [("hg_mix",), ("cmp_turn",), ("nsa",), ("dil",)]
        PAIRS = (3, 5, 7, 9)

        def last_use(g):
            if g in PAIRS:
                return half_done, PAIRS.index(g) + 1
            if g < N_IN:
                return job_done, jobs_by[g]
            if g < G_OUT:
                return y_mm, 8
            if g < G_MLP:
                c = g - G_OUT
                return (half_done, 5 + c // 2) if c % 2 == 0 else (y_mm, 8 + 2 * c + 2)
            if g < G_GATE:
                q = g - G_MLP
                e, c = q // 4, q % 4
                return (up_mm, 4 * e + 2 * c + 2) if c < 2 else (dn_mm, 8 * e + 4 * (c - 2) + 4)
            c = g - G_GATE
            return (half_done, 7 + c // 2) if c % 2 == 0 else (gt_mm, 2 * c + 2)

        NLEV = 10

        HGB = (4, 5, 6, 7)
        rows = [(h, b, i) for h in range(NH) for b in range(2) for i in range(TT)]
        ROWB, TRB, OB = (0, 1, 2), (3, 4, 5), (6, 7)
        drows = [(r, hh) for r in range(DIL) for hh in range(2)]

        block = ctx.enter_context(nc.Block())

        @block.sync
        def _(sp):
            def load_panel(g):
                if g >= 2:
                    sp.wait_ge(lo_done, g - 1)
                sp.dma_start(raw[:, g % 2, :], wst[g]).then_inc(raw_in[g % 2], 16)

            for t in range(TT):
                sp.dma_start(XN[:, t, :], xn[t * P:(t + 1) * P, :]).then_inc(x_in[t], 16)
                if t == 0:
                    sp.dma_start(ident, eye).then_inc(eye_in, 16)
            load_panel(0)
            load_panel(1)
            sp.dma_start(masks[:, :, :], lmask).then_inc(mask_in, 16)
            for g in range(2, G_OUT + 4):
                load_panel(g)
                if g == 5:
                    sp.wait_ge(kd_done, 1)
                    for b in range(2):
                        for par in range(2):
                            for k in range(NKV):
                                sp.dma_start(CA[par * HD:(par + 1) * HD, b, k, :],
                                             KD[k * HD:(k + 1) * HD, b, par, :]).then_inc(cmp_in, 16)
            sp.wait_ge(dpv_done, len(drows))
            sp.wait_ge(mix_lo, KT)
            sp.dma_start(H, xn.rearrange("(i p) n -> p i n", p=P)).then_inc(res_in, 16)
            for a in range(2):
                sp.dma_start(GB[:, a, :], gpost[a:a + 1, :].partition_broadcast(P)).then_inc(res_in, 16)
            for g in range(G_OUT + 4, G_MLP + 2):
                load_panel(g)
            with sp.Fori(0, EIGHTHS // 2) as i:
                for c in range(8):
                    sp.wait_ge(lo_done, G_MLP + 2 + c - 1 + i * 8)
                    sp.dma_start(raw[:, (G_MLP + c) % 2, :],
                                 wst[bass.ds(G_MLP + 2 + c + i * 8, 1), :, :].rearrange("o p n -> (o p) n")
                                 ).then_inc(raw_in[(G_MLP + c) % 2], 16)
            for g in range(G_GATE + 2, N_PANELS):
                load_panel(g)
            for n in range(8):
                sp.wait_ge(o_done, n + 1)
                t, nh = n % TT, n // TT
                sp.dma_start(out[t * P:(t + 1) * P, nh * 512:(nh + 1) * 512],
                             H[:, t, nh * 512:(nh + 1) * 512]).then_inc(out_sent, 16)
            sp.wait_ge(out_sent, 128)

        @block.gpsimd
        def _(pool):
            nc.gpsimd.memset(eps, EPS).then_inc(eps_set, 1)
            pool.dma_start(gvec_s[:, :, :], gvec).then_inc(small_in, 16)
            pool.dma_start(pos_s[:, :, :], pos).then_inc(small_in, 16)
            pool.dma_start(w2s, w2).then_inc(small_in, 16)
            pool.wait_ge(raw_in[0], 16)
            pool.dma_start(tab, ctab).then_inc(tab_in, 16)
            for u in (Uhi, Ulo):
                nc.gpsimd.memset(u[:, 3, 448:512].bitcast(fp32), 0.0).then_inc(z_done, 1)
            nc.gpsimd.memset(kcT, 0.0).then_inc(z_done, 1)
            nc.gpsimd.memset(vcR, 0.0).then_inc(z_done, 1)
            pool.wait_ge(job_evac, jobs_by[2])
            nc.gpsimd.tensor_copy(KD, KCV.rearrange("p b (u a) -> p b a u", a=2)).then_inc(kd_done, 1)
            pool.wait_ge(hg_k, 1)
            nc.gpsimd.memset(boff, 0.0).then_inc(off_seq, 1)
            done = 1
            bl = blk.rearrange("p (j c) -> p j c", j=2)
            for m, half in enumerate((1, 2, 4)):
                bo = boff[:, m * 16:(m + 1) * 16].rearrange("p (j c) -> p j c", j=2)
                for c0 in range(0, 8, 2 * half):
                    todo = [(c, bl[:, :, c], None if c == c0 + half - 1 else bo[:, :, c + 1])
                            for c in range(c0 + half - 1, c0 - 1, -1)]
                    todo += [(c, bl[:, :, c - 1], bo[:, :, c - 1]) for c in range(c0 + half + 1, c0 + 2 * half)]
                    for c, own, before in todo:
                        pool.wait_ge(off_seq, done)
                        if before is None:
                            nc.gpsimd.tensor_copy(bo[:, :, c], own).then_inc(off_seq, 1)
                        else:
                            nc.gpsimd.tensor_tensor(bo[:, :, c], own, before, ALU.add).then_inc(off_seq, 1)
                        done += 1
            pool.wait_ge(off_seq, done)
            nc.gpsimd.memset(warm, 0.0).then_inc(off_done, 1)
            pool.wait_ge(hi_done, G_PLE + 1)
            nc.gpsimd.tensor_tensor(Wlo[:, G_PLE % 2, :], raw[:, G_PLE % 2, :], Whi[:, G_PLE % 2, :].bitcast(fp32),
                                    ALU.subtract).then_inc(lo_done, 1)
            pool.wait_ge(h_done, TT)
            nc.gpsimd.memset(Y, 0.0).then_inc(dn_ev, 1)
            pool.wait_ge(hi_done, G_GATE + 1)
            pool.wait_ge(raw_in[G_GATE % 2], 16 * (G_GATE // 2 + 1))
            nc.gpsimd.tensor_tensor(Wlo[:, G_GATE % 2, :], raw[:, G_GATE % 2, :], Whi[:, G_GATE % 2, :].bitcast(fp32),
                                    ALU.subtract).then_inc(lo_done, 1)

        @block.scalar
        def _(act):
            seq = [0]

            def link(ins):
                seq[0] += 1
                ins.then_inc(act_seq, 1)
                act.wait_ge(act_seq, seq[0])

            def hi(g, count=None):
                act.wait_ge(raw_in[g % 2], 16 * (g // 2 + 1) if count is None else count)
                if count is None and g >= 2:
                    act.wait_ge(*last_use(g - 2))
                nc.scalar.activation(Whi[:, g % 2, :], raw[:, g % 2, :], ACT.Copy).then_inc(hi_done, 1)

            for step in steps:
                if step[0] == "norm0":
                    act.dma_start(gpre_s[:, :], gpre).then_inc(gain_in, 16)
                    act.wait_ge(eps_set, 1)
                    nc.scalar.activation(warm, eps, ACT.Sqrt)
                    for t in range(TT):
                        act.wait_ge(x_in[t], 16)
                        if t >= 2:
                            act.wait_ge(x_sq, t - 1)
                        nc.scalar.activation(sqs[:, t % 2, :], XN[:, t, :], ACT.Square,
                                             accum_out=ss_h[:, t:t + 1]).then_inc(x_sq, 1)
                        act.wait_ge(x_sq, t + 1)
                        nc.scalar.activation(rs_h[:, t:t + 1], ss_h[:, t:t + 1], ACT.Sqrt, scale=1.0 / DM,
                                             bias=eps).then_inc(x_rms, 1)
                elif step[0] == "scale0":
                    act.wait_ge(gain_in, 16)
                    act.wait_ge(raw_in[0], 16)
                    for m in range(2):
                        nc.scalar.activation(Whi[:, 0, m * 1024:(m + 1) * 1024], raw[:, 0, m * 1024:(m + 1) * 1024],
                                             ACT.Copy).then_inc((w_hi, hi_done)[m], 1)
                        for k in range(4 * m, 4 * m + 4):
                            act.wait_ge(x_turned, k + 1)
                            nc.scalar.activation(Xhi[:, k, :], PB[k][:, :], ACT.Copy,
                                                 scale=gpre_s[:, k:k + 1]).then_inc(hn_hi, 1)
                elif step[0] == "split":
                    hi(step[1])
                elif step[0] == "gemm":
                    for n in panel_jobs[step[1]]:
                        _, kind, _, w, tiles, dst, scale = jobs[n]
                        act.wait_ge(job_done, n + 1)
                        if step[1] == 15 and kind == "T":
                            act.wait_ge(hgo_mm, 2)
                        src = PB[n % 4][:, :]
                        if kind == "B":
                            for a, (c, cw, part) in enumerate(dst):
                                piece = src[:, c:c + cw]
                                if cw == 256 and c:
                                    piece = piece.rearrange("p (v e) -> p v e", v=2)
                                ins = nc.scalar.activation(part, piece, ACT.Copy)
                            ins.then_inc(job_evac, 1)
                            continue
                        if kind == "H":
                            src = src[0:2 * NC, 0:256]
                        elif kind == "X":
                            src = src.rearrange("p (r e) -> p r e", e=P)
                        nc.scalar.activation(dst, src, ACT.Copy, scale=scale).then_inc(job_evac, 1)
                elif step[0] == "decay":
                    act.wait_ge(dec_in, 1)
                    nc.scalar.activation(tB, tA, ACT.Exp, scale=-1.0).then_inc(dec_act, 1)
                    act.wait_ge(dec_in, 2)
                    link(nc.scalar.activation(tA, tA, ACT.Exp))
                    nc.scalar.activation(tA, tA, ACT.Ln, bias=1.0).then_inc(dec_act, 1)
                    act.wait_ge(dec_act, 1)
                    nc.scalar.activation(tD, tB, ACT.Ln, bias=1.0).then_inc(dec_act, 1)
                    act.wait_ge(dec_in, 3)
                    hf = HF.rearrange("p j t -> p (j t)")
                    nc.scalar.activation(hf, hf, ACT.Sigmoid, scale=-1.0).then_inc(dec_act, 1)
                elif step[0] == "level_start":
                    act.wait_ge(arg_done, 1)
                    nc.scalar.activation(tA, tA, ACT.Exp).then_inc(dec_done, 1)
                elif step[0] == "level":
                    act.wait_ge(arg_done, step[1])
                    nc.scalar.activation(tA, tA, ACT.Exp).then_inc(dec_done, 1)
                elif step[0] == "cmp_im2col":
                    act.wait_ge(ct_done, 1)
                    nc.scalar.activation(Uhi[:, :, :].rearrange("p a t -> p (a t)")[:, 0:1984],
                                         view(aC, 1984), ACT.Copy).then_inc(ct_hi, 1)
                elif step[0] == "gates":
                    act.wait_ge(job_evac, jobs_by[10])
                    nc.scalar.activation(CHS[0:2 * NC, :], CHN[0:2 * NC, :, :].rearrange("p b j -> p (b j)"),
                                         ACT.Sigmoid).then_inc(gate_sig, 1)
                    nc.scalar.activation(gates, gates, ACT.Sigmoid).then_inc(gate_sig, 1)
                    nc.scalar.activation(GS, HG.rearrange("p i c -> p (i c)"), ACT.Sigmoid).then_inc(gate_sig, 1)
                elif step[0] == "cmp_turn_hidden":
                    act.wait_ge(chT_mm, 1)
                    nc.scalar.activation(view(CHa, 248), PB[7][:, 0:248], ACT.Copy).then_inc(chT_ev, 1)
                elif step[0] == "hg_values":
                    for a in range(2):
                        act.wait_ge(hgo_mm, a + 1)
                        nc.scalar.activation(tA[:, a * 512:(a + 1) * 512], PB[HGB[a]][:, :], ACT.Copy).then_inc(hgo_ev, 1)
                elif step[0] == "hg_norm":
                    act.wait_ge(dec_in, 4)
                    nc.scalar.activation(hgs, hgs, ACT.Sqrt).then_inc(dec_act, 1)
                elif step[0] == "hg_mix":
                    for j in range(2):
                        act.wait_ge(mixT_mm, j + 1)
                        nc.scalar.activation(Xhi[:, 6 + j, :], PB[HGB[2 + j]][:, :], ACT.Copy).then_inc(mix_hi, 1)
                elif step[0] == "cmp_scores":
                    act.wait_ge(cs_ev, 1)
                    nc.scalar.activation(PC, PC, ACT.Exp, scale=-1.0).then_inc(cs_exp, 1)
                elif step[0] == "cmp_turn":
                    for k in range(NKV):
                        act.wait_ge(ct_mm, k + 1)
                        nc.scalar.activation(PCT[0:96, k, :], PB[4 + k][0:96, :], ACT.Copy).then_inc(ct_ev, 1)
                elif step[0] == "nsa":
                    def t_copy(n):
                        h, b, i = rows[n]
                        act.wait_ge(t_mm, n + 1)
                        if i == 0 and b == 0 and h >= 2:
                            act.wait_ge(pv_done, h - 1)
                        nc.scalar.activation(PT[:, h % 2, b, 0:i + 1, i * P:(i + 1) * P],
                                             PB[TRB[n % 3]][:, 0:(i + 1) * P].rearrange("p (j t) -> p j t", t=P),
                                             ACT.Copy).then_inc(t_ev, 1)

                    def mix_evac(j):
                        act.wait_ge(pv_done, 2 * j + 2)
                        nc.scalar.activation(Xhi[:, j, :], PB[OB[j % 2]][:, :], ACT.Copy).then_inc(mix_hi, 1)

                    for n in range(len(rows) + 3):
                        if n < len(rows):
                            w = (rows[n][2] + 1) * P
                            act.wait_ge(s_ev, n + 1)
                            nc.scalar.activation(SR[:, n % 4, 0:w], SR[:, n % 4, 0:w], ACT.Exp,
                                                 bias=mneg[:, n:n + 1], scale=-1.0,
                                                 accum_out=den[:, n:n + 1]).then_inc(p_exp, 1)
                        if 3 <= n < len(rows) + 3:
                            t_copy(n - 3)
                        if n == 24:
                            act.wait_ge(raw_in[G_PLE % 2], 16 * (G_PLE // 2 + 1))
                            act.wait_ge(*last_use(G_PLE - 2))
                        if 24 <= n < 28:
                            q = slice((n - 24) * 512, (n - 23) * 512)
                            ins = nc.scalar.activation(Whi[:, G_PLE % 2, q], raw[:, G_PLE % 2, q], ACT.Copy)
                            if n == 27:
                                ins.then_inc(hi_done, 1)
                        if n >= 27 and (n - 27) % 16 == 0:
                            mix_evac((n - 27) // 16)
                elif step[0] == "dil":
                    def dt_copy(n):
                        if n >= 2:
                            act.wait_ge(dpv_done, n - 1)
                        act.wait_ge(dt_mm, n + 1)
                        nc.scalar.activation(DPT[:, n % 2, 0:4, :], PB[3][:, :].rearrange("p (j t) -> p j t", t=P),
                                             ACT.Copy).then_inc(dt_ev, 1)
                        nc.scalar.activation(DPT[:, n % 2, 4:6, :], PB[4][:, 0:256].rearrange("p (j t) -> p j t", t=P),
                                             ACT.Copy).then_inc(dt_ev, 1)

                    for n in range(len(drows) + 2):
                        if n < len(drows):
                            act.wait_ge(ds_ev, n + 1)
                            nc.scalar.activation(DSR[:, n % 3, :], DSR[:, n % 3, :], ACT.Exp,
                                                 bias=mneg[:, 48 + n:49 + n], scale=-1.0,
                                                 accum_out=den[:, 48 + n:49 + n]).then_inc(dp_exp, 1)
                        if n == 1:
                            mix_evac(2)
                        if n >= 2:
                            dt_copy(n - 2)
                        if n >= len(drows):
                            hi(G_OUT + n - len(drows))
                    act.wait_ge(dpv_done, len(drows))
                    for g in range(3):
                        nc.scalar.activation(Xhi[:, 3 + g, :].rearrange("p (i r) -> p i r", r=DIL),
                                             PB[5 + g][:, :].rearrange("p (r i) -> p i r", r=DIL),
                                             ACT.Copy).then_inc(mix_hi, 1)

            def y_half(a, nh, t):
                if a == 0:
                    act.wait_ge(y_mm, 8 + 4 * nh + t + 1)
                    return PB[4 * nh + t][:, :]
                act.wait_ge(dn_ev, 1 + 8 * (EIGHTHS - 1) + 4 * nh + t + 1)
                return Y[:, t, nh * 512:(nh + 1) * 512]

            def first_halves(a):
                for t in range(TT):
                    src = y_half(a, 0, t)
                    if a:
                        act.wait_ge(y_sq, 4 + t + 1)
                    nc.scalar.activation(squares[:, t % 2, :], src, ACT.Square,
                                         accum_out=ss_a[:, 4 * a + t:4 * a + t + 1]).then_inc(y_sq, 1)
                    act.wait_ge(y_sq, 8 * a + t + 1)

            def post_norm(a):
                for s in range(TT + 1):
                    if s < TT:
                        k = TT * a + s
                        src = y_half(a, 1, s)
                        nc.scalar.activation(squares[:, s % 2, :], src, ACT.Square,
                                             accum_out=rs_y[:, k:k + 1]).then_inc(y_sq, 1)
                        act.wait_ge(y_sq, 8 * a + 4 + s + 1)
                        act.wait_ge(y_first, a + 1)
                        nc.scalar.activation(rs_y[:, k:k + 1], rs_y[:, k:k + 1], ACT.Sqrt, scale=1.0 / DM,
                                             bias=bias_a[:, k:k + 1]).then_inc(y_rms, 1)
                    if s >= 1:
                        k = TT * a + s - 1
                        act.wait_ge(h_done, k + 1)
                        nc.scalar.activation(squares[:, 2:4, :].rearrange("p a n -> p (a n)"), H[:, s - 1, :], ACT.Square,
                                             accum_out=ss_h[:, k:k + 1]).then_inc(h_sq, 1)
                        act.wait_ge(h_sq, k + 1)
                        act.wait_ge(eps_set, 1)
                        nc.scalar.activation(rs_h[:, k:k + 1], ss_h[:, k:k + 1], ACT.Sqrt, scale=1.0 / DM,
                                             bias=eps).then_inc(h_rms, 1)
                for k in range(KT):
                    act.wait_ge(h_turned, KT * a + k + 1)
                    nc.scalar.activation(Xhi[:, k, :], PB[k][:, :], ACT.Copy,
                                         scale=gvec_s[:, a, k:k + 1]).then_inc(x_hi, 1)

            nc.scalar.activation(st[:, 58:59], eps, ACT.Sqrt)
            for g in range(G_OUT + 2, G_OUT + 4):
                hi(g)
            first_halves(0)
            hi(G_MLP)
            post_norm(0)
            hi(G_MLP + 1)

            def mlp_turn(i, last):
                for e in range(2):
                    for c in range(4):
                        if c < 2:
                            for f in range(2 * c, 2 * c + 2):
                                u = 4 * e + f
                                act.wait_ge(up_mm, i * 8 + u + 1)
                                bank = PB[(0 if e == 0 else 4) + f]
                                nc.scalar.activation(relu[:, f % 2, :], bank[:, :], ACT.Relu).then_inc(up_relu, 1)
                                act.wait_ge(up_sq, i * 8 + u + 1)
                                nc.scalar.activation(Uhi[:, f, :], usq[:, f % 2, :], ACT.Copy).then_inc(up_hi, 1)
                        if last and e == 1 and c >= 2:
                            continue
                        g = G_MLP + 2 + 4 * e + c
                        if c < 2:
                            act.wait_ge(up_mm, i * 8 + 4 * e + 2 * c + 2)
                        else:
                            act.wait_ge(dn_mm, i * 16 + 8 * e + 4 * (c - 2) + 4)
                        hi(g, i * 64 + 16 * (g // 2 + 1))

            with act.Fori(0, EIGHTHS // 2 - 1) as i:
                mlp_turn(i, False)
            mlp_turn(EIGHTHS // 2 - 1, True)
            first_halves(1)
            hi(G_GATE)
            post_norm(1)
            hi(G_GATE + 1)
            for g in range(G_GATE + 2, N_PANELS):
                hi(g)
            act.wait_ge(h_rs, 2 * TT)
            for n in range(8):
                act.wait_ge(gt_mm, n + 1)
                if n >= 4:
                    act.wait_ge(o_done, n - 3)
                nc.scalar.activation(Gsig[:, n % 4, :], PB[n][:, :], ACT.Sigmoid,
                                     scale=rs_h[:, TT + n % TT:TT + n % TT + 1]).then_inc(gt_sig, 1)

        @block.vector
        def _(dve):
            seq = [0]

            def link(ins):
                seq[0] += 1
                ins.then_inc(dve_seq, 1)
                dve.wait_ge(dve_seq, seq[0])

            def lo(g, count=None):
                dve.wait_ge(hi_done, g + 1 if count is None else count)
                nc.vector.tensor_tensor(Wlo[:, g % 2, :], raw[:, g % 2, :], Whi[:, g % 2, :].bitcast(fp32),
                                        ALU.subtract).then_inc(lo_done, 1)

            V2 = nc.vector

            def level_args(lev):
                dve.wait_ge(hg_k, 1)
                if lev > 1:
                    dve.wait_ge(qk_done, lev - 1)
                if lev <= 6:
                    L = LEVELS[lev - 1]
                    tb = tB.rearrange("p (n a u) -> p n a u", a=2, u=L // 2)
                    ta = tA.rearrange("p (n a u) -> p n a u", a=2, u=L // 2)
                    mid = tb[:, :, 0, L // 2 - 1:L // 2].broadcast_to([P, 1024 // L, L // 2])
                    V2.tensor_tensor(ta[:, :, 1, :], tb[:, :, 1, :], mid, ALU.subtract).then_inc(dve_seq, 1)
                    V2.tensor_tensor(ta[:, :, 0, :], mid, tb[:, :, 0, :], ALU.subtract).then_inc(arg_done, 1)
                    seq[0] += 1
                else:
                    half = {7: 1, 8: 2, 9: 4}[lev]
                    dve.wait_ge(off_done, 1)
                    tb = tB.rearrange("p (n a h u) -> p n a h u", a=2, h=half, u=HGC)
                    ta = tA.rearrange("p (n a h u) -> p n a h u", a=2, h=half, u=HGC)
                    ov = boff[:, (lev - 7) * 16:(lev - 6) * 16].rearrange("p (n a h) -> p n a h", a=2, h=half)
                    wide = [P, 8 // half, half, HGC]
                    V2.tensor_tensor(ta[:, :, 1], tb[:, :, 1], ov[:, :, 1, :].unsqueeze(3).broadcast_to(wide),
                                     ALU.add).then_inc(dve_seq, 1)
                    V2.tensor_tensor(ta[:, :, 0], ov[:, :, 0, :].unsqueeze(3).broadcast_to(wide), tb[:, :, 0],
                                     ALU.subtract).then_inc(arg_done, 1)
                    seq[0] += 1

            def level_products(lev):
                dve.wait_ge(dec_done, lev)
                if lev > 1:
                    dve.wait_ge(hg_mm, 4 * lev)
                link(V2.tensor_tensor(tC, HQ.rearrange("p j t -> p (j t)"), tA, ALU.mult))
                V2.tensor_tensor(tD, HF.rearrange("p j t -> p (j t)"), tA, ALU.mult).then_inc(qk_done, 1)

            for step in steps:
                if step[0] == "norm0":
                    dve.wait_ge(eye_in, 16)
                    for t in range(TT):
                        dve.wait_ge(x_rms, t + 1)
                        link(V2.reciprocal(rs_h[:, t:t + 1], rs_h[:, t:t + 1]))
                        V2.tensor_scalar(diag0[:, t, :], ident, rs_h[:, t:t + 1], None, ALU.mult).then_inc(x_diag, 1)
                elif step[0] == "scale0":
                    dve.wait_ge(gain_in, 16)
                    for m in range(2):
                        dve.wait_ge((w_hi, hi_done)[m], 1)
                        V2.tensor_tensor(Wlo[:, 0, m * 1024:(m + 1) * 1024], raw[:, 0, m * 1024:(m + 1) * 1024],
                                         Whi[:, 0, m * 1024:(m + 1) * 1024].bitcast(fp32),
                                         ALU.subtract).then_inc((w_lo, lo_done)[m], 1)
                        for k in range(4 * m, 4 * m + 4):
                            dve.wait_ge(hn_hi, k + 1)
                            V2.scalar_tensor_tensor(out=Xlo[:, k, :], in0=PB[k][:, :], scalar=gpre_s[:, k:k + 1],
                                                    in1=Xhi[:, k, :].bitcast(fp32), op0=ALU.mult,
                                                    op1=ALU.subtract).then_inc(hn_lo, 1)
                elif step[0] == "split":
                    lo(step[1])
                elif step[0] == "decay":
                    hf = HF.rearrange("p j t -> p (j t)")
                    dve.wait_ge(job_evac, jobs_by[0])
                    V2.tensor_scalar(tA, hf, X_SPLIT, None, ALU.max).then_inc(dec_in, 1)
                    dve.wait_ge(dec_act, 1)
                    V2.tensor_scalar(tA, hf, X_SPLIT, -LOG_TINY, ALU.min, ALU.add).then_inc(dec_in, 1)
                    V2.tensor_scalar(tC, hf, X_SPLIT, None, ALU.is_lt).then_inc(dec_in, 1)
                    dve.wait_ge(dec_in, 3)
                    dve.wait_ge(dec_act, 2)
                    link(V2.scalar_tensor_tensor(out=tA, in0=tA, scalar=LOG_TINY - X_SPLIT, in1=tC,
                                                 op0=ALU.add, op1=ALU.mult))
                    dve.wait_ge(dec_act, 3)
                    link(V2.tensor_tensor(tA, tA, tD, ALU.subtract))
                    dve.wait_ge(mask_in, 16)
                    dve.wait_ge(tab_in, 16)
                    for j in range(2):
                        link(V2.tensor_tensor_scan(tB[:, j * SEQ:(j + 1) * SEQ], rst, tA[:, j * SEQ:(j + 1) * SEQ],
                                                   0.0, ALU.mult, ALU.add))
                    dve.wait_ge(dec_act, 4)
                    V2.tensor_copy(blk, tB.rearrange("p (c u) -> p c u", u=HGC)[:, :, HGC - 1]).then_inc(hg_k, 1)
                elif step[0] == "level_start":
                    level_args(1)
                    dve.wait_ge(job_evac, jobs_by[1])
                    level_products(1)
                    level_args(2)
                elif step[0] == "level":
                    level_products(step[1])
                    if step[1] < 9:
                        level_args(step[1] + 1)
                elif step[0] == "level_mm":
                    lev = step[1]
                    for h in range(HGH):
                        n = 4 * lev + h
                        dve.wait_ge(hg_mm, n + 1)
                        pb = PB[HGB[h]][:, :]
                        pb3 = pb.rearrange("p (i t) -> p i t", t=P)
                        if lev == 0:
                            V2.tensor_tensor(AD[:, h], pb3, ident.unsqueeze(1).broadcast_to([P, TT, P]),
                                             ALU.mult).then_inc(hg_ev, 1)
                        elif lev <= 7:
                            dve.wait_ge(hg_ev, 4 * (lev - 1) + h + 1)
                            V2.copy_predicated(AD[:, h], masks[:, lev - 1, :].unsqueeze(1).broadcast_to([P, TT, P]),
                                               pb3).then_inc(hg_ev, 1)
                        elif lev == 8:
                            V2.tensor_copy(AO[:, h, 0:2, :], pb3[:, 0:2, :]).then_inc(hg_ev, 1)
                        else:
                            V2.tensor_copy(AO[:, h, 2:6, :], pb3).then_inc(hg_ev, 1)
                elif step[0] == "cmp_im2col":
                    dve.wait_ge(cmp_in, 8 * 16)
                    last = None
                    for b in range(2):
                        for k in range(NKV):
                            for mh in range(2):
                                src = CA[:, b, k, :].rearrange("p (n m) -> p m n", m=8)[:, :, mh:mh + NC]
                                bias = pos_s[:, b, 8 * mh:8 * mh + 8].unsqueeze(2).broadcast_to([P, 8, NC])
                                ins = V2.tensor_tensor(CT[:, b, 8 * mh:8 * mh + 8, k, :], src, bias, ALU.add)
                                if b == 1 and k == 1 and mh == 1:
                                    ins.then_inc(ct_done, 1)
                    dve.wait_ge(ct_hi, 1)
                    dve.wait_ge(ct_done, 1)
                    V2.tensor_tensor(Ulo[:, :, :].rearrange("p a t -> p (a t)")[:, 0:1984], view(aC, 1984),
                                     Uhi[:, :, :].rearrange("p a t -> p (a t)")[:, 0:1984].bitcast(fp32),
                                     ALU.subtract).then_inc(ct_lo, 1)
                elif step[0] == "gates":
                    chn, hg = CHN[0:2 * NC, :, :].rearrange("p b j -> p (b j)"), HG.rearrange("p i c -> p (i c)")
                    dve.wait_ge(gate_sig, 1)
                    V2.tensor_tensor(chn, chn, CHS[0:2 * NC, :], ALU.mult).then_inc(ch_done, 1)
                    dve.wait_ge(gate_sig, 3)
                    V2.tensor_tensor(hg, hg, GS, ALU.mult).then_inc(silu_done, 1)
                elif step[0] == "cmp_mlp":
                    dve.wait_ge(z_done, 4)
                    dve.wait_ge(c2_mm, 1)
                    V2.tensor_copy(kcT[:, 0:NC], PB[6][:, 0:NC]).then_inc(c2_ev, 1)
                    for g in range(NG):
                        V2.tensor_copy(vcR[32 * g:32 * g + NC], PB[7][32 * g:32 * g + NC, 0:128]
                                       .rearrange("p (k e) -> p k e", k=NKV)).then_inc(c2_ev, 1)
                elif step[0] == "hg_norm":
                    dve.wait_ge(hgo_ev, 2)
                    link(V2.tensor_tensor(tB, tA, tA, ALU.mult))
                    link(V2.tensor_reduce(hgs, tB.rearrange("p (n e) -> p n e", e=HD), AX.X, ALU.add))
                    V2.tensor_scalar(hgs, hgs, 1.0 / HD, EPS, ALU.mult, ALU.add).then_inc(dec_in, 1)
                    dve.wait_ge(dec_act, 5)
                    link(V2.reciprocal(hgs, hgs))
                    link(V2.tensor_tensor(tA.rearrange("p (n e) -> p n e", e=HD), tA.rearrange("p (n e) -> p n e", e=HD),
                                          hgs.unsqueeze(2).broadcast_to([P, 16, HD]), ALU.mult))
                    dve.wait_ge(silu_done, 1)
                    V2.tensor_tensor(tD, tA, HG.rearrange("p i c -> p (i c)"), ALU.mult).then_inc(oh_done, 1)
                elif step[0] == "hg_mix":
                    for j in range(2):
                        dve.wait_ge(mix_hi, j + 1)
                        V2.tensor_tensor(Xlo[:, 6 + j, :], PB[HGB[2 + j]][:, :], Xhi[:, 6 + j, :].bitcast(fp32),
                                         ALU.subtract).then_inc(mix_lo, 1)
                elif step[0] == "cmp_scores":
                    dve.wait_ge(gate_sig, 3)
                    for k in range(NKV):
                        dve.wait_ge(cs_mm, k + 1)
                        link(V2.tensor_tensor(PC[:, k * 384:(k + 1) * 384], PB[4 + k][:, 0:384], ctb[:, k, :], ALU.add))
                    pc3 = PC.rearrange("p (n c) -> p n c", c=NCP)
                    link(V2.tensor_reduce(cst, pc3, AX.X, ALU.min))
                    link(V2.tensor_scalar(cst, cst, 1e25, None, ALU.min))
                    V2.tensor_tensor(pc3, pc3, cst.unsqueeze(2).broadcast_to([P, 24, NCP]), ALU.subtract).then_inc(cs_ev, 1)
                    dve.wait_ge(cs_exp, 1)
                    link(V2.tensor_reduce(csum, pc3, AX.X, ALU.add))
                    link(V2.tensor_scalar(csum, csum, 1e-30, None, ALU.max))
                    link(V2.reciprocal(csum, csum))
                    for k in range(NKV):
                        gv = gates.rearrange("p (i k g b) -> p i k g b", i=TT, k=NKV, b=3)[:, :, k, :, 0]
                        cv = csum[:, k * 12:(k + 1) * 12].rearrange("p (i g) -> p i g", g=NG)
                        link(V2.tensor_tensor(cv, cv, gv, ALU.mult))
                    V2.tensor_tensor(pc3, pc3, csum.unsqueeze(2).broadcast_to([P, 24, NCP]), ALU.mult).then_inc(cs_p, 1)
                elif step[0] == "nsa":
                    gv = gates.rearrange("p (i h b) -> p i h b", h=NH, b=3)

                    def normalise(n):
                        h, b, i = rows[n]
                        w = (i + 1) * P
                        dve.wait_ge(p_exp, n + 1)
                        link(V2.reciprocal(rden[:, n:n + 1], den[:, n:n + 1]))
                        V2.tensor_scalar(SR[:, n % 4, 0:w], SR[:, n % 4, 0:w], rden[:, n:n + 1],
                                         gv[:, i, h, 1 + b:2 + b], ALU.mult, ALU.mult).then_inc(p_done, 1)

                    def mix_lo_part(j):
                        dve.wait_ge(mix_hi, 2 + j + 1)
                        V2.tensor_tensor(Xlo[:, j, :], PB[OB[j % 2]][:, :], Xhi[:, j, :].bitcast(fp32),
                                         ALU.subtract).then_inc(mix_lo, 1)

                    for n in range(len(rows) + 3):
                        if n < len(rows):
                            h, b, i = rows[n]
                            w = (i + 1) * P
                            dve.wait_ge(s_mm, n + 1)
                            if n >= 4:
                                dve.wait_ge(t_mm, n - 3)
                            V2.tensor_tensor_reduce(out=SR[:, n % 4, 0:w], in0=ntab[:, h, SEQ - w:SEQ],
                                                    in1=PB[ROWB[n % 3]][:, 0:w], scale=1.0, scalar=3e38,
                                                    op0=ALU.add, op1=ALU.min,
                                                    accum_out=mneg[:, n:n + 1]).then_inc(s_ev, 1)
                        if 1 <= n < len(rows) + 1:
                            normalise(n - 1)
                        if n >= 27 and (n - 27) % 16 == 0:
                            mix_lo_part((n - 27) // 16)
                elif step[0] == "dil":
                    def normalise(n):
                        dve.wait_ge(dp_exp, n + 1)
                        link(V2.reciprocal(rden[:, 48 + n:49 + n], den[:, 48 + n:49 + n]))
                        V2.tensor_scalar(DSR[:, n % 3, :], DSR[:, n % 3, :], rden[:, 48 + n:49 + n], None,
                                         ALU.mult).then_inc(dp_done, 1)

                    for n in range(len(drows) + 1):
                        if n < len(drows):
                            r, hh = drows[n]
                            dve.wait_ge(ds_mm, n + 1)
                            if n >= 3:
                                dve.wait_ge(dt_mm, n - 2)
                            link(V2.tensor_tensor_reduce(out=DSR[:, n % 3, 0:SEQ], in0=d0tab[:, hh, 3 - r:3 - r + SEQ],
                                                         in1=PB[0][:, :],
                                                         scale=1.0, scalar=3e38, op0=ALU.add, op1=ALU.min,
                                                         accum_out=st[:, 32 + n:33 + n]))
                            link(V2.tensor_tensor_reduce(out=DSR[:, n % 3, SEQ:768], in0=d12tab[:, hh, :],
                                                         in1=PB[1][:, 0:256],
                                                         scale=1.0, scalar=3e38, op0=ALU.add, op1=ALU.min,
                                                         accum_out=st[:, 40 + n:41 + n]))
                            V2.tensor_tensor(mneg[:, 48 + n:49 + n], st[:, 32 + n:33 + n], st[:, 40 + n:41 + n],
                                             ALU.min).then_inc(ds_ev, 1)
                        if n >= 1:
                            normalise(n - 1)
                            if n == 1:
                                mix_lo_part(2)
                            m = n - 1
                            dve.wait_ge(y_mm, m + 1)
                            V2.tensor_copy(PR[:, m % TT, (m // TT) * 512:(m // TT + 1) * 512], PB[2][:, :]).then_inc(y_ev, 1)
                    lo(G_OUT)
                    lo(G_OUT + 1)
                    for g in range(3):
                        dve.wait_ge(mix_hi, 5 + g + 1)
                        V2.tensor_tensor(Xlo[:, 3 + g, :].rearrange("p (i r) -> p i r", r=DIL),
                                         PB[5 + g][:, :].rearrange("p (r i) -> p i r", r=DIL),
                                         Xhi[:, 3 + g, :].bitcast(fp32).rearrange("p (i r) -> p i r", r=DIL),
                                         ALU.subtract).then_inc(mix_lo, 1)

            def first_halves(a):
                if a == 0:
                    dve.wait_ge(res_in, 48)
                for t in range(TT):
                    dve.wait_ge(y_sq, 8 * a + t + 1)
                    V2.tensor_tensor(Y[:, t, 0:512], PB[t][:, :] if a == 0 else Y[:, t, 0:512], GB[:, a, 0:512],
                                     ALU.mult).then_inc(y_gain, 1)
                V2.tensor_scalar(bias_a[:, TT * a:TT * a + TT], ss_a[:, TT * a:TT * a + TT], 1.0 / DM, EPS,
                                 ALU.mult, ALU.add).then_inc(y_first, 1)

            def last_add(t):
                yv = Y[:, t, 512:1024]
                dve.wait_ge(dn_mm, 8 * EIGHTHS - 4 + t + 1)
                dve.wait_ge(dn_ev, 8 * (EIGHTHS - 1) + 1)
                V2.tensor_tensor(yv, yv, PB[4 + t][:, :], ALU.add).then_inc(dn_ev, 1)

            def post_norm(a):
                if a == 1:
                    last_add(0)
                for s in range(TT + 1):
                    if a == 1 and s + 1 < TT:
                        last_add(s + 1)
                    if s < TT:
                        k, yv = TT * a + s, Y[:, s, 512:1024]
                        dve.wait_ge(y_sq, 8 * a + 4 + s + 1)
                        V2.tensor_tensor(yv, PB[4 + s][:, :] if a == 0 else yv, GB[:, a, 512:1024],
                                         ALU.mult).then_inc(y_gain, 1)
                        dve.wait_ge(y_rms, k + 1)
                        link(V2.reciprocal(rs_y[:, k:k + 1], rs_y[:, k:k + 1]))
                        dve.wait_ge(y_gain, 8 * a + 4 + s + 1)
                        V2.scalar_tensor_tensor(out=H[:, s, :], in0=Y[:, s, :], scalar=rs_y[:, k:k + 1],
                                                in1=H[:, s, :], op0=ALU.mult, op1=ALU.add).then_inc(h_done, 1)
                    if s >= 1:
                        k = TT * a + s - 1
                        dve.wait_ge(h_rms, k + 1)
                        V2.reciprocal(rs_h[:, k:k + 1], rs_h[:, k:k + 1]).then_inc(h_rs, 1)
                        if a == 0:
                            dve.wait_ge(h_rs, k + 1)
                            V2.tensor_scalar(diag[:, s - 1, :], ident, rs_h[:, k:k + 1], None, ALU.mult).then_inc(diag_done, 1)
                for k in range(KT):
                    dve.wait_ge(x_hi, KT * a + k + 1)
                    V2.scalar_tensor_tensor(out=Xlo[:, k, :], in0=PB[k][:, :], scalar=gvec_s[:, a, k:k + 1],
                                            in1=Xhi[:, k, :].bitcast(fp32), op0=ALU.mult,
                                            op1=ALU.subtract).then_inc(x_lo, 1)

            for g in range(G_OUT + 2, G_OUT + 4):
                lo(g)
            first_halves(0)
            lo(G_MLP)
            post_norm(0)
            lo(G_MLP + 1)

            def mlp_turn(i, last):
                for e in range(2):
                    for c in range(4):
                        if c < 2:
                            for f in range(2 * c, 2 * c + 2):
                                u = 4 * e + f
                                dve.wait_ge(up_relu, i * 8 + u + 1)
                                if u:
                                    dve.wait_ge(up_lo, i * 8 + u)
                                V2.tensor_tensor(usq[:, f % 2, :], relu[:, f % 2, :], relu[:, f % 2, :],
                                                 ALU.mult).then_inc(up_sq, 1)
                                dve.wait_ge(up_hi, i * 8 + u + 1)
                                dve.wait_ge(up_sq, i * 8 + u + 1)
                                V2.tensor_tensor(Ulo[:, f, :], usq[:, f % 2, :], Uhi[:, f, :].bitcast(fp32),
                                                 ALU.subtract).then_inc(up_lo, 1)
                        elif not (last and e == 1 and c == 3):
                            nh = c - 2
                            for t in range(TT):
                                bank = PB[(4 if (nh == 0) == (e == 0) else 0) + t]
                                dve.wait_ge(dn_mm, i * 16 + 8 * e + 4 * nh + t + 1)
                                yv = Y[:, t, nh * 512:(nh + 1) * 512]
                                dve.wait_ge(dn_ev, i * 16 + 8 * e + 1)
                                V2.tensor_tensor(yv, yv, bank[:, :], ALU.add).then_inc(dn_ev, 1)
                        if last and e == 1 and c >= 2:
                            continue
                        g = G_MLP + 2 + 4 * e + c
                        lo(g, i * 8 + g + 1)
                dve.wait_ge(up_lo, i * 8 + 8)

            with dve.Fori(0, EIGHTHS // 2 - 1) as i:
                mlp_turn(i, False)
            mlp_turn(EIGHTHS // 2 - 1, True)
            first_halves(1)
            post_norm(1)
            dve.wait_ge(lo_done, G_GATE + 1)
            lo(G_GATE + 1)
            for g in range(G_GATE + 2, N_PANELS):
                lo(g)
            for n in range(8):
                t, nh = n % TT, n // TT
                dve.wait_ge(gt_sig, n + 1)
                link(V2.tensor_tensor(Gsig[:, n % 4, :], Gsig[:, n % 4, :], PR[:, t, nh * 512:(nh + 1) * 512], ALU.mult))
                hv = H[:, t, nh * 512:(nh + 1) * 512]
                V2.tensor_tensor(hv, hv, Gsig[:, n % 4, :], ALU.add).then_inc(o_done, 1)

        @block.tensor
        def _(pe):
            mm = nc.tensor.matmul

            def three(out_ap, w, x, start, stop):
                mm(out_ap, w[0], x[0], start=start, stop=False)
                mm(out_ap, w[0], x[1], start=False, stop=False)
                return mm(out_ap, w[1], x[0], start=False, stop=stop)

            def W(g, a, b):
                return Whi[:, g % 2, a:b], Wlo[:, g % 2, a:b]

            def X(k, sl):
                return Xhi[:, k, sl], Xlo[:, k, sl]

            def d_scores(n):
                r, hh = drows[n]
                if n == 0:
                    pe.wait_ge(s_ev, len(rows))
                else:
                    pe.wait_ge(ds_ev, n)
                p = slice(hh * HD, (hh + 1) * HD)
                mm(PB[0][:, :], T[p, DQ0, r:SEQ:DIL], T[p, DK0, :], start=True, stop=True)
                for g in range(1, 3):
                    last = mm(PB[1][:, (g - 1) * P:g * P],
                              T[p, DQ0 + g, r:SEQ:DIL], T[p, DK0 + g, r:SEQ:DIL], start=True, stop=True)
                last.then_inc(ds_mm, 1)

            for step in steps:
                if step[0] == "norm0":
                    for t in range(TT):
                        pe.wait_ge(x_diag, t + 1)
                        for k in range(KT):
                            last = mm(PB[k][:, t * P:(t + 1) * P], XN[:, t, k * P:(k + 1) * P], diag0[:, t, :],
                                      start=True, stop=True)
                            if t == TT - 1:
                                last.then_inc(x_turned, 1)
                elif step[0] == "gemm":
                    g = step[1]
                    if g:
                        pe.wait_ge(lo_done, g + 1)
                    mine = panel_jobs[g]
                    second = g - 1 in PAIRS
                    if g in PAIRS or second:
                        mine = panel_jobs[g if second else g + 1]
                    if g == 0:
                        for k in range(KT):
                            pe.wait_ge(hn_lo, max(k + 1, 2))
                            if k % 4 == 0:
                                pe.wait_ge(*((w_lo, 1) if k == 0 else (lo_done, 1)))
                            for n in mine:
                                c = jobs[n][2]
                                last = three(PB[n][:, :], W(g, k * 256 + c, k * 256 + c + P), X(k, slice(0, SEQ)),
                                             k == 0, k == KT - 1)
                                if k == KT - 1:
                                    last.then_inc(job_done, 1)
                        continue
                    for n in mine:
                        _, kind, c, w, t, dst, _ = jobs[n]
                        bank = PB[n % 4]
                        if n >= 4 and not second:
                            pe.wait_ge(job_evac, n - 3)
                        if kind == "T":
                            for k in range(KT):
                                last = three(bank[:, :], W(g, k * 256 + c, k * 256 + c + P), X(k, slice(0, SEQ)),
                                             k == 0, k == KT - 1)
                        elif kind == "B":
                            for k in range(4):
                                last = three(bank[:, 0:w], X(4 * second + k, slice(t * P, (t + 1) * P)),
                                             W(g, k * 512, k * 512 + w), not second and k == 0, second and k == 3)
                        elif kind == "H":
                            b = w
                            pe.wait_ge(ct_lo, 1)
                            pe.wait_ge(z_done, 2)
                            uh = Uhi[:, :, :].rearrange("p a t -> p (a t)")
                            ul = Ulo[:, :, :].rearrange("p a t -> p (a t)")
                            for m in range(8):
                                o = b * 992 + (8 * second + m) * 62
                                last = three(bank[0:124, 0:256], (uh[:, o:o + 124], ul[:, o:o + 124]),
                                             W(g, m * 256, (m + 1) * 256), not second and m == 0, second and m == 7)
                        else:
                            pe.wait_ge(job_evac, jobs_by[14])
                            flat = dst.rearrange("p j e -> p (j e)")
                            for r in range(DIL):
                                last = nc.tensor.transpose(bank[:, r * P:(r + 1) * P], flat[:, r:SEQ:DIL], ident)
                        if kind in "TX" or second:
                            last.then_inc(job_done, 1)
                        elif n == mine[-1]:
                            last.then_inc(half_done, 1)
                elif step[0] == "level_mm":
                    lev = step[1]
                    if lev == 0:
                        pe.wait_ge(hg_k, 1)
                        Qs, Ks = HQ, HF
                    else:
                        pe.wait_ge(qk_done, lev)
                        Qs = tC.rearrange("p (j t) -> p j t", j=2)
                        Ks = tD.rearrange("p (j t) -> p j t", j=2)
                    for h in range(HGH):
                        j, r = h // 2, slice((h % 2) * HD, (h % 2 + 1) * HD)
                        bank = PB[HGB[h]]
                        if lev:
                            pe.wait_ge(hg_ev, 4 * (lev - 1) + h + 1)
                        if lev == 5 and h == 3:
                            pe.wait_ge(chT_ev, 1)
                        if lev == 6 and h >= 2:
                            pe.wait_ge(c2_ev, 4)
                        if lev <= 7:
                            for i in range(TT):
                                last = mm(bank[:, i * P:(i + 1) * P], Ks[r, j, i * P:(i + 1) * P], Qs[r, j, i * P:(i + 1) * P],
                                          start=True, stop=True)
                        elif lev == 8:
                            for b, s in enumerate((0, 2)):
                                last = mm(bank[:, b * P:(b + 1) * P], Ks[r, j, s * P:(s + 1) * P],
                                          Qs[r, j, (s + 1) * P:(s + 2) * P], start=True, stop=True)
                        else:
                            for s in range(2):
                                last = mm(bank[:, s * 256:(s + 1) * 256], Ks[r, j, s * P:(s + 1) * P], Qs[r, j, 256:512],
                                          start=True, stop=True)
                        last.then_inc(hg_mm, 1)
                elif step[0] == "cmp_turn_hidden":
                    pe.wait_ge(ch_done, 1)
                    pe.wait_ge(eye_in, 16)
                    pe.wait_ge(hg_ev, 4 * 5)
                    for b in range(2):
                        for j in range(2):
                            last = nc.tensor.transpose(PB[7][:, (2 * b + j) * 62:(2 * b + j + 1) * 62],
                                                       CHN[0:2 * NC, b, j * P:(j + 1) * P], ident[0:2 * NC, 0:2 * NC])
                    last.then_inc(chT_mm, 1)
                elif step[0] == "cmp_mlp":
                    pe.wait_ge(small_in, 48)
                    pe.wait_ge(chT_ev, 1)
                    pe.wait_ge(hg_ev, 4 * 6)
                    for k in range(NKV):
                        for j in range(2):
                            mm(PB[6][k * HD:(k + 1) * HD, 0:NC], w2s[:, 0, j, :], CH[:, 0, j, k * NC:(k + 1) * NC],
                               start=(j == 0), stop=(j == 1))
                    for g in range(NG):
                        for k in range(NKV):
                            for j in range(2):
                                last = mm(PB[7][32 * g:32 * g + NC, k * HD:(k + 1) * HD], CH[:, 1, j, k * NC:(k + 1) * NC],
                                          w2s[:, 1, j, :], start=(j == 0), stop=(j == 1))
                    last.then_inc(c2_mm, 1)
                elif step[0] == "hg_values":
                    pe.wait_ge(hg_ev, 4 * NLEV)
                    pe.wait_ge(job_evac, jobs_by[4])
                    OFF = {(0, 1): 0, (2, 3): 1, (0, 2): 2, (0, 3): 3, (1, 2): 4, (1, 3): 5}
                    for a in range(2):
                        for i in (2 * a, 2 * a + 1):
                            for h in range(HGH):
                                o = (i % 2) * 256 + h * HD
                                for s in range(i + 1):
                                    lhs = AD[:, h, i, :] if s == i else AO[:, h, OFF[(s, i)], :]
                                    last = mm(PB[HGB[a]][:, o:o + HD], lhs, HI[:, s, h * HD:(h + 1) * HD],
                                              start=(s == 0), stop=(s == i))
                        last.then_inc(hgo_mm, 1)
                elif step[0] == "hg_mix":
                    pe.wait_ge(oh_done, 1)
                    for j in range(2):
                        for i in range(TT):
                            last = nc.tensor.transpose(PB[HGB[2 + j]][:, i * P:(i + 1) * P],
                                                       tD[:, i * 256 + j * P:i * 256 + (j + 1) * P], ident)
                        last.then_inc(mixT_mm, 1)
                elif step[0] == "cmp_scores":
                    pe.wait_ge(job_evac, jobs_by[12])
                    pe.wait_ge(hgo_ev, 2)
                    pe.wait_ge(c2_ev, 4)
                    for k in range(NKV):
                        r = slice(k * HD, (k + 1) * HD)
                        for i in range(TT):
                            for g in range(NG):
                                o = (i * NG + g) * NCP
                                last = mm(PB[4 + k][:, o:o + NCP], T[r, Q0 + g, i * P:(i + 1) * P], kcT[r, :],
                                          start=True, stop=True)
                        last.then_inc(cs_mm, 1)
                elif step[0] == "cmp_turn":
                    pe.wait_ge(cs_p, 1)
                    for k in range(NKV):
                        for i in range(TT):
                            last = nc.tensor.transpose(PB[4 + k][0:96, i * P:(i + 1) * P],
                                                       PC[:, k * 384 + i * 96:k * 384 + (i + 1) * 96], ident)
                        last.then_inc(ct_mm, 1)
                elif step[0] == "nsa":

                    def transposes(n):
                        h, b, i = rows[n]
                        pe.wait_ge(p_done, n + 1)
                        if n in (1, 2):
                            pe.wait_ge(ct_ev, n)
                        if n >= 3:
                            pe.wait_ge(t_ev, n - 2)
                        for j in range(i + 1):
                            last = nc.tensor.transpose(PB[TRB[n % 3]][:, j * P:(j + 1) * P],
                                                       SR[:, n % 4, j * P:(j + 1) * P], ident)
                        last.then_inc(t_mm, 1)

                    PIECES = [[None], [(0, 0)], [(0, 1)], [(0, 2), (0, 3)], [(1, 0)], [(1, 1)], [(1, 2), (1, 3)]]

                    def values(h, piece):
                        k, g, half = h // NG, h % NG, h % 2
                        j2 = h // 2
                        if piece == 0:
                            pe.wait_ge(t_ev, 8 * h + 8)
                            pe.wait_ge(mix_lo, 2)
                            if half == 0 and j2 >= 2:
                                pe.wait_ge(mix_lo, 2 + j2 - 1)
                        o = PB[OB[j2 % 2]][half * HD:(half + 1) * HD, :]
                        for what in PIECES[piece]:
                            if what is None:
                                mm(o, vcR[32 * g:32 * g + NCP, k, :], PCT[32 * g:32 * g + NCP, k, :], start=True, stop=False)
                                continue
                            b, s = what
                            last = mm(o[:, s * P:SEQ], V[:, (VS, VW)[b], s, k * HD:(k + 1) * HD],
                                      PT[:, h % 2, b, s, s * P:SEQ], start=False, stop=(b == 1 and s == TT - 1))
                        if piece == len(PIECES) - 1:
                            last.then_inc(pv_done, 1)

                    for n in range(len(rows) + 11):
                        if n < len(rows):
                            h, b, i = rows[n]
                            k, g = h // NG, h % NG
                            if n < 3:
                                pe.wait_ge(job_evac, len(jobs) - 2 + n)
                            else:
                                pe.wait_ge(s_ev, n - 2)
                            r = slice(k * HD, (k + 1) * HD)
                            mm(PB[ROWB[n % 3]][:, 0:(i + 1) * P], T[r, Q0 + g, i * P:(i + 1) * P],
                               T[r, (KS, KW)[b], 0:(i + 1) * P], start=True, stop=True).then_inc(s_mm, 1)
                        if 3 <= n < len(rows) + 3:
                            transposes(n - 3)
                        if n >= 12 and (n - 12) % 8 < len(PIECES):
                            values((n - 12) // 8, (n - 12) % 8)
                        if n == len(rows) + 2:
                            d_scores(0)
                elif step[0] == "dil":

                    def product(n):
                        t, c = n % TT, (n // TT) * 512
                        pe.wait_ge(lo_done, G_PLE + 1)
                        if n:
                            pe.wait_ge(y_ev, n)
                        for k in range(2):
                            last = three(PB[2][:, :], W(G_PT, k * SEQ + t * P, k * SEQ + (t + 1) * P),
                                         W(G_PLE, k * DM + c, k * DM + c + 512), k == 0, k == 1)
                        last.then_inc(y_mm, 1)

                    def transposes(n):
                        pe.wait_ge(dp_done, n + 1)
                        if n == 0:
                            pe.wait_ge(t_ev, len(rows))
                        if n >= 1:
                            pe.wait_ge(dt_ev, 2 * n)
                        for j in range(6):
                            bank = PB[3 + j // 4]
                            last = nc.tensor.transpose(bank[:, (j % 4) * P:(j % 4 + 1) * P],
                                                       DSR[:, n % 3, j * P:(j + 1) * P], ident)
                        last.then_inc(dt_mm, 1)

                    def values(n):
                        r, hh = drows[n]
                        pe.wait_ge(dt_ev, 2 * n + 2)
                        if n == 0:
                            pe.wait_ge(mix_lo, 5)
                        c = slice(hh * HD, (hh + 1) * HD)
                        for s in range(TT):
                            mm(PB[5][c, r * P:(r + 1) * P], V[:, DV0, s, c], DPT[:, n % 2, s, :], start=(s == 0), stop=(s == TT - 1))
                        for g in range(1, 3):
                            last = mm(PB[5 + g][c, r * P:(r + 1) * P], V[:, DV0 + g, r, c], DPT[:, n % 2, 3 + g, :],
                                      start=True, stop=True)
                        last.then_inc(dpv_done, 1)

                    for n in range(len(drows) + 3):
                        if n == 1:
                            product(0)
                        if 1 <= n < len(drows):
                            d_scores(n)
                        if 2 <= n <= len(drows):
                            product(n - 1)
                        if n == len(drows) + 1:
                            transposes(n - 2)
                        if n >= 3:
                            values(n - 3)
                        if 2 <= n <= len(drows):
                            transposes(n - 2)

            for c in range(4):
                g = G_OUT + c
                nh, kh = c // 2, c % 2
                pe.wait_ge(mix_lo, KT if kh else 5)
                pe.wait_ge(lo_done, g + 1)
                for t in range(TT):
                    if c == 0 and t == 2:
                        pe.wait_ge(y_ev, 8)
                    for k in range(4):
                        last = three(PB[4 * nh + t][:, :], X(MIX_ORDER[4 * kh + k], slice(t * P, (t + 1) * P)),
                                     W(g, k * 512, (k + 1) * 512), kh == 0 and k == 0, kh == 1 and k == 3)
                    if kh == 1:
                        last.then_inc(y_mm, 1)
                if kh == 0:
                    last.then_inc(half_done, 1)

            def turn_h(a):
                pe.wait_ge(y_gain, 8 * a + 4)
                for t in range(TT):
                    if a == 0:
                        pe.wait_ge(diag_done, t + 1)
                    else:
                        pe.wait_ge(h_done, TT + t + 1)
                    todo = [(k, t) for k in range(4 + t)] + [(4 + t, u) for u in range(t + 1)]
                    for k, u in todo:
                        dst, src = PB[k][:, u * P:(u + 1) * P], H[:, u, k * P:(k + 1) * P]
                        if a == 0:
                            last = mm(dst, src, diag[:, u, :], start=True, stop=True)
                        else:
                            last = nc.tensor.transpose(dst, src, ident)
                        if t == TT - 1 and u == TT - 1:
                            last.then_inc(h_turned, 1)

            turn_h(0)
            with pe.Fori(0, EIGHTHS // 2) as i:
                for e in range(2):
                    up0 = 0 if e == 0 else 4
                    for c in range(2):
                        g = G_MLP + 4 * e + c
                        pe.wait_ge(lo_done, i * 8 + g + 1)
                        for f in range(2 * c, 2 * c + 2):
                            if e == 1:
                                pe.wait_ge(dn_ev, i * 16 + 5)
                            for k in range(KT):
                                if e == 0 and f == 0:
                                    pe.wait_ge(x_lo, k + 1)
                                o = k * 256 + (f % 2) * P
                                last = three(PB[up0 + f][:, :], W(g, o, o + P), X(k, slice(0, SEQ)), k == 0, k == KT - 1)
                            last.then_inc(up_mm, 1)
                    for nh in range(2):
                        g = G_MLP + 4 * e + 2 + nh
                        b0 = 4 if (nh == 0) == (e == 0) else 0
                        pe.wait_ge(lo_done, i * 8 + g + 1)
                        if nh == 1:
                            pe.wait_ge(up_lo, i * 8 + 4 * e + 4)
                        else:
                            pe.wait_ge(dn_ev, i * 16 + 8 * e + 1)
                        order = [(k, t) for k in range(4) for t in range(TT)]
                        if nh == 1:
                            order = [(k, t) for t in range(TT) for k in range(4)]
                        for k, t in order:
                            if nh == 0 and t == 0:
                                pe.wait_ge(up_lo, i * 8 + 4 * e + k + 1)
                            last = three(PB[b0 + t][:, :], (Uhi[:, k, t * P:(t + 1) * P], Ulo[:, k, t * P:(t + 1) * P]),
                                         W(g, k * 512, (k + 1) * 512), k == 0, k == 3)
                            if k == 3:
                                last.then_inc(dn_mm, 1)
                pe.wait_ge(dn_ev, i * 16 + 13)
            turn_h(1)
            for c in range(4):
                g = G_GATE + c
                nh, kh = c // 2, c % 2
                pe.wait_ge(lo_done, g + 1)
                for t in range(TT):
                    for k in range(4):
                        if nh == 0 and t == 0:
                            pe.wait_ge(x_lo, KT + 4 * kh + k + 1)
                        last = three(PB[4 * nh + t][:, :], X(4 * kh + k, slice(t * P, (t + 1) * P)), W(g, k * 512, (k + 1) * 512),
                                     kh == 0 and k == 0, kh == 1 and k == 3)
                    if kh == 1:
                        last.then_inc(gt_mm, 1)
                    elif t == TT - 1:
                        last.then_inc(half_done, 1)


def panels(w_in, w_out, cmp_w1, w_up, w_down, w_gate, w_ple, p):
    out = np.zeros((N_PANELS, P, PAN), np.float32)

    def cols(g, parts):
        v = out[g].reshape(P, KT, 256)
        o = 0
        for c, n in parts:
            v[:, :, o:o + n] = w_in[:, c:c + n].reshape(KT, P, n).transpose(1, 0, 2)
            o += n

    def block(g, w):
        out[g] = w.reshape(4, P, 512).transpose(1, 0, 2).reshape(P, PAN)

    cols(0, [(C_HF, 256)])
    cols(1, [(C_HQ, 256)])
    cols(2, [(C_KC, 256)])
    def pair(g, parts):
        o = 0
        for c, n in parts:
            for m in range(2):
                out[g + m].reshape(P, 4, 512)[:, :, o:o + n] = \
                    w_in[m * 512:(m + 1) * 512, c:c + n].reshape(4, P, n).transpose(1, 0, 2)
            o += n

    pair(3, [(C_HI, 256), (C_VS, 128), (C_VW, 128)])
    for b in range(2):
        for m in range(2):
            out[5 + 4 * b + m] = cmp_w1[b, m * 1024:(m + 1) * 1024].reshape(8, P, 256).transpose(1, 0, 2).reshape(P, PAN)
    pair(7, [(C_HG, 256), (C_DV, 128), (C_GT, 18)])
    q = [(C_NQ + h * HD, HD) for h in (0, 3, 1, 4, 2, 5)]
    cols(11, q[:4])
    cols(12, q[4:] + [(C_KS, 128)])
    cols(13, [(C_KW, 128), (C_DV + 128, 128)])
    cols(14, [(C_DV + 256, 128)])
    cols(15, [(C_DQ, 256)])
    cols(16, [(C_DQ + 256, 256)])
    cols(17, [(C_DK + 128, 256)])
    for c in range(4):
        nh, kh = c // 2, c % 2
        rows = np.concatenate([np.arange(k * P, (k + 1) * P) for k in MIX_ORDER[4 * kh:4 * kh + 4]])
        block(G_OUT + c, w_out[rows, nh * 512:(nh + 1) * 512])
        block(G_GATE + c, w_gate[kh * 512:(kh + 1) * 512, nh * 512:(nh + 1) * 512])
    out[G_PT, :, :2 * SEQ] = p.T.reshape(2, P, SEQ).transpose(1, 0, 2).reshape(P, 2 * SEQ)
    out[G_PLE] = w_ple.reshape(2, P, DM).transpose(1, 0, 2).reshape(P, PAN)
    for e in range(EIGHTHS):
        for c in range(2):
            f = e * 512 + c * 256
            out[G_MLP + 4 * e + c] = w_up[:, f:f + 256].reshape(KT, P, 256).transpose(1, 0, 2).reshape(P, PAN)
            block(G_MLP + 4 * e + 2 + c, w_down[e * 512:(e + 1) * 512, c * 512:(c + 1) * 512])
    return out


def kernel(**inputs):
    import numpy as _np
    import concourse.bacc as _bacc
    from concourse import mybir as _mybir
    from concourse.bass_utils import run_bass_kernel_spmd as _run

    a = {k: _np.asarray(v) for k, v in inputs.items()}
    x = a["x"][0]
    tiles = lambda v: v.reshape(-1, P).T
    arrays = {
        "xn": x,
        "wst": panels(a["w_in"][0], a["w_out"][0], a["cmp_w1"][0], a["w_up"][0], a["w_down"][0],
                      a["w_ple_gate"][0], a["w_ple_proj"][0], a["p"][0, 0]),
        "gpre": tiles(a["g_pre_mix"][0]),
        "gvec": _np.stack([tiles(a["g_pre_mlp"][0]), tiles(a["g_ple"][0])], 1),
        "gpost": _np.stack([a["g_post_mix"][0], a["g_post_mlp"][0]]),
        "pos": a["cmp_pos"][0].reshape(2, 16, P).transpose(2, 0, 1),
        "w2": a["cmp_w2"][0].reshape(2, 2, P, HD).transpose(2, 0, 1, 3),
        "ctab": constant_table(),
        "lmask": level_masks(),
        "eye": _np.eye(P, dtype=_np.float32),
    }
    nc = _bacc.Bacc("TRN2", target_bir_lowering=False, num_devices=1)
    args = []
    for name in arrays:
        arrays[name] = _np.ascontiguousarray(arrays[name])
        args.append(nc.dram_tensor(name, arrays[name].shape, _mybir.dt.from_np(arrays[name].dtype),
                                   kind="ExternalInput").ap())
    args.append(nc.dram_tensor("out", (SEQ, DM), _mybir.dt.float32, kind="ExternalOutput").ap())
    build(nc, *args)
    r = _run(nc, [arrays], core_ids=[0])
    return r.results[0]["out"].reshape(1, SEQ, DM)
```
